# Optimizing a Trainium2 kernel written in Bass

```python
import math
import jax, jax.numpy as jnp
from jax import lax
import numpy as np

D_MODEL = 1024
BATCH = 1
SEQ = 512
DEPTH = 2

N_MIXERS = 2
SSM_GROUP = 16
SSM_GROUPS = D_MODEL // SSM_GROUP
SSM_STATE = 64
DT_MIN = 1e-3
DT_MAX = 1e-1
SSM_C_STD = 0.5
SB_HEADS = 16
SB_HEAD_DIM = D_MODEL // SB_HEADS
Q_BLOCK = 128
FFN_HIDDEN = -(-8 * D_MODEL // (3 * 256)) * 256
DEEPNORM_ALPHA = (2 * DEPTH) ** 0.25
DEEPNORM_BETA = (8 * DEPTH) ** -0.25
LN_EPS = 1e-5
N_SSM_LAYERS = (DEPTH + 1) // 2
N_SB_LAYERS = DEPTH // 2


def layer_norm(x, g, b):
    xf = x.astype(jnp.float32)
    mu = jnp.mean(xf, axis=-1, keepdims=True)
    var = jnp.mean(jnp.square(xf - mu), axis=-1, keepdims=True)
    y = (xf - mu) * lax.rsqrt(var + LN_EPS) * g.astype(jnp.float32) + b.astype(jnp.float32)
    return y.astype(x.dtype)

def _cmul(ar, ai, br, bi):
    return ar * br - ai * bi, ar * bi + ai * br

def _ssm_combine(left, right):
    alr, ali, blr, bli = left
    arr, ari, brr, bri = right
    ar, ai = _cmul(arr, ari, alr, ali)
    br, bi = _cmul(arr, ari, blr, bli)
    return ar, ai, br + brr, bi + bri

def s5_mixer(x, a_re, a_im, log_dt, b_re, b_im, c_re, c_im, d_skip, w_glu, w_out):
    bsz, seq, _ = x.shape
    f32 = jnp.float32
    u = x.astype(f32).reshape(bsz, seq, SSM_GROUPS, SSM_GROUP)
    dt = jnp.exp(log_dt.astype(f32))[:, None]
    lam_re = jnp.minimum(a_re.astype(f32), -1e-4)
    lam_im = a_im.astype(f32)
    mag = jnp.exp(lam_re * dt)
    lbar_re = mag * jnp.cos(lam_im * dt)
    lbar_im = mag * jnp.sin(lam_im * dt)
    den = lam_re * lam_re + lam_im * lam_im
    num_re = lbar_re - 1.0
    num_im = lbar_im
    coef_re = (num_re * lam_re + num_im * lam_im) / den
    coef_im = (num_im * lam_re - num_re * lam_im) / den
    bb_re, bb_im = _cmul(coef_re[..., None], coef_im[..., None],
                         b_re.astype(f32), b_im.astype(f32))
    bu_re = jnp.einsum('blgh,gph->lbgp', u, bb_re)
    bu_im = jnp.einsum('blgh,gph->lbgp', u, bb_im)
    a_seq_re = jnp.broadcast_to(lbar_re, (seq, 1, SSM_GROUPS, SSM_STATE))
    a_seq_im = jnp.broadcast_to(lbar_im, (seq, 1, SSM_GROUPS, SSM_STATE))
    _, _, s_re, s_im = lax.associative_scan(
        _ssm_combine, (a_seq_re, a_seq_im, bu_re, bu_im), axis=0)
    y = (jnp.einsum('lbgp,ghp->blgh', s_re, c_re.astype(f32))
         - jnp.einsum('lbgp,ghp->blgh', s_im, c_im.astype(f32)))
    y = y.reshape(bsz, seq, D_MODEL) + d_skip.astype(f32) * x.astype(f32)
    h = jax.nn.gelu(y).astype(x.dtype)
    val, gate = jnp.split(h @ w_glu, 2, axis=-1)
    z = val * jax.nn.sigmoid(gate)
    return (z @ w_out).astype(x.dtype)

def stick_breaking_mixer(x, w_qkv, w_o):
    bsz, seq, _ = x.shape
    f32 = jnp.float32
    q, k, v = jnp.split(x @ w_qkv, 3, axis=-1)
    to_heads = lambda t: t.reshape(bsz, seq, SB_HEADS, SB_HEAD_DIM).transpose(0, 2, 1, 3)
    q, k, v = to_heads(q), to_heads(k), to_heads(v)
    scale = SB_HEAD_DIM ** -0.5
    outs = []
    for blk in range(seq // Q_BLOCK):
        q0 = blk * Q_BLOCK
        kv_len = q0 + Q_BLOCK
        qb = q[:, :, q0:kv_len].astype(f32)
        kb = k[:, :, :kv_len].astype(f32)
        vb = v[:, :, :kv_len]
        z = jnp.einsum('bhqd,bhkd->bhqk', qb, kb) * scale
        t_idx = q0 + jnp.arange(Q_BLOCK)[:, None]
        s_idx = jnp.arange(kv_len)[None, :]
        past = s_idx < t_idx
        log_beta = jax.nn.log_sigmoid(z)
        log_1m_beta = jnp.where(past, jax.nn.log_sigmoid(-z), 0.0)
        between = lax.cumsum(log_1m_beta, axis=3, reverse=True) - log_1m_beta
        weights = jnp.where(past, jnp.exp(log_beta + between), 0.0)
        outs.append(jnp.einsum('bhqk,bhkd->bhqd', weights.astype(vb.dtype), vb))
    o = jnp.concatenate(outs, axis=2)
    o = o.transpose(0, 2, 1, 3).reshape(bsz, seq, D_MODEL)
    return (o @ w_o).astype(x.dtype)

def swiglu_ffn(x, w_gu, w_down):
    g, u = jnp.split(x @ w_gu, 2, axis=-1)
    return (jax.nn.silu(g) * u) @ w_down

def first_inputs(seed: int = 0) -> dict:
    key = jax.random.key(seed)
    ks = jax.random.split(key, 24)
    f32 = jnp.float32
    nrm = lambda k, shape, std: jax.random.normal(k, shape, f32) * std
    G, P, H, D, F = SSM_GROUPS, SSM_STATE, SSM_GROUP, D_MODEL, FFN_HIDDEN
    x = jax.random.normal(ks[0], (BATCH, SEQ, D), f32)
    ssm_a_re = -0.5 + nrm(ks[1], (N_SSM_LAYERS, G, P), 0.01)
    ssm_a_im = (math.pi * jnp.arange(P, dtype=f32))[None, None, :] + nrm(ks[2], (N_SSM_LAYERS, G, P), 0.01)
    ssm_log_dt = jax.random.uniform(ks[3], (N_SSM_LAYERS, G), f32,
                                    minval=math.log(DT_MIN), maxval=math.log(DT_MAX))
    ssm_b_re = nrm(ks[4], (N_SSM_LAYERS, G, P, H), (2 * H) ** -0.5)
    ssm_b_im = nrm(ks[5], (N_SSM_LAYERS, G, P, H), (2 * H) ** -0.5)
    ssm_c_re = nrm(ks[6], (N_SSM_LAYERS, G, H, P), SSM_C_STD)
    ssm_c_im = nrm(ks[7], (N_SSM_LAYERS, G, H, P), SSM_C_STD)
    ssm_d = nrm(ks[8], (N_SSM_LAYERS, D), 1.0)
    ssm_w_glu = nrm(ks[9], (N_SSM_LAYERS, D, 2 * D), D ** -0.5)
    ssm_w_out = nrm(ks[10], (N_SSM_LAYERS, D, D), D ** -0.5 * DEEPNORM_BETA)
    sb_w_qkv = nrm(ks[11], (N_SB_LAYERS, D, 3 * D), D ** -0.5)
    sb_w_o = nrm(ks[12], (N_SB_LAYERS, D, D), D ** -0.5 * DEEPNORM_BETA)
    ffn_w_gu = nrm(ks[13], (DEPTH, D, 2 * F), D ** -0.5)
    ffn_w_down = nrm(ks[14], (DEPTH, F, D), F ** -0.5 * DEEPNORM_BETA)
    ln_mix_g = 1.0 + nrm(ks[15], (DEPTH, D), 0.02)
    ln_mix_b = nrm(ks[16], (DEPTH, D), 0.02)
    ln_ffn_g = 1.0 + nrm(ks[17], (DEPTH, D), 0.02)
    ln_ffn_b = nrm(ks[18], (DEPTH, D), 0.02)
    return {"x": x,
            "ssm_a_re": ssm_a_re, "ssm_a_im": ssm_a_im, "ssm_log_dt": ssm_log_dt,
            "ssm_b_re": ssm_b_re, "ssm_b_im": ssm_b_im,
            "ssm_c_re": ssm_c_re, "ssm_c_im": ssm_c_im, "ssm_d": ssm_d,
            "ssm_w_glu": ssm_w_glu, "ssm_w_out": ssm_w_out,
            "sb_w_qkv": sb_w_qkv, "sb_w_o": sb_w_o,
            "ffn_w_gu": ffn_w_gu, "ffn_w_down": ffn_w_down,
            "ln_mix_g": ln_mix_g, "ln_mix_b": ln_mix_b,
            "ln_ffn_g": ln_ffn_g, "ln_ffn_b": ln_ffn_b}

def first_block(x, ssm_a_re, ssm_a_im, ssm_log_dt, ssm_b_re, ssm_b_im, ssm_c_re, ssm_c_im,
              ssm_d, ssm_w_glu, ssm_w_out, sb_w_qkv, sb_w_o, ffn_w_gu, ffn_w_down,
              ln_mix_g, ln_mix_b, ln_ffn_g, ln_ffn_b):
    h = x
    for i in range(DEPTH):
        j = i // N_MIXERS
        if i % N_MIXERS == 0:
            mix = s5_mixer(h, ssm_a_re[j], ssm_a_im[j], ssm_log_dt[j], ssm_b_re[j], ssm_b_im[j],
                           ssm_c_re[j], ssm_c_im[j], ssm_d[j], ssm_w_glu[j], ssm_w_out[j])
        else:
            mix = stick_breaking_mixer(h, sb_w_qkv[j], sb_w_o[j])
        h = layer_norm(DEEPNORM_ALPHA * h + mix, ln_mix_g[i], ln_mix_b[i])
        h = layer_norm(DEEPNORM_ALPHA * h + swiglu_ffn(h, ffn_w_gu[i], ffn_w_down[i]),
                       ln_ffn_g[i], ln_ffn_b[i])
    return h


A_GROUPS = 8
A_GROUP_DIM = 64
A_WIDTH = A_GROUPS * A_GROUP_DIM
A_CHUNK = 128
B_HEADS = 8
B_HEAD_DIM = 64
B_WIDTH = B_HEADS * B_HEAD_DIM
B_BRANCHES = ((128, 1), (512, 4), (2048, 16))
B_BLOCK = 128
C_HEADS = 4
C_DK = 128
C_DV = 256
C_GATE_RANK = 16
C_TAU = 16.0
C_CHUNK = 64
D_FF = 2816
CONV_W = 3

EPS = 1e-6
NEG = -1e30
N_EVEN = (DEPTH + 1) // 2
N_ODD = DEPTH // 2
EVEN_IN = 2 * A_WIDTH + 3 * B_WIDTH
ODD_IN = 2 * C_HEADS * C_DK + 2 * C_HEADS * C_DV + C_GATE_RANK


def rms_norm(x, g):
    xf = x.astype(jnp.float32)
    return xf * lax.rsqrt(jnp.mean(xf * xf, -1, keepdims=True) + EPS) * g.astype(jnp.float32)

def layer_norm_2(x, g, b):
    xf = x.astype(jnp.float32)
    mu = jnp.mean(xf, -1, keepdims=True)
    xc = xf - mu
    return xc * lax.rsqrt(jnp.mean(xc * xc, -1, keepdims=True) + EPS) * g + b

def causal_dwconv(h, w, b):
    S = h.shape[1]
    hp = jnp.pad(h, ((0, 0), (CONV_W - 1, 0), (0, 0)))
    out = b
    for k in range(CONV_W):
        out = out + hp[:, k:k + S] * w[k]
    return out

def chunked_gmlp(u, v, ln_g, ln_b, w_s, b_s):
    Bn, S, _ = u.shape
    nc = S // A_CHUNK
    vn = layer_norm_2(v, ln_g, ln_b).reshape(Bn, nc, A_CHUNK, A_GROUPS, A_GROUP_DIM)
    causal = jnp.tril(jnp.ones((A_CHUNK, A_CHUNK), dtype=bool))
    ws = jnp.where(causal[None], w_s.astype(jnp.float32), 0.0)
    mixed = jnp.einsum('gts,bnsgc->bntgc', ws, vn) + b_s.astype(jnp.float32).T[:, :, None]
    return u.astype(jnp.float32) * mixed.reshape(Bn, S, A_WIDTH)

def dilated_branch(q, k, v, window, dilation):
    Bn, H, S, hd = q.shape
    span = dilation * B_BLOCK
    Sp = -(-S // span) * span
    M = Sp // dilation
    nb = M // B_BLOCK
    n_back = window // dilation

    def to_blocks(t):
        t = jnp.pad(t, ((0, 0), (0, 0), (0, Sp - S), (0, 0)))
        t = t.reshape(Bn, H, M, dilation, hd)
        t = jnp.moveaxis(t, 3, 2)
        return t.reshape(Bn, H, dilation, nb, B_BLOCK, hd)

    def band(t):
        tp = jnp.pad(t, ((0, 0), (0, 0), (0, 0), (1, 0), (0, 0), (0, 0)))
        return jnp.concatenate([tp[:, :, :, :-1], tp[:, :, :, 1:]], axis=4)

    qb = to_blocks(q)
    kk = band(to_blocks(k))
    vv = band(to_blocks(v))

    i = jnp.arange(B_BLOCK)[:, None]
    j = jnp.arange(2 * B_BLOCK)[None, :]
    dist = B_BLOCK + i - j
    in_band = (dist >= 0) & (dist <= n_back)
    valid = in_band[None] & ((jnp.arange(nb) > 0)[:, None, None] | (j >= B_BLOCK)[None])

    s = jnp.einsum('bhrnic,bhrnjc->bhrnij', qb, kk) * (hd ** -0.5)
    s = jnp.where(valid, s, NEG)
    m = jnp.max(s, -1, keepdims=True)
    p = jnp.exp(s - m)
    den = jnp.sum(p, -1)
    o = jnp.einsum('bhrnij,bhrnjc->bhrnic', p, vv) / den[..., None]
    lse = m[..., 0] + jnp.log(den)

    def from_blocks(t):
        tail = t.shape[5:]
        t = t.reshape((Bn, H, dilation, M) + tail)
        t = jnp.moveaxis(t, 2, 3).reshape((Bn, H, Sp) + tail)
        return t[:, :, :S]

    return from_blocks(o), from_blocks(lse)

def even_mixer(h, w_in, a_ln_g, a_ln_b, a_ws, a_bs, q_g, k_g, w_out):
    Bn, S, _ = h.shape
    z = h @ w_in
    u, v, q, k, vb = jnp.split(
        z, [A_WIDTH, 2 * A_WIDTH, 2 * A_WIDTH + B_WIDTH, 2 * A_WIDTH + 2 * B_WIDTH], axis=-1)
    a_out = chunked_gmlp(jax.nn.gelu(u, approximate=False), jax.nn.gelu(v, approximate=False),
                         a_ln_g, a_ln_b, a_ws, a_bs)

    def heads(t):
        return t.reshape(Bn, S, B_HEADS, B_HEAD_DIM).transpose(0, 2, 1, 3)

    qh = rms_norm(heads(q), q_g)
    kh = rms_norm(heads(k), k_g)
    vh = heads(vb).astype(jnp.float32)
    outs, lses = [], []
    for window, dilation in B_BRANCHES:
        o_r, l_r = dilated_branch(qh, kh, vh, window, dilation)
        outs.append(o_r)
        lses.append(l_r)
    wts = jax.nn.softmax(jnp.stack(lses), axis=0)
    o = jnp.einsum('rbhs,rbhsc->bhsc', wts, jnp.stack(outs))
    b_out = o.transpose(0, 2, 1, 3).reshape(Bn, S, B_WIDTH)
    return jnp.concatenate([a_out, b_out], axis=-1).astype(h.dtype) @ w_out

def gla_chunked(q, k, v, log_a):
    Bn, H, S, dk = q.shape
    dv = v.shape[-1]
    nc = S // C_CHUNK

    def rs(t):
        return t.reshape(Bn, H, nc, C_CHUNK, t.shape[-1])

    q, k, v, log_a = rs(q), rs(k), rs(v), rs(log_a)
    b = jnp.cumsum(log_a, axis=3)
    b_last = b[:, :, :, -1:]
    q_t = q * jnp.exp(b)
    k_t = k * jnp.exp(-b)
    k_s = k * jnp.exp(b_last - b)
    causal = jnp.tril(jnp.ones((C_CHUNK, C_CHUNK), dtype=bool))
    attn = jnp.where(causal, jnp.einsum('bhnik,bhnjk->bhnij', q_t, k_t), 0.0)
    o_intra = jnp.einsum('bhnij,bhnjv->bhniv', attn, v)
    kv = jnp.einsum('bhnjk,bhnjv->bhnkv', k_s, v)
    decay = jnp.exp(b_last[:, :, :, 0])

    def step(state, inp):
        kv_n, d_n = inp
        return d_n[..., None] * state + kv_n, state

    init = jnp.zeros((Bn, H, dk, dv), jnp.float32)
    _, states = lax.scan(step, init, (jnp.moveaxis(kv, 2, 0), jnp.moveaxis(decay, 2, 0)))
    states = jnp.moveaxis(states, 0, 2)
    o_inter = jnp.einsum('bhnik,bhnkv->bhniv', q_t, states)
    return (o_intra + o_inter).reshape(Bn, H, S, dv)

def gla_mixer(h, w_in, w_a2, b_a, head_g, w_out):
    Bn, S, _ = h.shape
    hk, hv = C_HEADS * C_DK, C_HEADS * C_DV
    z = h @ w_in
    q, k, v, r, ga = jnp.split(z, [hk, 2 * hk, 2 * hk + hv, 2 * hk + 2 * hv], axis=-1)

    def heads(t, dh):
        return t.reshape(Bn, S, C_HEADS, dh).transpose(0, 2, 1, 3).astype(jnp.float32)

    log_a = jax.nn.log_sigmoid((ga @ w_a2 + b_a).astype(jnp.float32)) / C_TAU
    o = gla_chunked(heads(q, C_DK) * (C_DK ** -0.5), heads(k, C_DK), heads(v, C_DV),
                    heads(log_a, C_DK))
    o = rms_norm(o, head_g)
    o = o.transpose(0, 2, 1, 3).reshape(Bn, S, hv) * jax.nn.silu(r.astype(jnp.float32))
    return o.astype(h.dtype) @ w_out

def conv_ffn(h, w_gate, w_up, conv_w, conv_b, w_down):
    g = causal_dwconv(h @ w_gate, conv_w, conv_b)
    return (jax.nn.silu(g) * (h @ w_up)) @ w_down

def second_inputs(seed: int = 0) -> dict:
    key = jax.random.key(seed)
    ks = iter(jax.random.split(key, 32))

    def nrm(shape, scale):
        return jax.random.normal(next(ks), shape, jnp.float32) * scale

    res = (2 * DEPTH) ** -0.5
    return {
        "x": nrm((BATCH, SEQ, D_MODEL), 1.0),
        "norm_mix_g": 1.0 + nrm((DEPTH, D_MODEL), 0.1),
        "norm_ffn_g": 1.0 + nrm((DEPTH, D_MODEL), 0.1),
        "ev_w_in": nrm((N_EVEN, D_MODEL, EVEN_IN), D_MODEL ** -0.5),
        "ev_a_ln_g": 1.0 + nrm((N_EVEN, A_WIDTH), 0.1),
        "ev_a_ln_b": nrm((N_EVEN, A_WIDTH), 0.02),
        "ev_a_ws": nrm((N_EVEN, A_GROUPS, A_CHUNK, A_CHUNK), A_CHUNK ** -0.5),
        "ev_a_bs": 1.0 + nrm((N_EVEN, A_GROUPS, A_CHUNK), 0.1),
        "ev_q_g": 1.0 + nrm((N_EVEN, B_HEAD_DIM), 0.1),
        "ev_k_g": 1.0 + nrm((N_EVEN, B_HEAD_DIM), 0.1),
        "ev_w_out": nrm((N_EVEN, A_WIDTH + B_WIDTH, D_MODEL), (A_WIDTH + B_WIDTH) ** -0.5 * res),
        "od_w_in": nrm((N_ODD, D_MODEL, ODD_IN), D_MODEL ** -0.5),
        "od_w_a2": nrm((N_ODD, C_GATE_RANK, C_HEADS * C_DK), C_GATE_RANK ** -0.5),
        "od_b_a": nrm((N_ODD, C_HEADS * C_DK), 0.5),
        "od_head_g": 1.0 + nrm((N_ODD, C_DV), 0.1),
        "od_w_out": nrm((N_ODD, C_HEADS * C_DV, D_MODEL), (C_HEADS * C_DV) ** -0.5 * res),
        "ffn_w_gate": nrm((DEPTH, D_MODEL, D_FF), D_MODEL ** -0.5),
        "ffn_w_up": nrm((DEPTH, D_MODEL, D_FF), D_MODEL ** -0.5),
        "ffn_conv_w": nrm((DEPTH, CONV_W, D_FF), CONV_W ** -0.5),
        "ffn_conv_b": nrm((DEPTH, D_FF), 0.02),
        "ffn_w_down": nrm((DEPTH, D_FF, D_MODEL), D_FF ** -0.5 * res),
    }

def second_block(x, norm_mix_g, norm_ffn_g,
              ev_w_in, ev_a_ln_g, ev_a_ln_b, ev_a_ws, ev_a_bs, ev_q_g, ev_k_g, ev_w_out,
              od_w_in, od_w_a2, od_b_a, od_head_g, od_w_out,
              ffn_w_gate, ffn_w_up, ffn_conv_w, ffn_conv_b, ffn_w_down):
    for layer in range(DEPTH):
        h = rms_norm(x, norm_mix_g[layer]).astype(x.dtype)
        if layer % 2 == 0:
            e = layer // 2
            mix = even_mixer(h, ev_w_in[e], ev_a_ln_g[e], ev_a_ln_b[e], ev_a_ws[e], ev_a_bs[e],
                             ev_q_g[e], ev_k_g[e], ev_w_out[e])
        else:
            o = layer // 2
            mix = gla_mixer(h, od_w_in[o], od_w_a2[o], od_b_a[o], od_head_g[o], od_w_out[o])
        x = x + mix.astype(x.dtype)
        h = rms_norm(x, norm_ffn_g[layer]).astype(x.dtype)
        x = x + conv_ffn(h, ffn_w_gate[layer], ffn_w_up[layer], ffn_conv_w[layer],
                         ffn_conv_b[layer], ffn_w_down[layer]).astype(x.dtype)
    return x


def setup_inputs(seed=0):
    out = dict(first_inputs(seed))
    for name, value in second_inputs(seed + 1).items():
        if name != "x":
            out[name + "_2"] = value
    return out


def reference(
    x, ssm_a_re, ssm_a_im, ssm_log_dt, ssm_b_re, ssm_b_im, ssm_c_re, ssm_c_im, ssm_d, ssm_w_glu,
    ssm_w_out, sb_w_qkv, sb_w_o, ffn_w_gu, ffn_w_down, ln_mix_g, ln_mix_b, ln_ffn_g, ln_ffn_b,
    norm_mix_g_2, norm_ffn_g_2, ev_w_in_2, ev_a_ln_g_2, ev_a_ln_b_2, ev_a_ws_2, ev_a_bs_2,
    ev_q_g_2, ev_k_g_2, ev_w_out_2, od_w_in_2, od_w_a2_2, od_b_a_2, od_head_g_2, od_w_out_2,
    ffn_w_gate_2, ffn_w_up_2, ffn_conv_w_2, ffn_conv_b_2, ffn_w_down_2,
):
    x = first_block(
        x, ssm_a_re, ssm_a_im, ssm_log_dt, ssm_b_re, ssm_b_im, ssm_c_re, ssm_c_im, ssm_d,
        ssm_w_glu, ssm_w_out, sb_w_qkv, sb_w_o, ffn_w_gu, ffn_w_down, ln_mix_g, ln_mix_b,
        ln_ffn_g, ln_ffn_b,
    )
    return second_block(
        x, norm_mix_g_2, norm_ffn_g_2, ev_w_in_2, ev_a_ln_g_2, ev_a_ln_b_2, ev_a_ws_2,
        ev_a_bs_2, ev_q_g_2, ev_k_g_2, ev_w_out_2, od_w_in_2, od_w_a2_2, od_b_a_2, od_head_g_2,
        od_w_out_2, ffn_w_gate_2, ffn_w_up_2, ffn_conv_w_2, ffn_conv_b_2, ffn_w_down_2,
    )


_drawn_inputs = setup_inputs


def setup_inputs(seed=0):
    import zlib

    import numpy as np

    out = dict(_drawn_inputs(seed))
    spreads = {}
    factors = {'ssm_a_re': 8.0,
     'ev_a_ln_g_2': 3.069,
     'ev_a_ln_b_2': 8.0,
     'ev_q_g_2': 8.0,
     'ev_k_g_2': 8.0,
     'ffn_conv_b_2': 6.837}
    for name, (base, spread) in spreads.items():
        noise = np.random.default_rng([zlib.crc32(name.encode()), seed]).standard_normal(out[name].shape)
        drawn = base * np.exp(spread * noise) if base else spread * noise
        out[name] = __import__('jax').numpy.asarray(drawn.astype(out[name].dtype))
    for name, factor in factors.items():
        out[name] = (out[name] * factor).astype(out[name].dtype)
    return out
```

```python
from contextlib import ExitStack

import concourse.bass as bass
from concourse import mybir

ALU = mybir.AluOpType
ACT = mybir.ActivationFunctionType
AX = mybir.AxisListType
F32 = mybir.dt.float32
F32R = mybir.dt.float32r
I32 = mybir.dt.int32

P = 128
SEQ = 512
D = 1024
DC = D // P
TT = SEQ // P
FFN = 2816
FC = FFN // P
DEPTH = 2
ALPHA = (2 * DEPTH) ** 0.25
LN_EPS = 1e-5
RMS_EPS = 1e-6

GROUPS, GH, GP = 64, 16, 64
PAIRS = GROUPS // 2
TAU = 8
NCH = SEQ // TAU
LAGS = TAU + 1

HEADS, HD = 16, 64
STICK = 1280
REST = {0: 512, 2: 896, 1: 1024}

PT_AT = {0: 0, 1: 512, 3: 896, 2: 1024}
ROW_AT = [P * i * (i + 1) // 2 for i in range(TT)]
NEG = -1e30
HEADS_B = 8
GLA_HEADS, GLA_CHUNK, GLA_DV, GATE_RANK = 4, 64, 256, 16
GLA_CHUNKS = SEQ // GLA_CHUNK
GLA_TAU = 16.0
TAPS = 3

KB = 1024
TILE = 2048
DOWN_K = FC // 2

ROUND = 1.5 * 2.0 ** 23
TWO_PI = (6.28125, 0.00193500518798828125, 3.0199158988e-07)
LN2 = (0.693359375, -2.12194440e-4)
EXP_TAYLOR = (1.0, 1 / 2, 1 / 6, 1 / 24, 1 / 120, 1 / 720, 1 / 5040)


class Stage:

    def __init__(self, name, iters, parts, evacs):
        self.name, self.iters, self.parts, self.evacs = name, iters, parts, evacs


def plan_stages():
    rows = [
        ("glu", 4, 4, 2), ("ssm_out", 2, 4, 4), ("gu0", 11, 4, 2), ("down0", 8, 2, 1),
        ("q", 2, 4, 4), ("k", 2, 4, 4), ("v", 2, 8, 8), ("w_o", 2, 4, 4), ("gu1", 11, 4, 2), ("down1", 8, 2, 1),
        ("ev_u", 1, 4, 4), ("ev_qk", 2, 4, 4), ("ev_v", 1, 8, 8), ("ev_vb", 1, 8, 8),
        ("ev_out", 2, 4, 4), ("conv0", 11, 4, 2), ("cdown0", 8, 2, 1),
        ("od_q", 1, 4, 4), ("od_k", 1, 4, 4), ("od_v", 2, 8, 8), ("od_r", 2, 4, 4), ("od_out", 2, 4, 4),
        ("conv1", 11, 4, 2), ("cdown1", 8, 2, 1),
    ]
    stages, it, part, evac, pair, resid = {}, 0, 0, 4, DC, 0
    for row in rows:
        s = Stage(*row)
        s.it0, s.part0, s.evac0, s.pair0, s.res0 = it, part, evac, pair, resid
        it += s.iters
        part += s.iters * s.parts
        evac += s.iters * s.evacs
        pair += s.iters * s.evacs * (s.evacs == 2)
        resid += DC * ("out" in s.name or "down" in s.name or s.name == "w_o")
        s.part1, s.evac1, s.pair1, s.res1 = part, evac, pair, resid
        stages[s.name] = s
    return stages


def build_blocks(nc, t, out):
    ST = plan_stages()
    run = list(ST)

    with ExitStack() as ctx:
        top = [nc.sbuf_base]
        arena_size = (nc.sbuf_usable_end - nc.sbuf_base) // 64 * 64 - 64
        ctx.enter_context(nc.sbuf_tensor("arena", [P, arena_size // 4], F32))
        arena0 = (top[0] + 31) // 32 * 32
        top[0] = arena0

        def at(name, shape, offset, dtype=F32):
            return nc.alloc_sbuf_tensor_at(name, shape, dtype, offset=offset)

        def new(name, shape, dtype=F32):
            words = 1
            for n in shape[1:]:
                words *= n
            here = top[0]
            top[0] = here + (words * 4 + 31) // 32 * 32
            assert top[0] <= arena0 + arena_size, (name, top[0])
            return at(name, shape, here, dtype), here

        def sem(name):
            return ctx.enter_context(nc.semaphore(name))

        psum = ctx.enter_context(nc.psum_tensor("psum", [P, 8, 512], F32))
        bank = [psum[:, i, :] for i in range(8)]

        wst, wst_at = new("w_stage", [P, 2, TILE])
        whi, whi_at = new("w_hi", [P, 2, TILE], F32R)
        wlo, _ = new("w_lo", [P, 2, TILE], F32R)
        xhi, xhi_at = new("x_hi", [P, DC, SEQ], F32R)
        xlo, _ = new("x_lo", [P, DC, SEQ], F32R)
        res, res_at = new("residual", [P, DC, SEQ])
        hhi, hid_at = new("hidden_hi", [P, FC, SEQ], F32R)
        hlo, _ = new("hidden_lo", [P, FC, SEQ], F32R)
        tmp_a, tmp_at = new("tmp_a", [P, 2, SEQ])
        tmp_b, _ = new("tmp_b", [P, 2, SEQ])
        tmp_c, _ = new("tmp_c", [P, 2, SEQ])
        sq, _ = new("squares", [P, 2, SEQ])
        ident, _ = new("ident", [P, P])
        ones_mean, _ = new("ones_mean", [P, P])
        ones, _ = new("ones", [P, P])
        eps_ln, _ = new("eps_ln", [P, 1])
        eps_rms, _ = new("eps_rms", [P, 1])
        one_col, _ = new("one_col", [P, 1])
        pool_pad, _ = new("pool_pad", [P, 1])
        marks, _ = new("marks", [P, 16])
        NROW = 12 * DC
        CROW = (TAPS + 1) * FC
        SROW = 8
        prm, _ = new("params", [P, NROW + 2 * CROW + SROW])

        def tap(layer, k, m):
            return prm[:, bass.ds(m + (NROW + layer * CROW + k * FC), 1)]

        small0 = NROW + 2 * CROW
        gate_bias = prm[:, small0:small0 + GLA_HEADS]
        head_gain = prm[:, small0 + 4:small0 + 6]
        q_gain, k_gain = prm[:, small0 + 6:small0 + 7], prm[:, small0 + 7:small0 + 8]
        rstd = sq[:, 0, :]
        d_bc, _ = new("d_rows", [P, 512])
        prm_st = at("param_rows", [NROW, P], wst_at + 12 * KB)
        conv_st = at("conv_rows", [CROW, 2, P], wst_at + 12 * KB + 512)
        small_st = at("small_rows", [SROW, P], wst_at + 12 * KB + 1536)

        xnat = at("x_natural", [P, TAU, 512], hid_at + 72 * KB)
        w_re = at("cl_re", [P, PAIRS, LAGS, GH], hid_at)
        w_im = at("cl_im_neg", [P, PAIRS, LAGS, GH], hid_at + 18 * KB)
        toe = at("toeplitz", [P, GROUPS, P], hid_at + 36 * KB)
        v_tmp = at("v_tmp", [P, 2, 4, TAU, GH], hid_at + 68 * KB)
        uu = at("u_chunks", [P, GROUPS, NCH], res_at)
        vt = at("bl_rows", [P, 2, PAIRS, P], xhi_at)
        v_buf = at("bl_piece", [P, 2, 2, 4, TAU * GH], tmp_at)
        k_rows = at("k_rows", [P, 16, P], tmp_at + 8 * KB)
        w_tmp = at("w_tmp", [P, 2, 4, LAGS, GH], tmp_at + 8 * KB)
        b_st = at("b_stage", [PAIRS, 2, 2 * GP * GH], whi_at)
        c_st = at("c_stage", [P, 2, 8, 2, GP], whi_at + 16 * KB)
        states = at("states", [P, NCH + 1, 2, PAIRS], whi_at)
        s_tmp = at("state_tmp", [P, 2, 2, PAIRS], whi_at + 17 * KB)
        a_st = at("a_stage", [PAIRS, 3, 2 * GP], whi_at + 24 * KB)
        dt_st = at("dt_stage", [PAIRS, 2], whi_at + 26 * KB - 512)
        sp_ = at("ssm_scalars", [P, 24, PAIRS], whi_at + 26 * KB)
        lam = at("lam_powers", [P, 2, LAGS, PAIRS], whi_at + 29 * KB)
        ki = at("exp_bits", [P, PAIRS], whi_at + 29 * KB + 2304 + 256, I32)
        ll = at("lam_step", [P, 2, 2, PAIRS], whi_at + 17 * KB + 512)
        lam_rev = at("lam_powers_down", [P, 2, TAU, PAIRS], whi_at + 18 * KB)
        bt = at("b_cols", [P, 2, GH, PAIRS], wst_at)
        ct = at("c_cols", [P, 2, PAIRS, GH], wst_at + 4 * KB)
        bb = at("b_bar", [P, 2, 2 * GH, PAIRS], wst_at + 8 * KB)
        l_tmp = at("lam_tmp", [P, 2, GH, PAIRS], tmp_at)
        x_perm = at("x_by_group", [P, 32, TAU, GH], hid_at)

        q_f = at("q_feat", [P, DC, SEQ], hid_at + 16 * KB)
        k_f = at("k_feat", [P, DC, SEQ], hid_at + 60 * KB)
        v_t = at("v_tok", [P, TT, D], res_at)
        k_pair = at("k_pair", [P, 2, SEQ], hid_at + 32 * KB)
        v_pair = at("v_pair", [P, 2, TT, P], hid_at + 36 * KB)
        q_pair = at("q_pair", [P, 2, SEQ], hid_at + 40 * KB)
        drop = at("drop", [P, 2, STICK], tmp_at)
        keep = at("keep", [P, 2, STICK], hid_at + 76 * KB)
        lnp = at("ln_part", [P, STICK], tmp_at + 10 * KB)
        after, _ = new("mask_after", [P, P])
        before, _ = new("mask_before", [P, P])

        u_f = at("u_feat", [P, 4, SEQ], hid_at)
        qk_f = at("qk_feat", [P, 8, SEQ], hid_at + 8 * KB)
        gv_t = at("gate_tok", [P, TT, 512], hid_at + 24 * KB)
        vb_t = at("value_tok", [P, TT, 512], hid_at + 32 * KB)
        ws_t = at("mix_rows", [P, 8, P], hid_at + 40 * KB)
        qk_rs = at("qk_rstd", [P, 8, SEQ], hid_at + 44 * KB)
        ws_st = at("mix_stage", [P, 8, P], hid_at + 60 * KB)
        gv_gb = at("gate_norm", [P, 2, 512], hid_at + 64 * KB)
        bias_t = at("score_bias", [P, TT, P], hid_at + 68 * KB)
        mult_t = at("multiplicity", [P, TT, P], hid_at + 70 * KB)
        qn_pair = at("qn_pair", [P, 2, SEQ], hid_at + 72 * KB)
        kn_pair = at("kn_pair", [P, 2, SEQ], hid_at + 76 * KB)
        vb_pair = at("vb_pair", [P, 2, TT, P], hid_at + 80 * KB)
        bs_st = at("mix_bias", [1, 8, P], hid_at + 84 * KB)
        prob = at("prob", [P, 2, STICK], tmp_at)
        prob_t = at("prob_t", [P, STICK], tmp_at + 10 * KB)
        stat = at("even_stats", [P, 128], tmp_at + 15 * KB + 512)
        gv_stats, gv_mv = stat[:, 0:24].rearrange("p (n k) -> p n k", n=TT), stat[:, 24:32].rearrange("p (n k) -> p n k", n=TT)
        gv_rs = stat[:, 32:36]
        neg_max = stat[:, 40:48].rearrange("p (b n) -> p b n", b=2)
        den = stat[:, 48:56].rearrange("p (b n) -> p b n", b=2)
        rden = stat[:, 56:64].rearrange("p (b n) -> p b n", b=2)
        sq_even = at("even_squares", [P, 2, SEQ], tmp_at)
        resid4 = at("residue4", [P, 2, P], tmp_at + 8 * KB)
        head_mean, _ = new("head_mean", [P, P])

        gq = at("gla_q", [P, GLA_HEADS, SEQ], hid_at)
        gk = at("gla_k", [P, GLA_HEADS, SEQ], hid_at + 8 * KB)
        gvt = at("gla_v_tok", [P, TT, D], hid_at + 16 * KB)
        gr = at("gla_r", [P, DC, SEQ], hid_at + 32 * KB)
        cum = at("gla_cum", [P, GLA_HEADS, SEQ], hid_at + 48 * KB)
        attn_t = at("gla_attn", [P, GLA_HEADS, TT, P], hid_at + 48 * KB)
        la = at("gla_log_a", [P, GLA_HEADS, SEQ], hid_at + 56 * KB)
        gkt = at("gla_k_scaled", [P, GLA_HEADS, SEQ], hid_at + 56 * KB)
        ge = at("gla_exp", [P, GLA_HEADS, SEQ], hid_at + 64 * KB)
        gks = at("gla_k_state", [P, GLA_HEADS, SEQ], hid_at + 72 * KB)
        go = at("gla_o", [P, DC, SEQ], hid_at + 64 * KB)
        gks_t = at("gla_k_tok", [P, TT, GLA_HEADS, P], hid_at + 80 * KB)
        ga_t = at("gate_low", [P, SEQ], hid_at + 72 * KB)
        wa2 = at("gate_up", [GATE_RANK, 512], hid_at + 74 * KB)
        wga = at("gate_w", [P, DC, P], tmp_at)
        wga_hi = at("gate_w_hi", [P, DC, P], tmp_at + 4 * KB, F32R)
        wga_lo = at("gate_w_lo", [P, DC, P], tmp_at + 8 * KB, F32R)
        gst = at("gla_states", [P, 2, GLA_CHUNKS, GLA_DV], tmp_at)
        sq_odd = at("gla_squares", [P, 2, SEQ], tmp_at)
        o_rs = at("gla_rstd", [P, SEQ], tmp_at + 4 * KB)
        o_tmp = at("gla_tmp", [P, 2, SEQ], tmp_at + 6 * KB)
        decay = d_bc[:, 0:GLA_HEADS * GLA_CHUNKS].rearrange("p (h n) -> p h n", h=GLA_HEADS)
        chunk_mask, _ = new("chunk_mask", [P, P])
        keep_sum = at("keep_sum", [P, SEQ], hid_at + 78 * KB)

        out_t = at("out_tok", [P, TT, D], hid_at)

        w_landed = [sem("w_landed0"), sem("w_landed1")]
        whi_done, wlo_done = sem("whi_done"), sem("wlo_done")
        part_done, evac_done = sem("part_done"), sem("evac_done")
        act_out, zhi_done, res_ready = sem("act_out"), sem("zhi_done"), sem("res_ready")
        hid_ready = sem("hid_ready")
        ld_a, ld_b, ld_c, ld_x, ld_d, ld_prm = (sem(f"ld_{n}") for n in "a b c x d prm".split())
        consts, dve_link, act_link = sem("consts"), sem("dve_link"), sem("act_link")
        a_rows, tr_a, tr_b, tr_c, tr_prm = (sem(n) for n in "a_rows tr_a tr_b tr_c tr_prm".split())
        b_copied, c_copied, tr_u, u_copied = (sem(n) for n in "b_copied c_copied tr_u u_copied".split())
        trig_in, trig_out = sem("trig_in"), sem("trig_out")
        bb_ready, lam_ready, v_ready, tr_v, vt_copied = (
            sem(n) for n in "bb_ready lam_ready v_ready tr_v vt_copied".split())
        w_ready, pool_link, k_done, k_copied, toe_zero, toe_ready = (
            sem(n) for n in "w_ready pool_link k_done k_copied toe_zero toe_ready".split())
        s_in, s_copied, tr_x, xhi_done, xd_ready, scan_link, scan_done = (
            sem(n) for n in "s_in s_copied tr_x xhi_done xd_ready scan_link scan_done".split())
        y_done, y_copied, tr_y, gelu_done = (sem(n) for n in "y_done y_copied tr_y gelu_done".split())
        x_ready, x_permuted = sem("x_ready"), sem("x_permuted")
        ln_mean, ln_xc, ln_sq, ln_sq_used, ln_rs, ln_n, ln_a, ln_hi = (
            sem(n) for n in "ln_mean ln_xc ln_sq ln_sq_used ln_rs ln_n ln_a ln_hi".split())
        qkv_staged, z_done, ln_part, sp_done, lb_done, sp_masked = (
            sem(n) for n in "qkv_staged z_done ln_part sp_done lb_done sp_masked".split())
        cs_done, lw_done, w_done, w_masked, o_done, o_hi, o_ready, soft_link = (
            sem(n) for n in "cs_done lw_done w_done w_masked o_done o_hi o_ready soft_link".split())
        ld_even, tab_done, ws_tr, ws_copied, ws_ready, s4_ready, tables = (
            sem(n) for n in "ld_even tab_done ws_tr ws_copied ws_ready s4_ready tables".split())
        ev_link, qk_sq, qk_ms, qk_ln, qk_rstd, gv_var, gv_rstd, vn_ready = (
            sem(n) for n in "ev_link qk_sq qk_ms qk_ln qk_rstd gv_var gv_rstd vn_ready".split())
        gm_done, gm_copied, gm_hi, gm_ready = (sem(n) for n in "gm_done gm_copied gm_hi gm_ready".split())
        qn_ready, vb_staged, sc_done, sm_done, mx_done, pexp, den_done, pn_done, tr_p, pt_copied, pv_done, b_hi, b_ready, ttr_link = (
            sem(n) for n in ("qn_ready vb_staged sc_done sm_done mx_done pexp den_done pn_done tr_p pt_copied pv_done "
                             "b_hi b_ready ttr_link").split())
        ld_odd, wga_zero, wga_hi_s, wga_ready, ga_done, ga_copied, la_done, la_lin, la_link, ln_a1, cum_done = (
            sem(n) for n in ("ld_odd wga_zero wga_hi_s wga_ready ga_done ga_copied la_done la_lin la_link ln_a1 cum_done").split())
        ek_done, gq_done, en_done, gkt_done, last_done, es_done, gks_done, tr_k, kt_copied, at_done, at_ready = (
            sem(n) for n in ("ek_done gq_done en_done gkt_done last_done es_done gks_done tr_k kt_copied at_done at_ready").split())
        kv_done, st_ready, st_link, go_done, go_copied, go_sq, go_ms, go_rs, go_link, go_hi, go_ready = (
            sem(n) for n in ("kv_done st_ready st_link go_done go_copied go_sq go_ms go_rs go_link go_hi go_ready").split())
        conv_a, conv_b, conv_act, rms_t, tr_out, out_rows = (
            sem(n) for n in "conv_a conv_b conv_act rms_t tr_out out_rows".split())
        mask_ones = sem("mask_ones")
        prm_copied, out_done = sem("prm_copied"), sem("out_done")

        block = ctx.enter_context(nc.Block())

        def linker(eng, s):
            count = [0]

            def link(ins):
                count[0] += 1
                ins.then_inc(s, 1)
                eng.wait_ge(s, count[0])
            return link

        def gain(n, c):
            return prm[:, n * DC + c:n * DC + c + 1]

        def wcols(w, col, n=256):
            return w.rearrange("(k p) n -> p k n", p=P)[:, :, bass.ds(col, n)]

        def tile_source(name, i, half, first=0):
            if name == "glu":
                return wcols(t["ssm_w_glu"][0], i * 256 + (first * 256 + (1 - half) * D))
            if name in ("ssm_out", "w_o", "ev_out", "od_out"):
                w = {"ssm_out": "ssm_w_out", "w_o": "sb_w_o", "ev_out": "ev_w_out_2", "od_out": "od_w_out_2"}[name]
                return wcols(t[w][0], i * 512 + half * 256)
            if name in ("gu0", "gu1"):
                return wcols(t["ffn_w_gu"][int(name[-1])], i * 256 + half * FFN)
            if name in ("conv0", "conv1"):
                return wcols(t["ffn_w_up_2" if half else "ffn_w_gate_2"][int(name[-1])], i * 256)
            if name in ("down0", "down1", "cdown0", "cdown1"):
                w = t["ffn_w_down_2" if name[0] == "c" else "ffn_w_down"][int(name[-1])]
                rows = w.rearrange("(k p) n -> p k n", p=P)[:, half * DOWN_K:(half + 1) * DOWN_K]
                return rows[:, :, bass.ds(i * P, P)]
            w, col = {
                "q": ("sb_w_qkv", 0), "k": ("sb_w_qkv", D), "v": ("sb_w_qkv", 2 * D),
                "ev_u": ("ev_w_in_2", 0), "ev_v": ("ev_w_in_2", 512), "ev_qk": ("ev_w_in_2", 1024),
                "ev_vb": ("ev_w_in_2", 2048),
                "od_q": ("od_w_in_2", 0), "od_k": ("od_w_in_2", 512), "od_v": ("od_w_in_2", 1024), "od_r": ("od_w_in_2", 2048),
            }[name]
            return wcols(t[w][0], i * 512 + half * 256 + col)

        def tile_view(w, name, half):
            if "down" in name:
                return w[:, half, 0:DOWN_K * P].rearrange("p (k n) -> p k n", k=DOWN_K)
            return w[:, half, :].rearrange("p (k n) -> p k n", k=DC)

        @block.sync
        def _(sp):
            sp.dma_start(a_st[:, 0, :], t["ssm_a_re"][0].rearrange("(j g) p -> j (g p)", g=2)).then_inc(ld_a, 16)
            sp.dma_start(a_st[:, 1, :], t["ssm_a_im"][0].rearrange("(j g) p -> j (g p)", g=2)).then_inc(ld_a, 16)
            sp.dma_start(dt_st[:, :], t["ssm_log_dt"][0].rearrange("(j g) -> j g", g=2)).then_inc(ld_a, 16)
            for ri, name in enumerate(("ssm_b_re", "ssm_b_im")):
                sp.dma_start(b_st[:, ri, :], t[name][0].rearrange("(j g) p h -> j (g p h)", g=2)).then_inc(ld_b, 16)
            xv = t["x"][0].rearrange("(c s) (hf f) -> hf c s f", s=TAU, hf=2)
            for hf in range(2):
                sp.dma_start(xnat[hf * 64:hf * 64 + 64, :, :], xv[hf]).then_inc(ld_x, 16)
            for ri, name in enumerate(("ssm_c_re", "ssm_c_im")):
                cv = t[name][0].rearrange("(n q) h p -> (q h) n p", q=8)
                for dup in range(2):
                    sp.dma_start(c_st[:, ri, :, dup, :], cv).then_inc(ld_c, 16)
            for hf in range(2):
                sp.dma_start(d_bc[hf * 64:hf * 64 + 64, :],
                             t["ssm_d"][:, hf * 512:hf * 512 + 512].to_broadcast([64, 512])).then_inc(ld_d, 16)
            row = 0
            for name in ("ln_mix_g", "ln_mix_b", "ln_ffn_g", "ln_ffn_b", "norm_mix_g_2", "norm_ffn_g_2"):
                sp.dma_start(prm_st[row:row + 2 * DC, :], t[name].rearrange("l (c p) -> (l c) p", p=P)).then_inc(ld_prm, 16)
                row += 2 * DC
            sp.dma_start(conv_st[0:TAPS * FC, :, :],
                         t["ffn_conv_w_2"].rearrange("l k (c p) -> (k c) l p", p=P)).then_inc(ld_prm, 16)
            sp.dma_start(conv_st[TAPS * FC:CROW, :, :],
                         t["ffn_conv_b_2"].rearrange("l (c p) -> c l p", p=P)).then_inc(ld_prm, 16)
            sp.dma_start(small_st[0:4, :], t["od_b_a_2"][0].rearrange("(c p) -> c p", p=P)).then_inc(ld_prm, 16)
            sp.dma_start(small_st[4:6, :], t["od_head_g_2"][0].rearrange("(c p) -> c p", p=P)).then_inc(ld_prm, 16)
            for row, name in ((6, "ev_q_g_2"), (7, "ev_k_g_2")):
                for dup in range(2):
                    sp.dma_start(small_st[row:row + 1, dup * HD:(dup + 1) * HD], t[name]).then_inc(ld_prm, 16)
            sp.wait_ge(v_ready, 8)
            sp.wait_ge(w_ready, 8)
            sp.wait_ge(prm_copied, 1)
            sp.wait_ge(k_done, 4)
            sp.wait_ge(k_copied, 4)
            sp.wait_ge(toe_zero, 1)
            for s in range(TAU):
                for q in range(4):
                    sp.dma_start(toe[s * GH:(s + 1) * GH, (q // 2) * 32 + q % 2:(q // 2) * 32 + 32:2, s * GH:P],
                                 k_rows[q * 32:q * 32 + GH, :, 0:P - s * GH]).then_inc(toe_ready, 16)
            for name in run:
                st = ST[name]
                first = 1 if st.it0 == 0 else 0
                if first:
                    for half in range(2):
                        sp.dma_start(tile_view(wst, name, half), tile_source(name, 0, half)).then_inc(w_landed[half], 16)
                with sp.Fori(0, st.iters - first) as i:
                    for half in range(2):
                        source = tile_source(name, i, half, first)
                        sp.wait_ge(wlo_done, i * 2 + ((st.it0 + first) * 2 + half - 1))
                        sp.dma_start(tile_view(wst, name, half), source).then_inc(w_landed[half], 16)
            for n in range(TT):
                sp.wait_ge(out_rows, n + 1)
                sp.dma_start(out[0, n * P:(n + 1) * P, :], out_t[:, n, :]).then_inc(out_done, 16)
            sp.wait_ge(out_done, TT * 16)

        @block.gpsimd
        def _(pool):
            link = linker(pool, pool_link)
            link(nc.gpsimd.memset(ident[:, :], 0.0))
            nc.gpsimd.affine_select(out=ident[:, :], in_=ident[:, :], compare_op=ALU.not_equal, fill=1.0, base=0,
                                    pattern=[[-1, P]], channel_multiplier=1).then_inc(consts, 1)
            nc.gpsimd.memset(toe[:, :, :], 0.0).then_inc(toe_zero, 1)
            link(nc.gpsimd.memset(after[:, :], 1.0))
            nc.gpsimd.affine_select(out=after[:, :], in_=after[:, :], compare_op=ALU.is_gt, fill=0.0, base=0,
                                    pattern=[[1, P]], channel_multiplier=-1).then_inc(consts, 1)
            link(nc.gpsimd.memset(before[:, :], 1.0))
            nc.gpsimd.affine_select(out=before[:, :], in_=before[:, :], compare_op=ALU.is_gt, fill=0.0, base=0,
                                    pattern=[[-1, P]], channel_multiplier=1).then_inc(consts, 1)
            pool.wait_ge(mask_ones, 1)
            nc.gpsimd.affine_select(out=chunk_mask[:, :], in_=chunk_mask[:, :], compare_op=ALU.is_ge, fill=0.0, base=0,
                                    pattern=[[1, P]], channel_multiplier=-1).then_inc(consts, 1)
            pool.wait_ge(c_copied, 16)
            pool.wait_ge(lam_ready, 1)
            pool.wait_ge(tr_u, 8)
            shape = [P, 4, LAGS, GH]
            with pool.Fori(0, PAIRS // 4) as i:
                js = bass.ds(i * 4, 4)
                l4 = [lam[:, ri, :, js].rearrange("p k j -> p j k").unsqueeze(3).to_broadcast(shape) for ri in range(2)]
                c4 = [ct[:, ri, js, :].unsqueeze(2).to_broadcast(shape) for ri in range(2)]
                wr, wi = w_re[:, js, :, :], w_im[:, js, :, :]
                nc.gpsimd.tensor_tensor(wr, c4[0], l4[0], ALU.mult).then_inc(pool_link, 1)
                nc.gpsimd.tensor_tensor(w_tmp[:, 0], c4[1], l4[1], ALU.mult).then_inc(pool_link, 1)
                nc.gpsimd.tensor_tensor(wi, c4[0], l4[1], ALU.mult).then_inc(pool_link, 1)
                nc.gpsimd.tensor_tensor(w_tmp[:, 1], c4[1], l4[0], ALU.mult).then_inc(pool_link, 1)
                pool.wait_ge(pool_link, i * 4 + 7)
                nc.gpsimd.tensor_tensor(pool_pad[:, :], one_col[:, :], one_col[:, :], ALU.mult)
                nc.gpsimd.tensor_tensor(wr, wr, w_tmp[:, 0], ALU.subtract)
                nc.gpsimd.tensor_tensor(wi, wi, w_tmp[:, 1], ALU.add).then_inc(w_ready, 1)
                pool.wait_ge(w_ready, i + 1)
            w_flat = w_im[:, :, :, :].rearrange("p j k h -> p (j k h)")
            nc.gpsimd.tensor_scalar(w_flat, w_flat, -1.0, 0.0, ALU.mult, ALU.add).then_inc(w_ready, 1)
            pool.wait_ge(tr_x, 8)
            pool.wait_ge(tr_u, 8)
            pool.wait_ge(ld_d, 32)
            nc.gpsimd.tensor_tensor(xnat[:, :, :], xnat[:, :, :], d_bc[:, :].unsqueeze(1).to_broadcast([P, TAU, 512]),
                                    ALU.mult).then_inc(xd_ready, 1)

            pool.wait_ge(consts, 4)
            pool.wait_ge(evac_done, ST["v"].evac1)

            def stage_pair(i, pp):
                p = i * 2 + pp
                nc.gpsimd.tensor_copy(q_pair[:, pp:pp + 1, :], q_f[:, bass.ds(p, 1), :])
                nc.gpsimd.tensor_copy(k_pair[:, pp:pp + 1, :], k_f[:, bass.ds(p, 1), :])
                nc.gpsimd.tensor_copy(v_pair[:, pp, :, :], v_t[:, :, bass.ds(p * P, P)]).then_inc(qkv_staged, 1)

            def mask_tiles(buf, done, masked, count):
                pool.wait_ge(done, count)
                tiles = buf[:, 0:512].rearrange("p (j q) -> p j q", j=TT)
                nc.gpsimd.tensor_tensor(tiles, tiles, after[:, :].unsqueeze(1).to_broadcast([P, TT, P]),
                                        ALU.mult).then_inc(masked, 1)

            def heads4(i, last):
                for hd in range(4):
                    if not (last and hd == 3):
                        mask_tiles(drop[:, (hd + 1) % 2, :], sp_done, sp_masked, i * 4 + (hd + 2))
                    mask_tiles(keep[:, hd % 2, :], w_done, w_masked, i * 4 + (hd + 1))
                    if hd % 2 == 1 and not last:
                        pool.wait_ge(o_done, i * 4 + (hd + 2))
                        stage_pair(i + 1, hd // 2)

            for pp in range(2):
                stage_pair(0, pp)
            mask_tiles(drop[:, 0, :], sp_done, sp_masked, 1)
            with pool.Fori(0, HEADS // 4 - 1) as i:
                heads4(i, False)
            heads4(HEADS // 4 - 1, True)

            pool.wait_ge(part_done, ST["down1"].part1)
            pool.dma_start(ws_st[:, :, :], t["ev_a_ws_2"][0].rearrange("g t s -> t g s")).then_inc(ld_even, 16)
            pool.dma_start(bs_st[:, :, :], t["ev_a_bs_2"]).then_inc(ld_even, 16)
            for n, name in enumerate(("ev_a_ln_g_2", "ev_a_ln_b_2")):
                pool.dma_start(gv_gb[:, n, :], t[name].to_broadcast([P, 512])).then_inc(ld_even, 16)
            pool.wait_ge(x_ready, 5 * DC)
            nc.gpsimd.memset(resid4[:, :, :], 0.0).then_inc(s4_ready, 1)
            pool.wait_ge(s4_ready, 1)
            for n, m in enumerate((4, 16)):
                nc.gpsimd.affine_select(out=resid4[:, n, :].rearrange("p (a b) -> p a b", b=m),
                                        in_=resid4[:, n, :].rearrange("p (a b) -> p a b", b=m),
                                        compare_op=ALU.not_equal, fill=1.0, base=0, pattern=[[0, P // m], [-1, m]],
                                        channel_multiplier=1).then_inc(s4_ready, 1)
            pool.wait_ge(ws_copied, 2)
            for g in range(8):
                nc.gpsimd.affine_select(out=ws_t[:, g, :], in_=ws_t[:, g, :], compare_op=ALU.is_ge, fill=0.0, base=0,
                                        pattern=[[1, P]], channel_multiplier=-1).then_inc(ws_ready, 1)
            pool.wait_ge(evac_done, ST["ev_vb"].evac1)
            with pool.Fori(0, 2) as i:
                pool.wait_ge(pv_done, i * 4 + 1)
                for pp in range(2):
                    nc.gpsimd.tensor_copy(vb_pair[:, pp, :, :],
                                          vb_t[:, :, bass.ds(i * 256 + pp * P, P)]).then_inc(vb_staged, 1)

            pool.wait_ge(part_done, ST["cdown0"].part1)
            pool.wait_ge(x_ready, 7 * DC)
            nc.gpsimd.memset(wga[:, :, :], 0.0).then_inc(wga_zero, 1)
            pool.wait_ge(wga_zero, 1)
            pool.dma_start(wga[:, :, 0:GATE_RANK], t["od_w_in_2"][0].rearrange("(k p) n -> p k n", p=P)[:, :, 3072:3088])\
                .then_inc(ld_odd, 16)
            pool.dma_start(wa2[:, :], t["od_w_a2_2"][0]).then_inc(ld_odd, 16)

        @block.tensor
        def _(pe):
            pe.wait_ge(consts, 1)
            pe.wait_ge(a_rows, 1)
            for n in range(3):
                mm = nc.tensor.transpose(bank[0][:, n * PAIRS:(n + 1) * PAIRS], a_st[:, n, :], ident[0:PAIRS, 0:PAIRS])
            mm.then_inc(tr_a, 1)
            pe.wait_ge(ld_b, 32)
            for ri in range(2):
                rows = b_st[:, ri, :].rearrange("j (q h) -> j h q", h=GH)
                for h in range(GH):
                    mm = nc.tensor.transpose(bank[1 + ri][:, h * PAIRS:(h + 1) * PAIRS], rows[:, h, :],
                                             ident[0:PAIRS, 0:PAIRS])
                mm.then_inc(tr_b, 1)
            pe.wait_ge(ld_c, 64)
            for ri in range(2):
                for n in range(8):
                    mm = nc.tensor.transpose(bank[3 + 2 * ri + n // 4][:, (n % 4) * P:(n % 4 + 1) * P],
                                             c_st[:, ri, n, :, :].rearrange("p a b -> p (a b)"), ident[:, :])
                    if n % 4 == 3:
                        mm.then_inc(tr_c, 1)
            pe.wait_ge(ld_prm, 14 * 16)
            nc.tensor.transpose(bank[7][:, 0:NROW], prm_st[:, :], ident[0:NROW, 0:NROW])
            for layer in range(2):
                at_ = NROW + layer * CROW
                nc.tensor.transpose(bank[7][:, at_:at_ + CROW], conv_st[:, layer, :], ident[0:CROW, 0:CROW])
            nc.tensor.transpose(bank[7][:, small0:small0 + SROW], small_st[:, :], ident[0:SROW, 0:SROW]).then_inc(tr_prm, 1)
            pe.wait_ge(x_permuted, 1)
            pe.wait_ge(dve_link, 1)
            for b in range(8):
                if b == 1:
                    pe.wait_ge(b_copied, 2)
                if b == 3:
                    pe.wait_ge(c_copied, 16)
                if b == 7:
                    pe.wait_ge(prm_copied, 1)
                for n in range(8):
                    g = b * 8 + n
                    hf = g // 32
                    rows = x_perm[hf * 64:hf * 64 + 64, g % 32, :, :].rearrange("p s h -> p (s h)")
                    mm = nc.tensor.transpose(bank[b][:, n * NCH:(n + 1) * NCH], rows,
                                             ident[hf * 64:hf * 64 + 64, hf * 64:hf * 64 + 64])
                mm.then_inc(tr_u, 1)
            pe.wait_ge(u_copied, 4)
            with pe.Fori(0, 4) as i:
                for buf in range(2):
                    pe.wait_ge(v_ready, i * 2 + buf + 1)
                    pe.wait_ge(vt_copied, i * 4 + (buf * 2 + 1))
                    for ri in range(2):
                        for jj in range(4):
                            mm = nc.tensor.transpose(bank[2 * buf + ri][:, jj * P:(jj + 1) * P], v_buf[:, buf, ri, jj, :],
                                                     ident[:, :])
                        mm.then_inc(tr_v, 1)
            pe.wait_ge(w_ready, 9)
            pe.wait_ge(u_copied, 8)
            for b in range(4):
                for q in range(4):
                    for s in range(4):
                        g = (q // 2) * 32 + 2 * (b * 4 + s) + q % 2
                        j, half = g // 2, (g % 2) * 64
                        for ri, w in enumerate((w_re, w_im)):
                            mm = nc.tensor.matmul(bank[4 + b][q * 32:q * 32 + 32, s * P:(s + 1) * P],
                                                  bb[half:half + 64, ri, :, j], w[half:half + 64, j, 0:TAU, :], start=(ri == 0), stop=(ri == 1))
                mm.then_inc(k_done, 1)
            pe.wait_ge(vt_copied, 17)
            for b in range(8):
                if b == 4:
                    pe.wait_ge(k_copied, 4)
                for jj in range(4):
                    for ri in range(2):
                        for half in range(2):
                            j = b * 4 + jj
                            mm = nc.tensor.matmul(bank[b][half * 64:half * 64 + 64, (jj * 2 + ri) * NCH:(jj * 2 + ri + 1) * NCH],
                                                  vt[:, ri, j, half * 64:half * 64 + 64], uu[:, 2 * j + half, :],
                                                  start=True, stop=True)
                mm.then_inc(s_in, 1)
            for f in range(DC):
                pe.wait_ge(s_copied, f + 1)
                hf = f // 4
                for s in range(TAU):
                    mm = nc.tensor.transpose(bank[f][:, s * NCH:(s + 1) * NCH],
                                             xnat[hf * 64:hf * 64 + 64, s, (f % 4) * P:(f % 4 + 1) * P],
                                             ident[hf * 64:hf * 64 + 64, hf * 64:hf * 64 + 64])
                mm.then_inc(tr_x, 1)
            pe.wait_ge(toe_ready, 32 * 16)
            pe.wait_ge(scan_done, 1)
            for b in range(8):
                pe.wait_ge(x_ready, b + 1)
                for hf in range(2):
                    for s in range(4):
                        g = hf * 32 + (b // 2) * 8 + 2 * s + b % 2
                        j, half = g // 2, (g % 2) * 64
                        dst = bank[b][hf * 64:hf * 64 + 64, s * P:(s + 1) * P]
                        nc.tensor.matmul(dst, uu[:, g, :], toe[:, g, :], start=True, stop=False)
                        for ri, w in enumerate((w_re, w_im)):
                            mm = nc.tensor.matmul(dst, states[half:half + 64, 0:NCH, ri, j],
                                                  w[half:half + 64, j, 1:LAGS, :], start=False, stop=(ri == 1))
                mm.then_inc(y_done, 1)
            for f in range(DC):
                pe.wait_ge(y_copied, 8)
                hf = f // 4
                for s in range(TAU):
                    mm = nc.tensor.transpose(bank[f][:, s * NCH:(s + 1) * NCH],
                                             xnat[hf * 64:hf * 64 + 64, s, (f % 4) * P:(f % 4 + 1) * P],
                                             ident[hf * 64:hf * 64 + 64, hf * 64:hf * 64 + 64])
                mm.then_inc(tr_y, 1)

            def products(dst, name, half, col, kn, xh, xl, k0, start, stop):
                wh, wl = tile_view(whi, name, half), tile_view(wlo, name, half)
                for k in range(kn):
                    hi, lo = wh[:, k, col:col + P], wl[:, k, col:col + P]
                    nc.tensor.matmul(dst, hi, xh[:, k0 + k, :], start=(start and k == 0), stop=False)
                    nc.tensor.matmul(dst, hi, xl[:, k0 + k, :], start=False, stop=False)
                    mm = nc.tensor.matmul(dst, lo, xh[:, k0 + k, :], start=False, stop=(stop and k == kn - 1))
                return mm

            def feature_stage(name, xh, xl):
                st = ST[name]
                pe.wait_ge(evac_done, st.evac0)
                with pe.Fori(0, st.iters) as i:
                    for half in range(2):
                        pe.wait_ge(wlo_done, i * 2 + (st.it0 * 2 + half + 1))
                        for u in range(2):
                            b = 2 * half + u
                            if st.evacs == 2:
                                pe.wait_ge(evac_done, i * 2 + (st.evac0 + u - 1))
                            else:
                                pe.wait_ge(evac_done, i * 4 + (st.evac0 + b - 3))
                            mm = products(bank[b][:, :], name, half, u * P, DC, xh, xl, 0, True, True)
                            mm.then_inc(part_done, 1)

            def down_stage(name):
                st = ST[name]
                pe.wait_ge(evac_done, st.evac0)
                with pe.Fori(0, st.iters // 2) as i:
                    for u in range(2):
                        pe.wait_ge(evac_done, i * 2 + (st.evac0 + u - 1))
                        for half in range(2):
                            pe.wait_ge(wlo_done, i * 4 + ((st.it0 + u) * 2 + half + 1))
                            mm = products(bank[u][:, :], name, half, 0, DOWN_K, hhi, hlo, half * DOWN_K, half == 0, half == 1)
                            mm.then_inc(part_done, 1)

            def norm(n, st, mean):
                pe.wait_ge(res_ready, st.res1)
                if mean:
                    for c in range(DC):
                        mm = nc.tensor.matmul(bank[4][:, :], ones_mean[:, :], res[:, c, :], start=(c == 0), stop=(c == DC - 1))
                    mm.then_inc(ln_mean, 1)
                for c in range(DC):
                    pe.wait_ge(ln_sq, n * DC + c + 1)
                    nc.tensor.matmul(bank[5][:, :], ones_mean[:, :], sq[:, c % 2, :], start=(c == 0),
                                     stop=(c == DC - 1)).then_inc(ln_sq_used, 1)

            def token_stage(name, xh, xl):
                st = ST[name]
                pe.wait_ge(evac_done, st.evac0)
                with pe.Fori(0, st.iters) as i:
                    for half in range(2):
                        pe.wait_ge(wlo_done, i * 2 + (st.it0 * 2 + half + 1))
                        wh, wl = tile_view(whi, name, half), tile_view(wlo, name, half)
                        for n in range(TT):
                            pe.wait_ge(evac_done, i * 8 + (st.evac0 + 4 * half + n - 7))
                            dst = bank[4 * half + n][:, 0:256]
                            for k in range(DC):
                                hi, lo = xh[:, k, n * P:(n + 1) * P], xl[:, k, n * P:(n + 1) * P]
                                nc.tensor.matmul(dst, hi, wh[:, k, :], start=(k == 0), stop=False)
                                nc.tensor.matmul(dst, hi, wl[:, k, :], start=False, stop=False)
                                mm = nc.tensor.matmul(dst, lo, wh[:, k, :], start=False, stop=(k == DC - 1))
                            mm.then_inc(part_done, 1)

            def stick_attention():
                pe.wait_ge(evac_done, ST["v"].evac1)
                pe.wait_ge(consts, 4)

                def scores(pair, hd, count):
                    pe.wait_ge(qkv_staged, pair + 1)
                    if count is not None:
                        pe.wait_ge(lb_done, count)
                    half = slice((hd % 2) * 64, (hd % 2) * 64 + 64)
                    flat = psum[:, 0:3, :].rearrange("p b n -> p (b n)")
                    for j in range(TT):
                        kt = k_pair[half, (hd // 2) % 2, j * P:(j + 1) * P]
                        mm = nc.tensor.matmul(flat[:, j * P:(j + 1) * P], kt,
                                              q_pair[half, (hd // 2) % 2, j * P:(j + 1) * P],
                                              start=True, stop=True)
                        if j < TT - 1:
                            n = SEQ - (j + 1) * P
                            mm = nc.tensor.matmul(flat[:, REST[j]:REST[j] + n], kt,
                                                  q_pair[half, (hd // 2) % 2, (j + 1) * P:SEQ],
                                                  start=True, stop=True)
                    mm.then_inc(z_done, 1)

                def sums(hd, h):
                    pe.wait_ge(sp_masked, h + 1)
                    pe.wait_ge(lw_done, h + 1)
                    flat = psum[:, 4:7, :].rearrange("p b n -> p (b n)")
                    sp = drop[:, hd % 2, :]
                    for c0, c1 in ((0, 512), (512, 1024), (1024, 1280)):
                        nc.tensor.matmul(flat[:, c0:c1], before[:, :], sp[:, c0:c1], start=True, stop=(c0 == 0),
                                         skip_group_check=True)
                    for j in range(TT - 1):
                        for jj in range(j + 1, TT):
                            to = REST[j] + (jj - j - 1) * P
                            mm = nc.tensor.matmul(flat[:, to:to + P], ones[:, :], sp[:, jj * P:(jj + 1) * P],
                                                  start=False, stop=True, skip_group_check=True)
                            if jj < TT - 1:
                                n = SEQ - (jj + 1) * P
                                mm = nc.tensor.matmul(flat[:, to + P:to + P + n], ones[:, :], sp[:, REST[jj]:REST[jj] + n],
                                                      start=False, stop=True, skip_group_check=True)
                    mm.then_inc(cs_done, 1)

                def mix(hd, h, pair):
                    pe.wait_ge(w_masked, h + 1)
                    if hd % 2 == 0:
                        pe.wait_ge(o_ready, pair + 1)
                    half = (hd % 2) * 64
                    dst = bank[7][half:half + 64, :]
                    w = keep[:, hd % 2, :]
                    for j in range(TT):
                        vt_ = v_pair[:, (hd // 2) % 2, j, half:half + 64]
                        mm = nc.tensor.matmul(dst[:, j * P:(j + 1) * P], vt_, w[:, j * P:(j + 1) * P], start=(j == 0),
                                              stop=True, skip_group_check=True)
                        if j < TT - 1:
                            n = SEQ - (j + 1) * P
                            mm = nc.tensor.matmul(dst[:, (j + 1) * P:SEQ], vt_, w[:, REST[j]:REST[j] + n], start=False,
                                                  stop=True, skip_group_check=True)
                    mm.then_inc(o_done, 1)

                def heads4(i, last):
                    for hd in range(4):
                        if not (last and hd == 3):
                            scores(i * 2 + (hd + 1) // 2, (hd + 1) % 4, i * 4 + (hd + 2))
                        sums(hd, i * 4 + hd)
                        mix(hd, i * 4 + hd, i * 2 + hd // 2)

                scores(0, 0, None)
                with pe.Fori(0, HEADS // 4 - 1) as i:
                    heads4(i, False)
                heads4(HEADS // 4 - 1, True)

            def gated_mlp():
                pe.wait_ge(evac_done, ST["ev_vb"].evac1)
                pe.wait_ge(s4_ready, 3)
                nc.tensor.matmul(bank[0][:, 0:P], resid4[:, 0, :], resid4[:, 0, :], start=True, stop=False)
                nc.tensor.matmul(bank[0][:, 0:P], resid4[:, 1, :], resid4[:, 1, :], start=False, stop=True).then_inc(tab_done, 1)
                pe.wait_ge(ld_even, 4 * 16)
                for g in range(8):
                    mm = nc.tensor.transpose(bank[1 + g // 4][:, (g % 4) * P:(g % 4 + 1) * P], ws_st[:, g, :], ident[:, :])
                    if g % 4 == 3:
                        mm.then_inc(ws_tr, 1)
                for c in range(8):
                    pe.wait_ge(qk_sq, c + 1)
                    if c >= 4:
                        pe.wait_ge(qk_ln, c - 3)
                    nc.tensor.matmul(bank[3 + c % 4], head_mean[:, :], sq_even[:, c % 2, :], start=True,
                                     stop=True).then_inc(qk_ms, 1)
                pe.wait_ge(ws_ready, 8)
                pe.wait_ge(vn_ready, TT)
                for c in range(4):
                    if c >= 2:
                        pe.wait_ge(gm_copied, c - 1)
                    for gi in range(2):
                        g = 2 * c + gi
                        dst = bank[1 + c % 2][gi * 64:gi * 64 + 64, :]
                        nc.tensor.matmul(dst, ones[0:1, 0:64], bs_st[0:1, g:g + 1, :].to_broadcast([1, TT, P]), start=True,
                                         stop=False, skip_group_check=True)
                        for n in range(TT):
                            mm = nc.tensor.matmul(dst[:, n * P:(n + 1) * P], gv_t[:, n, g * 64:(g + 1) * 64], ws_t[:, g, :],
                                                  start=False, stop=True, skip_group_check=True)
                    mm.then_inc(gm_done, 1)

            def dilated_attention():
                pe.wait_ge(gm_copied, 4)
                pe.wait_ge(tables, 1)
                pe.wait_ge(qk_ln, 8)

                def scores(hd, h, pair):
                    pe.wait_ge(qn_ready, pair + 1)
                    half = slice((hd % 2) * 64, (hd % 2) * 64 + 64)
                    for n in range(TT):
                        pe.wait_ge(sm_done, h * 4 + (n + 1))
                        nc.tensor.matmul(bank[n][:, 0:(n + 1) * P], qn_pair[half, hd // 2, n * P:(n + 1) * P],
                                         kn_pair[half, hd // 2, 0:(n + 1) * P], start=True, stop=True).then_inc(sc_done, 1)

                def turn(hd, h):
                    pe.wait_ge(pt_copied, h + 1)
                    flat = psum[:, 4:7, :].rearrange("p b n -> p (b n)")
                    for n in range(TT):
                        pe.wait_ge(pn_done, h * 4 + (n + 1))
                        for j in range(n + 1):
                            to = PT_AT[j] + (n - j) * P
                            mm = nc.tensor.transpose(flat[:, to:to + P], prob[:, hd % 2, ROW_AT[n] + j * P:ROW_AT[n] + (j + 1) * P],
                                                     ident[:, :])
                    mm.then_inc(tr_p, 1)

                def mix(hd, h, pair):
                    pe.wait_ge(pt_copied, h + 2)
                    pe.wait_ge(vb_staged, pair + 1)
                    if hd % 2 == 0:
                        pe.wait_ge(b_ready, pair + 1)
                    half = (hd % 2) * 64
                    for j in range(TT):
                        mm = nc.tensor.matmul(bank[7][half:half + 64, j * P:SEQ], vb_pair[:, hd // 2, j, half:half + 64],
                                              prob_t[:, PT_AT[j]:PT_AT[j] + SEQ - j * P], start=(j == 0), stop=(j == TT - 1))
                    mm.then_inc(pv_done, 1)

                with pe.Fori(0, 2) as i:
                    scores(0, i * 4, i * 2)
                    for hd in range(4):
                        if hd < 3:
                            scores(hd + 1, i * 4 + (hd + 1), i * 2 + (hd + 1) // 2)
                        turn(hd, i * 4 + hd)
                        mix(hd, i * 4 + hd, i * 2 + hd // 2)

            def linear_attention():
                pe.wait_ge(evac_done, ST["od_r"].evac1)
                pe.wait_ge(wga_ready, 1)
                for k in range(DC):
                    nc.tensor.matmul(bank[4], wga_hi[:, k, :], xhi[:, k, :], start=(k == 0), stop=False)
                    nc.tensor.matmul(bank[4], wga_hi[:, k, :], xlo[:, k, :], start=False, stop=False)
                    mm = nc.tensor.matmul(bank[4], wga_lo[:, k, :], xhi[:, k, :], start=False, stop=(k == DC - 1))
                mm.then_inc(ga_done, 1)
                pe.wait_ge(ga_copied, 1)
                for h in range(GLA_HEADS):
                    nc.tensor.matmul(bank[h], wa2[:, h * P:(h + 1) * P], ga_t[0:GATE_RANK, :], start=True,
                                     stop=True).then_inc(la_done, 1)
                pe.wait_ge(gq_done, 1)
                pe.wait_ge(gkt_done, 1)
                for h in range(GLA_HEADS):
                    for n in range(TT):
                        mm = nc.tensor.matmul(bank[4 + h][:, n * P:(n + 1) * P], gkt[:, h, n * P:(n + 1) * P],
                                              gq[:, h, n * P:(n + 1) * P], start=True, stop=True)
                    mm.then_inc(at_done, 1)
                pe.wait_ge(gks_done, 1)
                for n in range(TT):
                    for h in range(GLA_HEADS):
                        mm = nc.tensor.transpose(bank[n][:, h * P:(h + 1) * P], gks[:, h, n * P:(n + 1) * P], ident[:, :])
                    mm.then_inc(tr_k, 1)
                pe.wait_ge(kt_copied, TT)
                pe.wait_ge(at_ready, GLA_HEADS)
                for h in range(GLA_HEADS):
                    for hf in range(2):
                        for m in range(2):
                            for a in range(2):
                                n = 4 * m + 2 * a + hf
                                if n == GLA_CHUNKS - 1:
                                    continue
                                rows = slice(hf * 64, hf * 64 + 64)
                                if h > 0:
                                    pe.wait_ge(st_ready, h * GLA_CHUNKS)
                                mm = nc.tensor.matmul(bank[2 * hf + m][:, a * GLA_DV:(a + 1) * GLA_DV],
                                                      gks_t[rows, n // 2, h, :],
                                                      gvt[rows, n // 2, h * GLA_DV:(h + 1) * GLA_DV], start=True, stop=True)
                    mm.then_inc(kv_done, 1)
                    pe.wait_ge(st_ready, (h + 1) * GLA_CHUNKS)
                    for dv in range(2):
                        dst = bank[4 + 2 * (h % 2) + dv]
                        if h >= 2:
                            pe.wait_ge(go_copied, 2 * (h - 2) + dv + 1)
                        cols = slice(h * GLA_DV + dv * P, h * GLA_DV + (dv + 1) * P)
                        for n in range(TT):
                            nc.tensor.matmul(dst[:, n * P:(n + 1) * P], gvt[:, n, cols], attn_t[:, h, n, :], start=(n == 0),
                                             stop=False, skip_group_check=True)
                        for n in range(GLA_CHUNKS):
                            to = slice(n * GLA_CHUNK, (n + 1) * GLA_CHUNK)
                            mm = nc.tensor.matmul(dst[:, to], gst[:, h % 2, n, dv * P:(dv + 1) * P], gq[:, h, to],
                                                  start=False, stop=(n == GLA_CHUNKS - 1), skip_group_check=True)
                        mm.then_inc(go_done, 1)
                for h in range(GLA_HEADS):
                    for dv in range(2):
                        pe.wait_ge(go_sq, 2 * h + dv + 1)
                        mm = nc.tensor.matmul(bank[h], ones[:, :], sq_odd[:, dv, :], start=(dv == 0), stop=(dv == 1))
                        mm.then_inc(go_ms, 1)

            for name in run:
                if name == "glu":
                    pe.wait_ge(hid_ready, DC)
                    feature_stage(name, hhi, hlo)
                elif name == "ssm_out":
                    pe.wait_ge(hid_ready, 2 * DC)
                    feature_stage(name, hhi[:, DC:2 * DC, :], hlo[:, DC:2 * DC, :])
                    norm(0, ST[name], True)
                elif name == "gu0":
                    pe.wait_ge(x_ready, 2 * DC)
                    feature_stage(name, xhi, xlo)
                elif name == "down0":
                    pe.wait_ge(hid_ready, ST[name].pair0)
                    down_stage(name)
                    norm(1, ST[name], True)
                elif name == "q":
                    pe.wait_ge(x_ready, 3 * DC)
                    feature_stage(name, xhi, xlo)
                elif name == "k":
                    feature_stage(name, xhi, xlo)
                elif name == "v":
                    token_stage(name, xhi, xlo)
                    stick_attention()
                elif name == "w_o":
                    pe.wait_ge(o_ready, DC + 1)
                    feature_stage(name, hhi, hlo)
                    norm(2, ST[name], True)
                elif name == "gu1":
                    pe.wait_ge(x_ready, 4 * DC)
                    feature_stage(name, xhi, xlo)
                elif name == "down1":
                    pe.wait_ge(hid_ready, ST[name].pair0)
                    down_stage(name)
                    norm(3, ST[name], True)
                    norm(4, ST[name], False)
                elif name in ("ev_u", "ev_qk"):
                    pe.wait_ge(x_ready, 5 * DC)
                    feature_stage(name, xhi, xlo)
                elif name in ("ev_v", "ev_vb"):
                    token_stage(name, xhi, xlo)
                    if name == "ev_vb":
                        gated_mlp()
                        dilated_attention()
                elif name == "ev_out":
                    pe.wait_ge(gm_ready, 4)
                    pe.wait_ge(b_ready, 5)
                    feature_stage(name, xhi, xlo)
                    norm(5, ST[name], False)
                elif name in ("conv0", "conv1"):
                    pe.wait_ge(x_ready, (6 if name == "conv0" else 8) * DC)
                    feature_stage(name, xhi, xlo)
                elif name in ("cdown0", "cdown1"):
                    pe.wait_ge(hid_ready, ST[name].pair0)
                    down_stage(name)
                    if name == "cdown0":
                        norm(6, ST[name], False)
                    else:
                        pe.wait_ge(res_ready, ST[name].res1)
                        for n in range(TT):
                            for c in range(DC):
                                mm = nc.tensor.transpose(bank[2 * n + c // 4][:, (c % 4) * P:(c % 4 + 1) * P],
                                                         res[:, c, n * P:(n + 1) * P], ident[:, :])
                                if c % 4 == 3:
                                    mm.then_inc(tr_out, 1)
                elif name in ("od_q", "od_k"):
                    pe.wait_ge(x_ready, 7 * DC)
                    feature_stage(name, xhi, xlo)
                elif name == "od_v":
                    token_stage(name, xhi, xlo)
                elif name == "od_r":
                    feature_stage(name, xhi, xlo)
                    linear_attention()
                elif name == "od_out":
                    pe.wait_ge(go_ready, DC)
                    feature_stage(name, xhi, xlo)
                    norm(7, ST[name], False)

        @block.scalar
        def _(act):
            act.wait_ge(tr_c, 4)
            for ri in range(2):
                for n in range(8):
                    src = bank[3 + 2 * ri + n // 4][:, (n % 4) * P:(n % 4 + 1) * P].rearrange(
                        "p (j g h) -> p j g h", g=2, h=GH)
                    for gi in range(2):
                        half = slice(gi * 64, gi * 64 + 64)
                        ins = nc.scalar.copy(ct[half, ri, n * 4:(n + 1) * 4, :], src[half, :, gi, :])
                    ins.then_inc(c_copied, 1)
            act.wait_ge(tr_prm, 1)
            nc.scalar.copy(prm[:, :], bank[7][:, 0:small0 + SROW]).then_inc(prm_copied, 1)
            act.wait_ge(trig_in, 1)
            nc.scalar.activation(sp_[:, 8, :], sp_[:, 6, :], ACT.Sin).then_inc(trig_out, 1)
            nc.scalar.activation(sp_[:, 9, :], sp_[:, 7, :], ACT.Sin).then_inc(trig_out, 1)
            for b in range(8):
                act.wait_ge(tr_u, b + 1)
                nc.scalar.copy(uu[:, b * 8:(b + 1) * 8, :],
                               bank[b][:, :].rearrange("p (g c) -> p g c", g=8)).then_inc(u_copied, 1)
            with act.Fori(0, 4) as i:
                for buf in range(2):
                    for ri in range(2):
                        act.wait_ge(tr_v, i * 4 + (buf * 2 + ri + 2))
                        nc.scalar.copy(vt[:, ri, bass.ds(i * 8 + buf * 4, 4), :],
                                       bank[2 * buf + ri][:, :].rearrange("p (j n) -> p j n", j=4)).then_inc(vt_copied, 1)
            for b in range(4):
                act.wait_ge(k_done, b + 1)
                nc.scalar.copy(k_rows[:, b * 4:(b + 1) * 4, :],
                               bank[4 + b][:, :].rearrange("p (g n) -> p g n", g=4)).then_inc(k_copied, 1)
            for b in range(8):
                act.wait_ge(s_in, b + 1)
                src = bank[b][:, :].rearrange("p (j r c) -> p r c j", j=4, r=2)
                dst = states[:, 1:NCH + 1, :, b * 4:(b + 1) * 4].rearrange("p c r j -> p r c j")
                nc.scalar.copy(dst, src).then_inc(s_copied, 1)
            for f in range(DC):
                act.wait_ge(tr_x, f + 1)
                nc.scalar.copy(xhi[:, f, :].rearrange("p (c s) -> p s c", s=TAU),
                               bank[f][:, :].rearrange("p (s c) -> p s c", s=TAU)).then_inc(xhi_done, 1)
            for f in range(DC):
                act.wait_ge(tr_y, f + 1)
                if f >= 2:
                    act.wait_ge(hid_ready, f - 1)
                nc.scalar.activation(tmp_a[:, f % 2, :].rearrange("p (c s) -> p s c", s=TAU),
                                     bank[f][:, :].rearrange("p (s c) -> p s c", s=TAU),
                                     ACT.Gelu_apprx_tanh).then_inc(gelu_done, 1)

            def split(it, half, wait_parts):
                act.wait_ge(w_landed[half], it * 16 + 16)
                if wait_parts is not None:
                    act.wait_ge(part_done, wait_parts)
                nc.scalar.copy(whi[:, half, :], wst[:, half, :]).then_inc(whi_done, 1)

            def stage_loop(name, body):
                st = ST[name]
                last = name == run[-1]
                def split_next(i):
                    def do(half):
                        split(i + (st.it0 + 1), half, i * st.parts + (st.part0 + st.parts // 2 * (half + 1)))
                    return do
                if st.iters > last:
                    with act.Fori(0, st.iters - last) as i:
                        body(i, split_next(i))
                if last:
                    body(st.iters - 1, lambda half: None)

            def gate_stage(name, func):
                st = ST[name]
                def body(i, split_next):
                    split_next(0)
                    for u in range(2):
                        act.wait_ge(part_done, i * 4 + (st.part0 + u + 1))
                        act.wait_ge(evac_done, i * 2 + (st.evac0 + u - 1))
                        nc.scalar.activation(tmp_a[:, u, :], bank[u][:, :], func).then_inc(act_out, 1)
                    split_next(1)
                stage_loop(name, body)

            def split_stage(name):
                def body(i, split_next):
                    split_next(0)
                    split_next(1)
                stage_loop(name, body)

            def norm(n, mean, bias, split_out):
                link_base = n * 2
                for c in range(DC):
                    if mean:
                        act.wait_ge(ln_xc, n * DC + c + 1)
                    elif c == 0:
                        if n == 4:
                            act.wait_ge(ln_a, 4 * DC)
                        else:
                            act.wait_ge(res_ready, n * DC)
                    if n * DC + c >= 2:
                        act.wait_ge(ln_sq_used, n * DC + c - 1)
                    nc.scalar.activation(sq[:, c % 2, :], res[:, c, :], ACT.Square).then_inc(ln_sq, 1)
                act.wait_ge(ln_sq_used, (n + 1) * DC)
                nc.scalar.activation(rstd, bank[5][:, :], ACT.Ln,
                                     bias=(eps_ln if n < 4 else eps_rms)[:, 0:1]).then_inc(act_link, 1)
                act.wait_ge(act_link, 2 * n + 1)
                nc.scalar.activation(rstd, rstd, ACT.Exp, scale=-0.5).then_inc(act_link, 1)
                if bias is not None:
                    gcol, bcol = bias
                    for c in range(DC):
                        act.wait_ge(ln_n, n * DC + c + 1)
                        nc.scalar.activation(res[:, c, :], res[:, c, :], ACT.Identity, bias=prm[:, bcol + c:bcol + c + 1],
                                             scale=prm[:, gcol + c:gcol + c + 1]).then_inc(ln_a, 1)

            def stick_attention():
                def soft(hd, h):
                    act.wait_ge(z_done, h + 1)
                    act.wait_ge(lb_done, h + 1)
                    z = psum[:, 0:3, :].rearrange("p b n -> p (b n)")[:, 0:STICK]
                    nc.scalar.activation(lnp[:, :], z, ACT.Abs).then_inc(soft_link, 1)
                    act.wait_ge(soft_link, h * 2 + 1)
                    nc.scalar.activation(lnp[:, :], lnp[:, :], ACT.Exp, scale=-1.0).then_inc(soft_link, 1)
                    act.wait_ge(soft_link, h * 2 + 2)
                    nc.scalar.activation(lnp[:, :], lnp[:, :], ACT.Ln, bias=one_col[:, 0:1]).then_inc(ln_part, 1)

                def weigh(hd, h):
                    act.wait_ge(lw_done, h + 2)
                    nc.scalar.activation(keep[:, hd % 2, :], keep[:, hd % 2, :], ACT.Exp).then_inc(w_done, 1)

                def heads4(i, last):
                    for hd in range(4):
                        if not (last and hd == 3):
                            soft((hd + 1) % 4, i * 4 + (hd + 1))
                        weigh(hd, i * 4 + hd)

                soft(0, 0)
                with act.Fori(0, HEADS // 4 - 1) as i:
                    heads4(i, False)
                heads4(HEADS // 4 - 1, True)

            def feature_stage(name, func, dst):
                st = ST[name]
                def body(i, split_next):
                    for half in range(2):
                        for u in range(2):
                            n = 2 * half + u
                            act.wait_ge(part_done, i * 4 + (st.part0 + n + 1))
                            nc.scalar.activation(dst[:, bass.ds(i * 4 + n, 1), :], bank[n].unsqueeze(1), func).then_inc(evac_done, 1)
                        split_next(half)
                stage_loop(name, body)

            def token_stage(name, func, dst):
                st = ST[name]
                def body(i, split_next):
                    for half in range(2):
                        for n in range(TT):
                            act.wait_ge(part_done, i * 8 + (st.part0 + 4 * half + n + 1))
                            nc.scalar.activation(dst[:, n, bass.ds(i * 512 + half * 256, 256)], bank[4 * half + n][:, 0:256],
                                                 func).then_inc(evac_done, 1)
                        split_next(half)
                stage_loop(name, body)

            def conv_stage(name):
                st = ST[name]
                layer = int(name[-1])
                def body(i, split_next):
                    split_next(0)
                    for u in range(2):
                        act.wait_ge(part_done, i * 4 + (st.part0 + u + 1))
                        act.wait_ge(evac_done, i * 2 + (st.evac0 + u - 1))
                        nc.scalar.activation(tmp_a[:, u, :], bank[u], ACT.Identity, bias=tap(layer, TAPS, i * 2 + u),
                                             scale=tap(layer, TAPS - 1, i * 2 + u)).then_inc(conv_a, 1)
                    for u in range(2):
                        act.wait_ge(conv_b, i * 2 + (st.evac1 - st.evac0) * layer + (u + 1))
                        nc.scalar.activation(tmp_a[:, u, :], tmp_a[:, u, :], ACT.Silu).then_inc(act_out, 1)
                    split_next(1)
                stage_loop(name, body)

            def gated_mlp():
                for n in range(2):
                    act.wait_ge(ws_tr, n + 1)
                    nc.scalar.copy(ws_t[:, 4 * n:4 * n + 4, :], bank[1 + n].rearrange("p (g s) -> p g s", g=4)).then_inc(ws_copied, 1)
                act.wait_ge(evac_done, ST["ev_vb"].evac1)
                for c in range(9):
                    if c < 8:
                        if c >= 2:
                            act.wait_ge(qk_ms, c - 1)
                        nc.scalar.activation(sq_even[:, c % 2, :], qk_f[:, c, :], ACT.Square).then_inc(qk_sq, 1)
                    if c >= 1:
                        act.wait_ge(qk_ms, c)
                        nc.scalar.activation(qk_rs[:, c - 1, :], bank[3 + (c - 1) % 4], ACT.Ln,
                                             bias=eps_rms[:, 0:1]).then_inc(qk_ln, 1)
                act.wait_ge(gv_var, 1)
                nc.scalar.activation(gv_rs, gv_mv[:, :, 1], ACT.Ln, bias=eps_rms[:, 0:1]).then_inc(qk_ln, 1)
                act.wait_ge(qk_ln, 9)
                nc.scalar.activation(gv_rs, gv_rs, ACT.Exp, scale=-0.5).then_inc(gv_rstd, 1)
                nc.scalar.activation(qk_rs[:, :, :], qk_rs[:, :, :], ACT.Exp, scale=-0.5).then_inc(qk_rstd, 1)

            def dilated_attention():
                def expo(hd, h):
                    for n in range(TT):
                        act.wait_ge(mx_done, h * 4 + (n + 1))
                        row = prob[:, hd % 2, ROW_AT[n]:ROW_AT[n] + (n + 1) * P]
                        nc.scalar.activation(row, row, ACT.Exp, bias=neg_max[:, hd % 2, n:n + 1]).then_inc(pexp, 1)

                def normalise(hd, h):
                    act.wait_ge(den_done, h + 1)
                    for n in range(TT):
                        row = prob[:, hd % 2, ROW_AT[n]:ROW_AT[n] + (n + 1) * P]
                        nc.scalar.activation(row, row, ACT.Copy, scale=rden[:, hd % 2, n:n + 1]).then_inc(pn_done, 1)

                def copy_turned(h):
                    act.wait_ge(tr_p, h + 1)
                    act.wait_ge(pv_done, h + 1)
                    nc.scalar.copy(prob_t[:, :], psum[:, 4:7, :].rearrange("p b n -> p (b n)")[:, 0:STICK]).then_inc(pt_copied, 1)

                with act.Fori(0, 2) as i:
                    expo(0, i * 4)
                    for hd in range(4):
                        normalise(hd, i * 4 + hd)
                        if hd < 3:
                            expo(hd + 1, i * 4 + (hd + 1))
                        copy_turned(i * 4 + hd)

            def linear_attention():
                act.wait_ge(ga_done, 1)
                nc.scalar.copy(ga_t[:, :], bank[4]).then_inc(ga_copied, 1)
                for h in range(GLA_HEADS):
                    act.wait_ge(la_done, h + 1)
                    nc.scalar.activation(la[:, h, :], bank[h], ACT.Identity, bias=gate_bias[:, h:h + 1]).then_inc(la_lin, 1)
                act.wait_ge(la_lin, GLA_HEADS)
                nc.scalar.activation(ge[:, :, :], la[:, :, :], ACT.Abs).then_inc(la_link, 1)
                act.wait_ge(la_link, 1)
                nc.scalar.activation(ge[:, :, :], ge[:, :, :], ACT.Exp, scale=-1.0).then_inc(la_link, 1)
                act.wait_ge(la_link, 2)
                nc.scalar.activation(ge[:, :, :], ge[:, :, :], ACT.Ln, bias=one_col[:, 0:1]).then_inc(ln_a1, 1)
                act.wait_ge(cum_done, GLA_HEADS)
                nc.scalar.activation(ge[:, :, :], cum[:, :, :], ACT.Exp, scale=1.0 / GLA_TAU).then_inc(ek_done, 1)
                act.wait_ge(gq_done, 1)
                nc.scalar.activation(ge[:, :, :], cum[:, :, :], ACT.Exp, scale=-1.0 / GLA_TAU).then_inc(en_done, 1)
                act.wait_ge(last_done, 1)
                nc.scalar.activation(gks[:, :, :], gks[:, :, :], ACT.Exp, scale=1.0 / GLA_TAU).then_inc(es_done, 1)
                for n in range(TT):
                    act.wait_ge(tr_k, n + 1)
                    nc.scalar.copy(gks_t[:, n, :, :], bank[n].rearrange("p (h d) -> p h d", h=GLA_HEADS)).then_inc(kt_copied, 1)
                for m in range(DC):
                    act.wait_ge(go_done, m + 1)
                    if m == 0:
                        act.wait_ge(tr_k, TT)
                    nc.scalar.copy(go[:, m, :], bank[4 + m % 4]).then_inc(go_copied, 1)
                act.wait_ge(go_copied, DC)
                for m in range(DC):
                    if m >= 2:
                        act.wait_ge(go_ms, m - 1)
                    else:
                        act.wait_ge(go_done, DC)
                    nc.scalar.activation(sq_odd[:, m % 2, :], go[:, m, :], ACT.Square).then_inc(go_sq, 1)
                for h in range(GLA_HEADS):
                    act.wait_ge(go_ms, 2 * h + 2)
                    if h > 0:
                        act.wait_ge(go_hi, 2 * h)
                    nc.scalar.activation(o_rs[:, :], bank[h], ACT.Ln, bias=eps_rms[:, 0:1],
                                         scale=1.0 / GLA_DV).then_inc(go_link, 1)
                    act.wait_ge(go_link, 2 * h + 1)
                    nc.scalar.activation(o_rs[:, :], o_rs[:, :], ACT.Exp, scale=-0.5).then_inc(go_link, 1)

            act.wait_ge(y_done, 8)
            split(0, 0, None)
            split(0, 1, None)
            for name in run:
                if name == "glu":
                    gate_stage(name, ACT.Sigmoid)
                elif name == "ssm_out":
                    split_stage(name)
                    norm(0, True, (0, 16), True)
                elif name == "gu0":
                    gate_stage(name, ACT.Silu)
                elif name == "down0":
                    split_stage(name)
                    norm(1, True, (32, 48), True)
                elif name in ("q", "k"):
                    split_stage(name)
                elif name == "v":
                    split_stage(name)
                    stick_attention()
                elif name == "w_o":
                    split_stage(name)
                    norm(2, True, (8, 24), True)
                elif name == "gu1":
                    gate_stage(name, ACT.Silu)
                elif name == "down1":
                    split_stage(name)
                    norm(3, True, (40, 56), False)
                    norm(4, False, None, None)
                elif name == "ev_u":
                    feature_stage(name, ACT.Gelu, u_f)
                elif name == "ev_v":
                    token_stage(name, ACT.Gelu, gv_t)
                elif name in ("ev_qk", "od_q", "od_k", "od_v"):
                    split_stage(name)
                elif name == "ev_vb":
                    split_stage(name)
                    gated_mlp()
                    dilated_attention()
                elif name == "ev_out":
                    split_stage(name)
                    norm(5, False, None, None)
                elif name in ("conv0", "conv1"):
                    conv_stage(name)
                elif name in ("cdown0", "cdown1"):
                    split_stage(name)
                    if name == "cdown0":
                        norm(6, False, None, None)
                    else:
                        for n in range(2 * TT):
                            if n % 2 == 0:
                                continue
                            act.wait_ge(tr_out, n + 1)
                            nc.scalar.copy(out_t[:, n // 2, 512:1024], bank[n]).then_inc(go_link, 1)
                elif name == "od_r":
                    feature_stage(name, ACT.Silu, gr)
                    linear_attention()
                elif name == "od_out":
                    split_stage(name)
                    norm(7, False, None, None)

        @block.vector
        def _(dve):
            link = linker(dve, dve_link)
            V = nc.vector
            V.memset(ones_mean[:, :], 1.0 / D)
            V.memset(ones[:, :], 1.0)
            V.memset(eps_ln[:, :], LN_EPS)
            V.memset(eps_rms[:, :], RMS_EPS)
            for half in range(2):
                rows, other = slice(half * 64, half * 64 + 64), slice(64 - half * 64, 128 - half * 64)
                V.memset(head_mean[rows, rows], 1.0 / HD)
                V.memset(head_mean[rows, other], 0.0)
                V.memset(chunk_mask[rows, rows], 1.0)
                V.memset(chunk_mask[rows, other], 0.0)
            V.memset(one_col[:, :], 1.0).then_inc(mask_ones, 1)
            V.memset(marks[:, 0:1], 0.0).then_inc(evac_done, 4)
            for n, primed in enumerate((lw_done, o_ready, vt_copied, pt_copied, b_ready, lb_done, pv_done, o_done, tr_v, sc_done)):
                V.memset(marks[:, n + 1:n + 2], 0.0).then_inc(primed, 1)
            dve.wait_ge(ld_a, 48)
            V.tensor_copy(a_st[:, 2, :].rearrange("j (g p) -> j g p", g=2),
                          dt_st[:, :].unsqueeze(2).to_broadcast([PAIRS, 2, GP])).then_inc(a_rows, 1)
            dve.wait_ge(ld_x, 32)
            V.tensor_copy(x_perm[:, :, :, :], xnat[:, :, :].rearrange("p s (g h) -> p g s h", h=GH)).then_inc(x_permuted, 1)
            dve.wait_ge(tr_a, 1)
            link(V.tensor_copy(sp_[:, 0:3, :], bank[0][:, 0:3 * PAIRS].rearrange("p (n j) -> p n j", n=3)))

            def s(n):
                return sp_[:, n, :]

            def tt(o, a, b, op):
                link(V.tensor_tensor(o, a, b, op))

            def ts(o, a, c1, c2, op0, op1):
                link(V.tensor_scalar(o, a, c1, c2, op0, op1))

            def stt(o, a, c, b, op0, op1):
                link(V.scalar_tensor_tensor(o, a, c, b, op0, op1))

            def exp_(o, x):
                ts(s(12), x, -87.0, 88.0, ALU.max, ALU.min)
                ts(s(13), s(12), 1.4426950408889634, ROUND, ALU.mult, ALU.add)
                ts(s(13), s(13), -ROUND, 0.0, ALU.add, ALU.add)
                stt(s(14), s(13), -LN2[0], s(12), ALU.mult, ALU.add)
                stt(s(14), s(13), -LN2[1], s(14), ALU.mult, ALU.add)
                ts(s(15), s(14), EXP_TAYLOR[-1], 0.0, ALU.mult, ALU.add)
                for coef in EXP_TAYLOR[-2::-1]:
                    stt(s(15), s(15), coef, s(14), ALU.add, ALU.mult)
                ts(ki[:, :], s(13), 127.0, 2.0 ** 23, ALU.add, ALU.mult)
                stt(o, s(15), 1.0, ki[:, :].bitcast(F32), ALU.add, ALU.mult)

            exp_(s(3), s(2))
            ts(s(4), s(0), -1e-4, 0.0, ALU.min, ALU.add)
            tt(s(10), s(4), s(3), ALU.mult)
            exp_(s(5), s(10))
            tt(s(10), s(1), s(3), ALU.mult)
            ts(s(11), s(10), 0.15915494309189535, ROUND, ALU.mult, ALU.add)
            ts(s(11), s(11), -ROUND, 0.0, ALU.add, ALU.add)
            for part in TWO_PI:
                stt(s(10), s(11), -part, s(10), ALU.mult, ALU.add)
            ts(s(6), s(10), -3.1415925, 3.1415925, ALU.max, ALU.min)
            ts(s(7), s(6), -1.0, 0.0, ALU.mult, ALU.add)
            tt(s(7), s(7), s(6), ALU.max)
            V.tensor_scalar(s(7), s(7), -1.0, 1.5707963267948966, ALU.mult, ALU.add).then_inc(trig_in, 1)
            dve.wait_ge(tr_b, 2)
            for ri in range(2):
                V.tensor_copy(bt[:, ri, :, :], bank[1 + ri][:, :].rearrange("p (h j) -> p h j", h=GH)).then_inc(b_copied, 1)
            dve.wait_ge(trig_out, 2)
            link(V.memset(lam[:, 0, 0, :], 1.0))
            link(V.memset(lam[:, 1, 0, :], 0.0))
            tt(lam[:, 0, 1, :], s(5), s(9), ALU.mult)
            tt(lam[:, 1, 1, :], s(5), s(8), ALU.mult)

            def cmul(o, a, b, tmp):
                V.tensor_tensor(o[0], a[0], b[0], ALU.mult)
                tt(tmp[0], a[1], b[1], ALU.mult)
                V.tensor_tensor(o[1], a[0], b[1], ALU.mult)
                tt(tmp[1], a[1], b[0], ALU.mult)
                tt(o[0], o[0], tmp[0], ALU.subtract)
                tt(o[1], o[1], tmp[1], ALU.add)

            def powers(k0, n):
                return [lam[:, ri, k0:k0 + n, :] for ri in range(2)]

            def power(k, n):
                return [lam[:, ri, k:k + 1, :].to_broadcast([P, n, PAIRS]) for ri in range(2)]

            for n in (1, 2, 4):
                cmul(powers(n + 1, n), powers(1, n), power(n, n), [l_tmp[:, ri, 0:n, :] for ri in range(2)])
            for k in range(TAU):
                V.tensor_copy(lam_rev[:, :, k, :], lam[:, :, TAU - 1 - k, :])
            V.tensor_copy(ll[:, 0, :, :], lam[:, 0, TAU:TAU + 1, :].to_broadcast([P, 2, PAIRS]))
            V.tensor_copy(ll[:, 1, 0, :], lam[:, 1, TAU, :])
            V.tensor_scalar(ll[:, 1, 1, :], lam[:, 1, TAU, :], -1.0, 0.0, ALU.mult, ALU.add).then_inc(lam_ready, 1)
            tt(s(12), s(4), s(4), ALU.mult)
            tt(s(13), s(1), s(1), ALU.mult)
            tt(s(12), s(12), s(13), ALU.add)
            link(V.reciprocal(s(12), s(12)))
            ts(s(13), lam[:, 0, 1, :], -1.0, 0.0, ALU.add, ALU.add)
            tt(s(14), s(13), s(4), ALU.mult)
            tt(s(15), lam[:, 1, 1, :], s(1), ALU.mult)
            tt(s(14), s(14), s(15), ALU.add)
            tt(s(16), s(14), s(12), ALU.mult)
            tt(s(14), lam[:, 1, 1, :], s(4), ALU.mult)
            tt(s(15), s(13), s(1), ALU.mult)
            tt(s(14), s(14), s(15), ALU.subtract)
            tt(s(17), s(14), s(12), ALU.mult)
            cmul([bb[:, ri, 0:GH, :] for ri in range(2)], [bt[:, ri, :, :] for ri in range(2)],
                 [s(16 + ri).unsqueeze(1).to_broadcast([P, GH, PAIRS]) for ri in range(2)],
                 [l_tmp[:, ri, :, :] for ri in range(2)])
            link(V.tensor_copy(bb[:, :, GH:2 * GH, :], bb[:, :, 0:GH, :]))
            shape = [P, 4, TAU, GH]
            with dve.Fori(0, 4) as i:
                for buf in range(2):
                    n = i * 2 + buf
                    js = bass.ds(i * 8 + buf * 4, 4)
                    lv = [lam_rev[:, ri, :, js].rearrange("p k j -> p j k").unsqueeze(3).to_broadcast(shape)
                          for ri in range(2)]
                    bv = [bb[:, ri, 0:GH, js].rearrange("p h j -> p j h").unsqueeze(2).to_broadcast(shape) for ri in range(2)]
                    o = [v_buf[:, buf, ri, :, :].rearrange("p j (k h) -> p j k h", k=TAU) for ri in range(2)]
                    dve.wait_ge(tr_v, i * 4 + 1)
                    V.tensor_tensor(o[0], lv[0], bv[0], ALU.mult)
                    V.tensor_tensor(v_tmp[:, 0], lv[1], bv[1], ALU.mult)
                    V.tensor_tensor(o[1], lv[0], bv[1], ALU.mult)
                    V.tensor_tensor(v_tmp[:, 1], lv[1], bv[0], ALU.mult).then_inc(bb_ready, 1)
                    dve.wait_ge(bb_ready, n + 1)
                    V.tensor_tensor(o[0], o[0], v_tmp[:, 0], ALU.subtract)
                    V.tensor_tensor(o[1], o[1], v_tmp[:, 1], ALU.add).then_inc(v_ready, 1)
                    dve.wait_ge(v_ready, n + 1)
            dve.wait_ge(vt_copied, 17)
            for f in range(DC):
                dve.wait_ge(xhi_done, f + 1)
                V.tensor_tensor(xlo[:, f, :].rearrange("p (c s) -> p s c", s=TAU),
                                bank[f][:, :].rearrange("p (s c) -> p s c", s=TAU),
                                xhi[:, f, :].bitcast(F32).rearrange("p (c s) -> p s c", s=TAU),
                                ALU.subtract).then_inc(x_ready, 1)
            dve.wait_ge(s_copied, 8)
            V.memset(states[:, 0, :, :], 0.0).then_inc(scan_link, 1)
            dve.wait_ge(scan_link, 1)
            with dve.Fori(0, (NCH - 1) // 7) as i:
                for n in range(7):
                    here = states[:, bass.ds(i * 7 + n, 1), :, :]
                    then = states[:, bass.ds(i * 7 + (n + 1), 1), :, :]
                    V.tensor_tensor(s_tmp[:, :, :, :], ll[:, :, :, :], here.to_broadcast([P, 2, 2, PAIRS]), ALU.mult).then_inc(scan_link, 1)
                    dve.wait_ge(scan_link, i * 21 + (3 * n + 2))
                    V.tensor_tensor(then[:, 0], then[:, 0], s_tmp[:, 0, :, :], ALU.add).then_inc(scan_link, 1)
                    dve.wait_ge(scan_link, i * 21 + (3 * n + 3))
                    V.tensor_tensor(then[:, 0, 0], then[:, 0, 0], s_tmp[:, 1, 1, :], ALU.add)
                    V.tensor_tensor(then[:, 0, 1], then[:, 0, 1], s_tmp[:, 1, 0, :], ALU.add).then_inc(scan_link, 1)
                    dve.wait_ge(scan_link, i * 21 + (3 * n + 4))
            V.memset(s_tmp[:, 0, 0, 0:1], 0.0).then_inc(scan_done, 1)
            dve.wait_ge(xd_ready, 1)
            for b in range(8):
                dve.wait_ge(y_done, b + 1)
                y = xnat[:, :, (b // 2) * P:(b // 2 + 1) * P].rearrange("p s (g h) -> p g s h", g=8)[:, b % 2::2, :, :]
                V.tensor_tensor(y, bank[b][:, :].rearrange("p (g s h) -> p g s h", g=4, s=TAU), y, ALU.add).then_inc(y_copied, 1)
            for f in range(DC):
                dve.wait_ge(gelu_done, f + 1)
                V.tensor_copy(hhi[:, f, :], tmp_a[:, f % 2, :]).then_inc(zhi_done, 1)
                dve.wait_ge(zhi_done, f + 1)
                V.tensor_tensor(hlo[:, f, :], tmp_a[:, f % 2, :], hhi[:, f, :].bitcast(F32), ALU.subtract).then_inc(hid_ready, 1)

            def split(it, half):
                dve.wait_ge(whi_done, it * 2 + half + 1)
                V.tensor_tensor(wlo[:, half, :], wst[:, half, :], whi[:, half, :].bitcast(F32),
                                ALU.subtract).then_inc(wlo_done, 1)

            def stage_loop(name, body):
                st = ST[name]
                last = name == run[-1]
                def split_next(i):
                    return lambda half: split(i + (st.it0 + 1), half)
                if st.iters > last:
                    with dve.Fori(0, st.iters - last) as i:
                        body(i, split_next(i))
                if last:
                    body(st.iters - 1, lambda half: None)

            def put_hidden(src, m, count):
                V.tensor_copy(hhi[:, bass.ds(m, 1), :], src).then_inc(zhi_done, 1)
                dve.wait_ge(zhi_done, count)
                V.tensor_tensor(hlo[:, bass.ds(m, 1), :], src, hhi[:, bass.ds(m, 1), :].bitcast(F32),
                                ALU.subtract).then_inc(hid_ready, 1)

            def gate_stage(name, m0):
                st = ST[name]
                def body(i, split_next):
                    split_next(0)
                    for u in range(2):
                        dve.wait_ge(part_done, i * 4 + (st.part0 + u + 3))
                        dve.wait_ge(act_out, i * 2 + (st.pair0 - DC + u + 1))
                        V.tensor_tensor(tmp_b[:, u, :], bank[2 + u][:, :], tmp_a[:, u, :], ALU.mult).then_inc(evac_done, 1)
                        dve.wait_ge(evac_done, i * 2 + (st.evac0 + u + 1))
                        put_hidden(tmp_b[:, u:u + 1, :], i * 2 + (m0 + u), i * 2 + (st.pair0 + u + 1))
                    split_next(1)
                stage_loop(name, body)

            def residual(bank_, m, evac, count, plain=False):
                if plain:
                    V.tensor_tensor(res[:, bass.ds(m, 1), :], res[:, bass.ds(m, 1), :], bank_.unsqueeze(1),
                                    ALU.add).then_inc(evac_done, 1)
                    dve.wait_ge(evac_done, evac)
                    V.memset(stat[:, 127:128], 0.0).then_inc(res_ready, 1)
                    return
                residual_scaled(bank_, m, evac, count)

            def residual_scaled(bank_, m, evac, count):
                V.scalar_tensor_tensor(tmp_b[:, 0:1, :], xlo[:, bass.ds(m, 1), :].bitcast(F32), ALPHA,
                                       bank_[:, :].unsqueeze(1), ALU.mult, ALU.add).then_inc(evac_done, 1)
                dve.wait_ge(evac_done, evac)
                V.scalar_tensor_tensor(res[:, bass.ds(m, 1), :], xhi[:, bass.ds(m, 1), :].bitcast(F32), ALPHA,
                                       tmp_b[:, 0:1, :], ALU.mult, ALU.add).then_inc(res_ready, 1)
                dve.wait_ge(res_ready, count)

            def out_stage(name):
                st = ST[name]
                def body(i, split_next):
                    for half in range(2):
                        for u in range(2):
                            n = 2 * half + u
                            dve.wait_ge(part_done, i * 4 + (st.part0 + n + 1))
                            residual(bank[n], i * 4 + n, i * 4 + (st.evac0 + n + 1), i * 4 + (st.res0 + n + 1), name[0] in "eo")
                        split_next(half)
                stage_loop(name, body)

            def down_stage(name):
                st = ST[name]
                last = name == run[-1]
                def body(i, u, ahead):
                    if ahead:
                        split(i + (st.it0 + u + 1), 0)
                    dve.wait_ge(part_done, i * 2 + (st.part0 + 2 * u + 2))
                    residual(bank[u], i + u, i + (st.evac0 + u + 1), i + (st.res0 + u + 1), name[0] == "c")
                    if ahead:
                        split(i + (st.it0 + u + 1), 1)
                n = st.iters // 2 - last
                with dve.Fori(0, n) as i:
                    for u in range(2):
                        body(i * 2, u, True)
                if last:
                    body(2 * n, 0, True)
                    body(2 * n, 1, False)

            def norm(n, mean, split_out, x0):
                if mean:
                    dve.wait_ge(ln_mean, n + 1)
                    for c in range(DC):
                        V.tensor_tensor(res[:, c, :], res[:, c, :], bank[4][:, :], ALU.subtract).then_inc(ln_xc, 1)
                dve.wait_ge(act_link, 2 * n + 2)
                for c in range(DC + 2):
                    if c < DC:
                        V.tensor_tensor(res[:, c, :], res[:, c, :], rstd, ALU.mult).then_inc(ln_n, 1)
                    if split_out and c >= 2:
                        m = c - 2
                        dve.wait_ge(ln_a, n * DC + m + 1)
                        V.tensor_copy(xhi[:, m, :], res[:, m, :]).then_inc(ln_hi, 1)
                        dve.wait_ge(ln_hi, n * DC + m + 1)
                        V.tensor_tensor(xlo[:, m, :], res[:, m, :], xhi[:, m, :].bitcast(F32), ALU.subtract).then_inc(x_ready, 1)

            def copy_stage(name, dst, scale):
                st = ST[name]
                def body(i, split_next):
                    for half in range(2):
                        for u in range(2):
                            n = 2 * half + u
                            dve.wait_ge(part_done, i * 4 + (st.part0 + n + 1))
                            V.tensor_scalar(dst[:, bass.ds(i * 4 + n, 1), :], bank[n].unsqueeze(1), scale, 0.0,
                                            ALU.mult, ALU.add).then_inc(evac_done, 1)
                        split_next(half)
                stage_loop(name, body)

            def token_stage(name, dst):
                st = ST[name]
                def body(i, split_next):
                    for half in range(2):
                        for n in range(TT):
                            dve.wait_ge(part_done, i * 8 + (st.part0 + 4 * half + n + 1))
                            V.tensor_copy(dst[:, n, bass.ds(i * 512 + half * 256, 256)],
                                          bank[4 * half + n][:, 0:256]).then_inc(evac_done, 1)
                        split_next(half)
                stage_loop(name, body)

            def stick_attention():
                z = psum[:, 0:3, :].rearrange("p b n -> p (b n)")[:, 0:STICK]
                cs = psum[:, 4:7, :].rearrange("p b n -> p (b n)")[:, 0:STICK]

                def soft(hd, h, first):
                    dve.wait_ge(ln_part, h + 1)
                    if not first:
                        dve.wait_ge(o_done, h)
                    V.scalar_tensor_tensor(drop[:, hd % 2, :], z, 0.0, lnp[:, :], ALU.max, ALU.add).then_inc(sp_done, 1)
                    V.scalar_tensor_tensor(keep[:, hd % 2, :], z, 0.0, lnp[:, :], ALU.min, ALU.subtract).then_inc(lb_done, 1)

                def log_weights(hd, h):
                    dve.wait_ge(cs_done, h + 1)
                    dve.wait_ge(lb_done, h + 2)
                    V.tensor_tensor(keep[:, hd % 2, :], keep[:, hd % 2, :], cs, ALU.subtract).then_inc(lw_done, 1)

                def put_pair(p):
                    dve.wait_ge(o_done, p * 2 + 3)
                    V.tensor_copy(hhi[:, bass.ds(p, 1), :], bank[7].unsqueeze(1)).then_inc(o_hi, 1)
                    dve.wait_ge(o_hi, p + 1)
                    V.tensor_tensor(hlo[:, bass.ds(p, 1), :], bank[7].unsqueeze(1), hhi[:, bass.ds(p, 1), :].bitcast(F32),
                                    ALU.subtract).then_inc(o_ready, 1)

                def heads4(i, last, first=False):
                    for hd in range(4):
                        if not (last and hd == 3):
                            soft((hd + 1) % 4, i * 4 + (hd + 1), False)
                        log_weights(hd, i * 4 + hd)
                        if hd % 2 == 1:
                            put_pair(i * 2 + hd // 2)

                soft(0, 0, True)
                with dve.Fori(0, HEADS // 4 - 1) as i:
                    heads4(i, False)
                heads4(HEADS // 4 - 1, True)

            def rms(n, gcol):
                dve.wait_ge(act_link, 2 * n + 2)
                first = (n - 4) * DC
                for c in range(DC + 1):
                    if 2 <= c < DC:
                        dve.wait_ge(x_ready, n * DC + c - 1)
                    if c < DC:
                        V.scalar_tensor_tensor(tmp_c[:, c % 2, :], res[:, c, :], prm[:, gcol + c:gcol + c + 1], rstd,
                                               ALU.mult, ALU.mult).then_inc(rms_t, 1)
                    if c >= 1:
                        m = c - 1
                        dve.wait_ge(rms_t, first + m + 1)
                        V.tensor_copy(xhi[:, m, :], tmp_c[:, m % 2, :]).then_inc(ln_hi, 1)
                        dve.wait_ge(ln_hi, 3 * DC + first + m + 1)
                        V.tensor_tensor(xlo[:, m, :], tmp_c[:, m % 2, :], xhi[:, m, :].bitcast(F32), ALU.subtract).then_inc(x_ready, 1)

            def split_stage(name):
                def body(i, split_next):
                    split_next(0)
                    split_next(1)
                stage_loop(name, body)

            def conv_stage(name):
                st = ST[name]
                layer = int(name[-1])
                n0 = (st.evac1 - st.evac0) * layer
                def body(i, split_next):
                    split_next(0)
                    for u in range(2):
                        dve.wait_ge(conv_a, i * 2 + (n0 + u + 1))
                        V.scalar_tensor_tensor(tmp_a[:, u, 1:SEQ], bank[u][:, 0:SEQ - 1], tap(layer, 1, i * 2 + u),
                                               tmp_a[:, u, 1:SEQ], ALU.mult, ALU.add).then_inc(ttr_link, 1)
                        dve.wait_ge(ttr_link, i * 2 + (4 * HEADS_B + n0 + u + 1))
                        V.scalar_tensor_tensor(tmp_a[:, u, 2:SEQ], bank[u][:, 0:SEQ - 2], tap(layer, 0, i * 2 + u),
                                               tmp_a[:, u, 2:SEQ], ALU.mult, ALU.add).then_inc(conv_b, 1)
                    for u in range(2):
                        dve.wait_ge(part_done, i * 4 + (st.part0 + u + 3))
                        dve.wait_ge(act_out, i * 2 + (st.pair0 - DC + u + 1))
                        V.tensor_tensor(tmp_b[:, u, :], bank[2 + u], tmp_a[:, u, :], ALU.mult).then_inc(evac_done, 1)
                        dve.wait_ge(evac_done, i * 2 + (st.evac0 + u + 1))
                        put_hidden(tmp_b[:, u:u + 1, :], i * 2 + u, i * 2 + (st.pair0 + u + 1))
                    split_next(1)
                stage_loop(name, body)

            def put_x(src, m, hi_sem, ready, count):
                V.tensor_copy(xhi[:, bass.ds(m, 1), :], src).then_inc(hi_sem, 1)
                dve.wait_ge(hi_sem, count)
                V.tensor_tensor(xlo[:, bass.ds(m, 1), :], src, xhi[:, bass.ds(m, 1), :].bitcast(F32),
                                ALU.subtract).then_inc(ready, 1)

            def gated_mlp():
                link = linker(dve, ev_link)
                dve.wait_ge(tab_done, 1)
                dve.wait_ge(consts, 4)
                for n in range(3):
                    link(V.tensor_copy(mult_t[:, n, :], bank[0][:, 0:P]))
                link(V.tensor_scalar(mult_t[:, 3, :], bank[0][:, 0:P], 1.0, 0.0, ALU.add, ALU.add))
                link(V.tensor_tensor(mult_t[:, 2, :], mult_t[:, 2, :], after[:, :], ALU.add))
                link(V.tensor_tensor(mult_t[:, 2, :], mult_t[:, 2, :], ident[:, :], ALU.add))
                link(V.tensor_tensor(bias_t[:, 0, :], before[:, :], ident[:, :], ALU.add))
                link(V.tensor_tensor(mult_t[:, 3, :], mult_t[:, 3, :], bias_t[:, 0, :], ALU.mult))
                link(V.tensor_scalar(bias_t[:, :, :], mult_t[:, :, :], 1.0, -1.0, ALU.min, ALU.add))
                link(V.tensor_scalar(bias_t[:, :, :], bias_t[:, :, :], -NEG, 0.0, ALU.mult, ALU.add))
                V.memset(stat[:, 126:127], 0.0).then_inc(sm_done, 4)
                dve.wait_ge(evac_done, ST["ev_vb"].evac1)
                for n in range(TT):
                    link(V.bn_stats(gv_stats[:, n, :], gv_t[:, n, :]))
                    link(V.bn_aggr(gv_mv[:, n, :], gv_stats[:, n, :]))
                V.memset(stat[:, 125:126], 0.0).then_inc(gv_var, 1)
                dve.wait_ge(gv_rstd, 1)
                dve.wait_ge(ld_even, 4 * 16)
                for n in range(TT):
                    link(V.tensor_scalar(gv_t[:, n, :], gv_t[:, n, :], gv_mv[:, n, 0:1], gv_rs[:, n:n + 1],
                                         ALU.subtract, ALU.mult))
                    link(V.tensor_tensor(gv_t[:, n, :], gv_t[:, n, :], gv_gb[:, 0, :], ALU.mult))
                    V.tensor_tensor(gv_t[:, n, :], gv_t[:, n, :], gv_gb[:, 1, :], ALU.add).then_inc(vn_ready, 1)
                V.memset(stat[:, 124:125], 0.0).then_inc(tables, 1)
                for c in range(4):
                    dve.wait_ge(gm_done, c + 1)
                    V.tensor_tensor(u_f[:, c, :], u_f[:, c, :], bank[1 + c % 2], ALU.mult).then_inc(gm_copied, 1)
                    dve.wait_ge(gm_copied, c + 1)
                    put_x(u_f[:, c:c + 1, :], c, gm_hi, gm_ready, c + 1)

            def dilated_attention():
                dve.wait_ge(qk_rstd, 1)

                def rows(hd, h):
                    for n in range(TT):
                        dve.wait_ge(sc_done, h * 4 + (n + 2))
                        row = prob[:, hd % 2, ROW_AT[n]:ROW_AT[n] + (n + 1) * P]
                        V.scalar_tensor_tensor(row.rearrange("p (j k) -> p j k", k=P),
                                               bank[n][:, 0:(n + 1) * P].rearrange("p (j k) -> p j k", k=P), HD ** -0.5,
                                               bias_t[:, 3 - n:4, :], ALU.mult, ALU.add).then_inc(sm_done, 1)
                        dve.wait_ge(sm_done, h * 4 + (n + 5))
                        V.tensor_reduce(neg_max[:, hd % 2, n:n + 1], row, AX.X, ALU.max, negate=True).then_inc(mx_done, 1)

                def sums(hd, h):
                    for n in range(TT):
                        dve.wait_ge(pexp, h * 4 + (n + 1))
                        row = prob[:, hd % 2, ROW_AT[n]:ROW_AT[n] + (n + 1) * P]
                        V.tensor_tensor_reduce(row, row, mult_t[:, 3 - n:4, :].rearrange("p j k -> p (j k)"), 1.0, 0.0,
                                               ALU.mult, ALU.add, den[:, hd % 2, n:n + 1]).then_inc(ttr_link, 1)
                    dve.wait_ge(ttr_link, h * 4 + 4)
                    V.reciprocal(rden[:, hd % 2, :], den[:, hd % 2, :]).then_inc(den_done, 1)

                def put_pair(p):
                    dve.wait_ge(pv_done, p * 2 + 3)
                    put_x(bank[7].unsqueeze(1), p + 4, b_hi, b_ready, p + 1)

                with dve.Fori(0, 2) as i:
                    dve.wait_ge(sc_done, i * 16 + 1)
                    for pp in range(2):
                        for dst, c0, g in ((qn_pair, 0, q_gain), (kn_pair, 4, k_gain)):
                            c = bass.ds(i * 2 + (c0 + pp), 1)
                            ins = V.scalar_tensor_tensor(dst[:, pp:pp + 1, :], qk_f[:, c, :], g, qk_rs[:, c, :], ALU.mult, ALU.mult)
                        ins.then_inc(qn_ready, 1)
                    rows(0, i * 4)
                    for hd in range(4):
                        sums(hd, i * 4 + hd)
                        if hd < 3:
                            rows(hd + 1, i * 4 + (hd + 1))
                        if hd % 2 == 1:
                            put_pair(i * 2 + hd // 2)

            def linear_attention():
                V.memset(keep_sum[:, :], 1.0).then_inc(st_link, 1)
                dve.wait_ge(st_link, 1)
                V.memset(keep_sum[:, ::GLA_CHUNK], 0.0).then_inc(st_link, 1)
                dve.wait_ge(ld_odd, 32)
                V.tensor_copy(wga_hi[:, :, :], wga[:, :, :]).then_inc(wga_hi_s, 1)
                dve.wait_ge(wga_hi_s, 1)
                V.tensor_tensor(wga_lo[:, :, :], wga[:, :, :], wga_hi[:, :, :].bitcast(F32), ALU.subtract).then_inc(wga_ready, 1)
                dve.wait_ge(ln_a1, 1)
                flat = "p h s -> p (h s)"
                V.scalar_tensor_tensor(la[:, :, :].rearrange(flat), la[:, :, :].rearrange(flat), 0.0, ge[:, :, :].rearrange(flat),
                                       ALU.min, ALU.subtract).then_inc(st_link, 1)
                dve.wait_ge(st_link, 3)
                for h in range(GLA_HEADS):
                    V.tensor_tensor_scan(cum[:, h, :], keep_sum[:, :], la[:, h, :], 0.0, ALU.mult, ALU.add).then_inc(cum_done, 1)
                dve.wait_ge(cum_done, GLA_HEADS)
                c4 = cum[:, :, :].rearrange("p h (n s) -> p (h n) s", s=GLA_CHUNK)
                V.tensor_tensor(gks[:, :, :].rearrange("p h (n s) -> p (h n) s", s=GLA_CHUNK),
                                c4[:, :, GLA_CHUNK - 1:GLA_CHUNK].to_broadcast([P, GLA_HEADS * GLA_CHUNKS, GLA_CHUNK]), c4,
                                ALU.subtract).then_inc(last_done, 1)
                dve.wait_ge(ek_done, 1)
                V.tensor_copy(decay, ge[:, :, GLA_CHUNK - 1::GLA_CHUNK]).then_inc(st_link, 1)
                V.tensor_tensor(gq[:, :, :], gq[:, :, :], ge[:, :, :], ALU.mult).then_inc(gq_done, 1)
                dve.wait_ge(en_done, 1)
                V.tensor_tensor(gkt[:, :, :], gk[:, :, :], ge[:, :, :], ALU.mult).then_inc(gkt_done, 1)
                dve.wait_ge(es_done, 1)
                V.tensor_tensor(gks[:, :, :], gk[:, :, :], gks[:, :, :], ALU.mult).then_inc(gks_done, 1)
                for h in range(GLA_HEADS):
                    dve.wait_ge(at_done, h + 1)
                    V.tensor_tensor(attn_t[:, h, :, :], bank[4 + h].rearrange("p (n s) -> p n s", n=TT),
                                    chunk_mask[:, :].unsqueeze(1).to_broadcast([P, TT, P]), ALU.mult).then_inc(at_ready, 1)
                for h in range(GLA_HEADS):
                    if h >= 2:
                        dve.wait_ge(go_done, 2 * h - 2)
                    else:
                        dve.wait_ge(ga_done, 1)
                    V.memset(gst[:, h % 2, 0, :], 0.0).then_inc(st_ready, 1)
                    dve.wait_ge(kv_done, h + 1)
                    for n in range(GLA_CHUNKS - 1):
                        hf, m, a = n % 2, n // 4, (n // 2) % 2
                        dve.wait_ge(st_ready, h * GLA_CHUNKS + n + 1)
                        V.scalar_tensor_tensor(gst[:, h % 2, n + 1, :], gst[:, h % 2, n, :], decay[:, h, n:n + 1],
                                               bank[2 * hf + m][:, a * GLA_DV:(a + 1) * GLA_DV], ALU.mult,
                                               ALU.add).then_inc(st_ready, 1)
                for m in range(DC):
                    h = m // 2
                    dve.wait_ge(go_link, 2 * h + 2)
                    V.scalar_tensor_tensor(o_tmp[:, m % 2, :], go[:, m, :], head_gain[:, m % 2:m % 2 + 1], o_rs[:, :],
                                           ALU.mult, ALU.mult).then_inc(go_hi, 1)
                    dve.wait_ge(go_hi, m + 1)
                    V.tensor_tensor(o_tmp[:, m % 2, :], o_tmp[:, m % 2, :], gr[:, m, :], ALU.mult).then_inc(st_link, 1)
                    dve.wait_ge(st_link, m + 5)
                    put_x(o_tmp[:, m % 2:m % 2 + 1, :], m, b_hi, go_ready, 4 + m + 1)

            split(0, 0)
            split(0, 1)
            for name in run:
                if name == "glu":
                    gate_stage(name, DC)
                elif name == "ssm_out":
                    out_stage(name)
                    norm(0, True, True, DC)
                elif name == "gu0":
                    gate_stage(name, 0)
                elif name == "down0":
                    down_stage(name)
                    norm(1, True, True, 2 * DC)
                elif name == "q":
                    copy_stage(name, q_f, HD ** -0.5)
                elif name == "k":
                    copy_stage(name, k_f, 1.0)
                elif name == "v":
                    token_stage(name, v_t)
                    stick_attention()
                elif name == "w_o":
                    out_stage(name)
                    norm(2, True, True, 3 * DC)
                elif name == "gu1":
                    gate_stage(name, 0)
                elif name == "down1":
                    down_stage(name)
                    norm(3, True, False, None)
                    rms(4, 64)
                elif name in ("ev_u", "ev_v"):
                    split_stage(name)
                elif name == "ev_qk":
                    copy_stage(name, qk_f, 1.0)
                elif name == "ev_vb":
                    token_stage(name, vb_t)
                    gated_mlp()
                    dilated_attention()
                elif name == "ev_out":
                    out_stage(name)
                    rms(5, 80)
                elif name in ("conv0", "conv1"):
                    conv_stage(name)
                elif name == "cdown0":
                    down_stage(name)
                    rms(6, 72)
                elif name == "cdown1":
                    down_stage(name)
                    for n in range(TT):
                        dve.wait_ge(tr_out, 2 * n + 1)
                        V.tensor_copy(out_t[:, n, 0:512], bank[2 * n]).then_inc(go_hi, 1)
                        dve.wait_ge(go_hi, DC + n + 1)
                        dve.wait_ge(go_link, DC + n + 1)
                        V.memset(stat[:, 0:1], 0.0).then_inc(out_rows, 1)
                elif name == "od_q":
                    copy_stage(name, gq, 128 ** -0.5)
                elif name == "od_k":
                    copy_stage(name, gk, 1.0)
                elif name == "od_v":
                    token_stage(name, gvt)
                elif name == "od_r":
                    split_stage(name)
                    linear_attention()
                elif name == "od_out":
                    out_stage(name)
                    rms(7, 88)


_INS = [
    "x", "ssm_a_re", "ssm_a_im", "ssm_log_dt", "ssm_b_re", "ssm_b_im", "ssm_c_re", "ssm_c_im", "ssm_d", "ssm_w_glu",
    "ssm_w_out", "sb_w_qkv", "sb_w_o", "ffn_w_gu", "ffn_w_down", "ln_mix_g", "ln_mix_b", "ln_ffn_g", "ln_ffn_b",
    "norm_mix_g_2", "norm_ffn_g_2", "ev_w_in_2", "ev_a_ln_g_2", "ev_a_ln_b_2", "ev_a_ws_2", "ev_a_bs_2",
    "ev_q_g_2", "ev_k_g_2", "ev_w_out_2", "od_w_in_2", "od_w_a2_2", "od_b_a_2", "od_head_g_2", "od_w_out_2",
    "ffn_w_gate_2", "ffn_w_up_2", "ffn_conv_w_2", "ffn_conv_b_2", "ffn_w_down_2",
]


def kernel(**inputs):
    import numpy as _np
    import concourse.bacc as _bacc
    from concourse import mybir as _mybir
    from concourse.bass_utils import run_bass_kernel_spmd as _run

    nc = _bacc.Bacc("TRN2", target_bir_lowering=False, num_devices=1)
    arrays, views = {}, {}
    for name in _INS:
        a = _np.ascontiguousarray(inputs[name])
        arrays[f"in_{name}_dram"] = a
        views[name] = nc.dram_tensor(f"in_{name}_dram", a.shape, _mybir.dt.from_np(a.dtype), kind="ExternalInput").ap()
    out = nc.dram_tensor("out_0_dram", (1, SEQ, D), _mybir.dt.float32, kind="ExternalOutput").ap()
    build_blocks(nc, views, out)
    r = _run(nc, [arrays], core_ids=[0])
    return r.results[0]["out_0_dram"]
```

```python
import math
from contextlib import ExitStack

import concourse.bass as bass
from concourse import mybir

ALU = mybir.AluOpType
ACT = mybir.ActivationFunctionType
AX = mybir.AxisListType
F32 = mybir.dt.float32
F32R = mybir.dt.float32r
I32 = mybir.dt.int32

P = 128
SEQ = 512
D = 1024
DC = D // P
TT = SEQ // P
FFN = 2816
FC = FFN // P
DEPTH = 2
ALPHA = (2 * DEPTH) ** 0.25
LN_EPS = 1e-5
RMS_EPS = 1e-6

GROUPS, GH, GP = 64, 16, 64
PAIRS = GROUPS // 2
TAU = 8
NCH = SEQ // TAU
LAGS = TAU + 1
SEGS = 8

HEADS, HD = 16, 64
STICK = 1280
REST = {0: 512, 2: 896, 1: 1024}

PT_AT = {0: 0, 1: 512, 3: 896, 2: 1024}
ROW_AT = [P * i * (i + 1) // 2 for i in range(TT)]
NEG = -1e30
HEADS_B = 8
GLA_HEADS, GLA_CHUNK, GLA_DV, GATE_RANK = 4, 64, 256, 16
GLA_CHUNKS = SEQ // GLA_CHUNK
GLA_TAU = 16.0
TAPS = 3

KB = 1024
TILE = 2048
DOWN_K = FC // 2

ROUND = 1.5 * 2.0 ** 23
TWO_PI = (6.28125, 0.00193500518798828125, 3.0199158988e-07)
LN2 = (0.693359375, -2.12194440e-4)
EXP_TAYLOR = (1.0, 1 / 2, 1 / 6, 1 / 24, 1 / 120, 1 / 720, 1 / 5040)


class Stage:

    def __init__(self, name, iters, parts, evacs):
        self.name, self.iters, self.parts, self.evacs = name, iters, parts, evacs


def plan_stages():
    rows = [
        ("glu", 4, 4, 2), ("ssm_out", 2, 4, 4), ("gu0", 11, 4, 2), ("down0", 8, 2, 1),
        ("q", 2, 4, 4), ("k", 2, 4, 4), ("v", 2, 8, 8), ("w_o", 2, 4, 4), ("gu1", 11, 4, 2), ("down1", 8, 2, 1),
        ("ev_u", 1, 4, 4), ("ev_v", 1, 8, 8), ("ev_qk", 2, 4, 4), ("ev_vb", 1, 8, 8),
        ("ev_out", 2, 4, 4), ("conv0", 11, 4, 2), ("cdown0", 8, 2, 1),
        ("od_q", 1, 4, 4), ("od_k", 1, 4, 4), ("od_v", 2, 8, 8), ("od_r", 2, 4, 4), ("od_out", 2, 4, 4),
        ("conv1", 11, 4, 2), ("cdown1", 8, 2, 1),
    ]
    stages, it, part, evac, pair = {}, 0, 0, 4, DC
    for row in rows:
        s = Stage(*row)
        s.it0, s.part0, s.evac0, s.pair0 = it, part, evac, pair
        it += s.iters
        part += s.iters * s.parts
        evac += s.iters * s.evacs
        pair += s.iters * s.evacs * (s.evacs == 2)
        s.part1, s.evac1, s.pair1 = part, evac, pair
        stages[s.name] = s
    return stages


def build_blocks(nc, t, out):
    ST = plan_stages()
    run = list(ST)

    with ExitStack() as ctx:
        top = [nc.sbuf_base]
        arena_size = (nc.sbuf_usable_end - nc.sbuf_base) // 64 * 64 - 64
        ctx.enter_context(nc.sbuf_tensor("arena", [P, arena_size // 4], F32))
        arena0 = (top[0] + 31) // 32 * 32
        top[0] = arena0

        def at(name, shape, offset, dtype=F32):
            return nc.alloc_sbuf_tensor_at(name, shape, dtype, offset=offset)

        def new(name, shape, dtype=F32):
            words = 1
            for n in shape[1:]:
                words *= n
            here = top[0]
            top[0] = here + (words * 4 + 31) // 32 * 32
            assert top[0] <= arena0 + arena_size, (name, top[0])
            return at(name, shape, here, dtype), here

        def sem(name):
            return ctx.enter_context(nc.semaphore(name))

        psum = ctx.enter_context(nc.psum_tensor("psum", [P, 8, 512], F32))
        bank = [psum[:, i, :] for i in range(8)]

        wst, wst_at = new("w_stage", [P, 2, TILE])
        whi, whi_at = new("w_hi", [P, 2, TILE], F32R)
        wlo, _ = new("w_lo", [P, 2, TILE], F32R)
        xhi, xhi_at = new("x_hi", [P, DC, SEQ], F32R)
        xlo, _ = new("x_lo", [P, DC, SEQ], F32R)
        res, res_at = new("residual", [P, DC, SEQ])
        hhi, hid_at = new("hidden_hi", [P, FC, SEQ], F32R)
        hlo, _ = new("hidden_lo", [P, FC, SEQ], F32R)
        tmp_a, tmp_at = new("tmp_a", [P, 2, SEQ])
        tmp_b, _ = new("tmp_b", [P, 2, SEQ])
        tmp_c, _ = new("tmp_c", [P, 2, SEQ])
        sq, _ = new("squares", [P, 2, SEQ])
        ident, _ = new("ident", [P, P])
        ones_mean, _ = new("ones_mean", [P, P])
        ones, _ = new("ones", [P, P])
        eps_ln, _ = new("eps_ln", [P, 1])
        eps_rms, _ = new("eps_rms", [P, 1])
        one_col, _ = new("one_col", [P, 1])
        pool_pad, _ = new("pool_pad", [P, 1])
        marks, _ = new("marks", [P, 16])
        NROW = 12 * DC
        CROW = (TAPS + 1) * FC
        SROW = 8
        prm, _ = new("params", [P, NROW + 2 * CROW + SROW])

        def tap(layer, k, m):
            return prm[:, bass.ds(m + (NROW + layer * CROW + k * FC), 1)]

        small0 = NROW + 2 * CROW
        gate_bias = prm[:, small0:small0 + GLA_HEADS]
        head_gain = prm[:, small0 + 4:small0 + 6]
        q_gain, k_gain = prm[:, small0 + 6:small0 + 7], prm[:, small0 + 7:small0 + 8]
        rstd = sq[:, 0, :]
        acc, acc_sq = tmp_a[:, 0, :], tmp_a[:, 1, :]
        dev_slot = [acc_sq, tmp_b[:, 0, :], tmp_b[:, 1, :], tmp_c[:, 0, :], tmp_c[:, 1, :], sq[:, 0, :], sq[:, 1, :], tmp_b[:, 0, :]]
        mean, mean_sq, variance, rstd_ln = acc, tmp_c[:, 0, :], tmp_c[:, 1, :], tmp_b[:, 1, :]
        d_bc, _ = new("d_rows", [P, 512])
        prm_st = at("param_rows", [NROW, P], wst_at + 12 * KB)
        conv_st = at("conv_rows", [CROW, 2, P], wst_at + 12 * KB + 512)
        small_st = at("small_rows", [SROW, P], wst_at + 12 * KB + 1536)

        xnat = at("x_natural", [P, TAU, 512], hid_at + 72 * KB)
        w_re = at("cl_re", [P, PAIRS, LAGS, GH], hid_at)
        w_im = at("cl_im_neg", [P, PAIRS, LAGS, GH], hid_at + 18 * KB)
        toe = at("toeplitz", [P, GROUPS, P], hid_at + 36 * KB)
        v_tmp = at("v_tmp", [P, 2, 4, TAU, GH], hid_at + 68 * KB)
        uu = at("u_chunks", [P, GROUPS, NCH], res_at)
        vt = [at("bl_rows0", [P, 2, 4, P], wst_at), at("bl_rows1", [P, 2, 4, P], tmp_at + 8 * KB)]
        v_buf = at("bl_piece", [P, 2, 2, 4, TAU * GH], tmp_at)
        k_rows = at("k_rows", [P, 16, P], tmp_at + 8 * KB)
        w_tmp = at("w_tmp", [P, 4, LAGS, GH], tmp_at + 13 * KB + 512)
        b_st = at("b_stage", [PAIRS, 2, 2 * GP * GH], whi_at)
        c_st = at("c_stage", [P, 2, 8, 2, GP], whi_at + 16 * KB)
        states = at("states", [P, NCH + 1, 2, PAIRS], whi_at)
        seg_pow = at("segment_powers", [P, 2, SEGS, 2, PAIRS], hid_at + 68 * KB)
        s_tmp = at("state_tmp", [P, SEGS * (SEGS - 1) // 2 * 2 * PAIRS], tmp_at)
        a_st = at("a_stage", [PAIRS, 3, 2 * GP], whi_at + 24 * KB)
        dt_st = at("dt_stage", [PAIRS, 2], whi_at + 26 * KB - 512)
        sp_ = at("ssm_scalars", [P, 24, PAIRS], whi_at + 26 * KB)
        lam = at("lam_powers", [P, 2, LAGS, PAIRS], whi_at + 29 * KB)
        ki = at("exp_bits", [P, PAIRS], whi_at + 29 * KB + 2304 + 256, I32)
        ll = at("lam_step", [P, 2, 2, PAIRS], whi_at + 17 * KB + 512)
        lam_neg = at("lam_powers_neg", [P, 2, LAGS, PAIRS], whi_at + 20 * KB)
        lam_rev = at("lam_powers_down", [P, 2, TAU, PAIRS], whi_at + 18 * KB)
        bt = at("b_cols", [P, 2, GH, PAIRS], wst_at)
        ct = at("c_cols", [P, 2, PAIRS, GH], wst_at + 4 * KB)
        bb = at("b_bar", [P, 2, 2 * GH, PAIRS], wst_at + 8 * KB)
        l_tmp = at("lam_tmp", [P, 2, GH, PAIRS], tmp_at)
        y_gelu = at("y_gelu", [P, 4, SEQ], tmp_at)
        x_perm = at("x_by_group", [P, 32, TAU, GH], hid_at)

        q_f = at("q_feat", [P, DC, SEQ], hid_at + 16 * KB)
        k_f = at("k_feat", [P, DC, SEQ], hid_at + 60 * KB)
        v_t = at("v_tok", [P, TT, D], res_at)
        k_pair = at("k_pair", [P, 2, SEQ], hid_at + 32 * KB)
        v_pair = at("v_pair", [P, 2, TT, P], hid_at + 36 * KB)
        q_pair = at("q_pair", [P, 2, SEQ], hid_at + 40 * KB)
        drop = at("drop", [P, 2, STICK], tmp_at)
        keep = at("keep", [P, 2, STICK], hid_at + 76 * KB)
        lnp = at("ln_part", [P, STICK], tmp_at + 10 * KB)
        drop_sum = at("drop_sums", [P, 3 * P], hid_at + 86 * KB)
        after, _ = new("mask_after", [P, P])
        before, _ = new("mask_before", [P, P])
        ident_r, _ = new("ident_rounded", [P, P], F32R)
        not_past, _ = new("not_past", [P, P], F32R)

        u_f = at("u_feat", [P, 4, SEQ], hid_at)
        qk_f = at("qk_feat", [P, 8, SEQ], hid_at + 8 * KB)
        gv_t = at("gate_tok", [P, TT, 512], hid_at + 24 * KB)
        vb_t = at("value_tok", [P, TT, 512], hid_at + 32 * KB)
        ws_t = at("mix_rows", [P, 8, P], hid_at + 40 * KB)
        qk_rs = at("qk_rstd", [P, 8, SEQ], hid_at + 44 * KB)
        ws_st = at("mix_stage", [P, 8, P], hid_at + 60 * KB)
        gv_gb = at("gate_norm", [P, 2, 512], hid_at + 64 * KB)
        bias_t = at("score_bias", [P, TT, P], hid_at + 68 * KB)
        mult_t = at("multiplicity", [P, TT, P], hid_at + 70 * KB)
        qn_pair = at("qn_pair", [P, 2, SEQ], hid_at + 72 * KB)
        kn_pair = at("kn_pair", [P, 2, SEQ], hid_at + 76 * KB)
        vb_pair = at("vb_pair", [P, 2, TT, P], hid_at + 80 * KB)
        bs_st = at("mix_bias", [1, 8, P], hid_at + 84 * KB)
        prob = at("prob", [P, 2, STICK], tmp_at)
        prob_t = at("prob_t", [P, STICK], tmp_at + 10 * KB)
        stat = at("even_stats", [P, 128], tmp_at + 15 * KB + 512)
        gv_stats, gv_mv = stat[:, 0:24].rearrange("p (n k) -> p n k", n=TT), stat[:, 24:32].rearrange("p (n k) -> p n k", n=TT)
        gv_rs = stat[:, 32:36]
        neg_max = stat[:, 40:48].rearrange("p (b n) -> p b n", b=2)
        den = stat[:, 48:56].rearrange("p (b n) -> p b n", b=2)
        rden = stat[:, 56:64].rearrange("p (b n) -> p b n", b=2)
        sq_even = at("even_squares", [P, 2, SEQ], tmp_at)
        resid4 = at("residue4", [P, 2, P], tmp_at + 8 * KB)
        head_mean, _ = new("head_mean", [P, P])

        gq = at("gla_q", [P, GLA_HEADS, SEQ], hid_at)
        gk = at("gla_k", [P, GLA_HEADS, SEQ], hid_at + 8 * KB)
        gvt = at("gla_v_tok", [P, TT, D], hid_at + 16 * KB)
        gr = at("gla_r", [P, DC, SEQ], hid_at + 32 * KB)
        cum = at("gla_cum", [P, GLA_HEADS, SEQ], hid_at + 48 * KB)
        attn_t = at("gla_attn", [P, GLA_HEADS, TT, P], hid_at + 48 * KB)
        la = at("gla_log_a", [P, GLA_HEADS, SEQ], hid_at + 56 * KB)
        gkt = at("gla_k_scaled", [P, GLA_HEADS, SEQ], hid_at + 56 * KB)
        ge = at("gla_exp", [P, GLA_HEADS, SEQ], hid_at + 64 * KB)
        gks = at("gla_k_state", [P, GLA_HEADS, SEQ], hid_at + 72 * KB)
        go = at("gla_o", [P, DC, SEQ], hid_at + 64 * KB)
        gks_t = at("gla_k_tok", [P, TT, GLA_HEADS, P], hid_at + 80 * KB)
        ga_t = at("gate_low", [P, SEQ], hid_at + 72 * KB)
        wa2 = at("gate_up", [GATE_RANK, 512], hid_at + 74 * KB)
        wga = at("gate_w", [P, DC, P], tmp_at)
        wga_hi = at("gate_w_hi", [P, DC, P], tmp_at + 4 * KB, F32R)
        wga_lo = at("gate_w_lo", [P, DC, P], tmp_at + 8 * KB, F32R)
        gst = at("gla_states", [P, 2, GLA_CHUNKS, GLA_DV], tmp_at)
        sq_odd = at("gla_squares", [P, 2, SEQ], hid_at + 56 * KB)
        o_rs = at("gla_rstd", [P, 2, SEQ], hid_at + 60 * KB)
        decay = d_bc[:, 0:GLA_HEADS * GLA_CHUNKS].rearrange("p (h n) -> p h n", h=GLA_HEADS)
        chunk_mask, _ = new("chunk_mask", [P, P])
        keep_sum = at("keep_sum", [P, SEQ], hid_at + 78 * KB)

        out_t = at("out_tok", [P, TT, D], hid_at)

        w_landed = [sem("w_landed0"), sem("w_landed1")]
        whi_done, wlo_done = sem("whi_done"), sem("wlo_done")
        part_done, evac_done = sem("part_done"), sem("evac_done")
        act_out, zhi_done = sem("act_out"), sem("zhi_done")
        hid_ready = sem("hid_ready")
        ld_a, ld_b, ld_c, ld_x, ld_d, ld_prm = (sem(f"ld_{n}") for n in "a b c x d prm".split())
        consts, dve_link, act_link = sem("consts"), sem("dve_link"), sem("act_link")
        a_rows, tr_a, tr_b, tr_c, tr_prm = (sem(n) for n in "a_rows tr_a tr_b tr_c tr_prm".split())
        b_copied, c_copied, tr_u, u_copied = (sem(n) for n in "b_copied c_copied tr_u u_copied".split())
        trig_in, trig_out = sem("trig_in"), sem("trig_out")
        bb_ready, lam_ready, v_ready, tr_v, vt_copied = (
            sem(n) for n in "bb_ready lam_ready v_ready tr_v vt_copied".split())
        w_ready, pool_link, k_done, k_copied, toe_zero, toe_ready, toe_last = (
            sem(n) for n in "w_ready pool_link k_done k_copied toe_zero toe_ready toe_last".split())
        s_in, s_copied, tr_x, xhi_done, xd_ready, scan_done = (
            sem(n) for n in "s_in s_copied tr_x xhi_done xd_ready scan_done".split())
        y_done, y_copied, tr_y, gelu_done = (sem(n) for n in "y_done y_copied tr_y gelu_done".split())
        x_ready, x_permuted = sem("x_ready"), sem("x_permuted")
        ln_sums, ln_xc, ln_sq, ln_sq_used, ln_n, ln_a, ln_hi = (
            sem(n) for n in "ln_sums ln_xc ln_sq ln_sq_used ln_n ln_a ln_hi".split())
        shift_done, ln_shifted, dev_sq, ln_m2, ln_var = (
            sem(n) for n in "shift_done ln_shifted dev_sq ln_m2 ln_var".split())
        qk_staged, v_staged, z_done, z_copied, ln_part, sp_done, lb_done = (
            sem(n) for n in "qk_staged v_staged z_done z_copied ln_part sp_done lb_done".split())
        cs_done, lw_done, w_done, o_done, o_hi, o_ready, soft_link = (
            sem(n) for n in "cs_done lw_done w_done o_done o_hi o_ready soft_link".split())
        ld_even, tab_done, ws_tr, ws_copied, ws_ready, s4_ready, tables = (
            sem(n) for n in "ld_even tab_done ws_tr ws_copied ws_ready s4_ready tables".split())
        ev_link, gv_link, qk_sq, qk_ms, qk_ln, qk_rstd, gv_var, gv_rstd, gv_scaled, gv_gained, vn_ready = (
            sem(n) for n in "ev_link gv_link qk_sq qk_ms qk_ln qk_rstd gv_var gv_rstd gv_scaled gv_gained vn_ready".split())
        gm_done, gm_copied, gm_hi, gm_ready = (sem(n) for n in "gm_done gm_copied gm_hi gm_ready".split())
        qn_ready, vb_staged, sc_done, sm_done, mx_done, pexp, den_done, pn_done, tr_p, pt_copied, pv_done, b_hi, b_ready, ttr_link = (
            sem(n) for n in ("qn_ready vb_staged sc_done sm_done mx_done pexp den_done pn_done tr_p pt_copied pv_done "
                             "b_hi b_ready ttr_link").split())
        ld_odd, wga_zero, wga_hi_s, wga_ready, ga_done, ga_copied, la_done, la_lin, la_link, ln_a1, cum_done = (
            sem(n) for n in ("ld_odd wga_zero wga_hi_s wga_ready ga_done ga_copied la_done la_lin la_link ln_a1 cum_done").split())
        ek_done, gq_done, en_done, gkt_done, last_done, es_done, gks_done, tr_k, kt_copied, at_done, at_ready = (
            sem(n) for n in ("ek_done gq_done en_done gkt_done last_done es_done gks_done tr_k kt_copied at_done at_ready").split())
        kv_done, st_ready, st_link, go_done, go_copied, go_sq, go_ms, go_link, go_hi, go_ready = (
            sem(n) for n in ("kv_done st_ready st_link go_done go_copied go_sq go_ms go_link go_hi go_ready").split())
        conv_a, conv_b, rms_t, tr_out, out_rows = (
            sem(n) for n in "conv_a conv_b rms_t tr_out out_rows".split())
        acc_link = sem("acc_link")
        mask_ones, mask_rounded = sem("mask_ones"), sem("mask_rounded")
        prm_copied, out_done = sem("prm_copied"), sem("out_done")

        block = ctx.enter_context(nc.Block())

        def linker(eng, s):
            count = [0]

            def link(ins):
                count[0] += 1
                ins.then_inc(s, 1)
                eng.wait_ge(s, count[0])
            return link

        norm_stage = {0: "ssm_out", 1: "down0", 2: "w_o", 3: "down1", 5: "ev_out", 6: "cdown0", 7: "od_out"}

        def chunk_done(n, c):
            return ST[norm_stage[n]].evac0 + c + 1

        def sq_count(n):
            return 0 if n <= 4 else DC + n - 5

        def acc_count(n):
            return 18 * min(n + 1, 4) + 14 * max(n - 4, 0)

        def wcols(w, col, n=256):
            return w.rearrange("(k p) n -> p k n", p=P)[:, :, bass.ds(col, n)]

        def tile_source(name, i, half, first=0):
            if name == "glu":
                return wcols(t["ssm_w_glu"][0], i * 256 + (first * 256 + (1 - half) * D))
            if name in ("ssm_out", "w_o", "ev_out", "od_out"):
                w = {"ssm_out": "ssm_w_out", "w_o": "sb_w_o", "ev_out": "ev_w_out_2", "od_out": "od_w_out_2"}[name]
                return wcols(t[w][0], i * 512 + half * 256)
            if name in ("gu0", "gu1"):
                return wcols(t["ffn_w_gu"][int(name[-1])], i * 256 + half * FFN)
            if name in ("conv0", "conv1"):
                return wcols(t["ffn_w_up_2" if half else "ffn_w_gate_2"][int(name[-1])], i * 256)
            if name in ("down0", "down1", "cdown0", "cdown1"):
                w = t["ffn_w_down_2" if name[0] == "c" else "ffn_w_down"][int(name[-1])]
                rows = w.rearrange("(k p) n -> p k n", p=P)[:, half * DOWN_K:(half + 1) * DOWN_K]
                return rows[:, :, bass.ds(i * P, P)]
            w, col = {
                "q": ("sb_w_qkv", 0), "k": ("sb_w_qkv", D), "v": ("sb_w_qkv", 2 * D),
                "ev_u": ("ev_w_in_2", 0), "ev_v": ("ev_w_in_2", 512), "ev_qk": ("ev_w_in_2", 1024),
                "ev_vb": ("ev_w_in_2", 2048),
                "od_q": ("od_w_in_2", 0), "od_k": ("od_w_in_2", 512), "od_v": ("od_w_in_2", 1024), "od_r": ("od_w_in_2", 2048),
            }[name]
            return wcols(t[w][0], i * 512 + half * 256 + col)

        def tile_view(w, name, half):
            if "down" in name:
                return w[:, half, 0:DOWN_K * P].rearrange("p (k n) -> p k n", k=DOWN_K)
            return w[:, half, :].rearrange("p (k n) -> p k n", k=DC)

        TOE_POOL = 5 * TAU // 8

        def toeplitz_rows(eng, s, done):
            for q in range(4):
                eng.dma_start(toe[s * GH:(s + 1) * GH, (q // 2) * 32 + q % 2:(q // 2) * 32 + 32:2, s * GH:P],
                              k_rows[q * 32:q * 32 + GH, :, 0:P - s * GH]).then_inc(done, 16)

        @block.sync
        def _(sp):
            sp.dma_start(a_st[:, 0, :], t["ssm_a_re"][0].rearrange("(j g) p -> j (g p)", g=2)).then_inc(ld_a, 16)
            sp.dma_start(a_st[:, 1, :], t["ssm_a_im"][0].rearrange("(j g) p -> j (g p)", g=2)).then_inc(ld_a, 16)
            sp.dma_start(dt_st[:, :], t["ssm_log_dt"][0].rearrange("(j g) -> j g", g=2)).then_inc(ld_a, 16)
            for ri, name in enumerate(("ssm_b_re", "ssm_b_im")):
                sp.dma_start(b_st[:, ri, :], t[name][0].rearrange("(j g) p h -> j (g p h)", g=2)).then_inc(ld_b, 16)
            xv = t["x"][0].rearrange("(c s) (hf f) -> hf c s f", s=TAU, hf=2)
            for hf in range(2):
                sp.dma_start(xnat[hf * 64:hf * 64 + 64, :, :], xv[hf]).then_inc(ld_x, 16)
            for ri, name in enumerate(("ssm_c_re", "ssm_c_im")):
                cv = t[name][0].rearrange("(n q) h p -> (q h) n p", q=8)
                for dup in range(2):
                    sp.dma_start(c_st[:, ri, :, dup, :], cv).then_inc(ld_c, 16)
            for hf in range(2):
                sp.dma_start(d_bc[hf * 64:hf * 64 + 64, :],
                             t["ssm_d"][:, hf * 512:hf * 512 + 512].to_broadcast([64, 512])).then_inc(ld_d, 16)
            row = 0
            for name in ("ln_mix_g", "ln_mix_b", "ln_ffn_g", "ln_ffn_b", "norm_mix_g_2", "norm_ffn_g_2"):
                sp.dma_start(prm_st[row:row + 2 * DC, :], t[name].rearrange("l (c p) -> (l c) p", p=P)).then_inc(ld_prm, 16)
                row += 2 * DC
            sp.dma_start(conv_st[0:TAPS * FC, :, :],
                         t["ffn_conv_w_2"].rearrange("l k (c p) -> (k c) l p", p=P)).then_inc(ld_prm, 16)
            sp.dma_start(conv_st[TAPS * FC:CROW, :, :],
                         t["ffn_conv_b_2"].rearrange("l (c p) -> c l p", p=P)).then_inc(ld_prm, 16)
            sp.dma_start(small_st[0:4, :], t["od_b_a_2"][0].rearrange("(c p) -> c p", p=P)).then_inc(ld_prm, 16)
            sp.dma_start(small_st[4:6, :], t["od_head_g_2"][0].rearrange("(c p) -> c p", p=P)).then_inc(ld_prm, 16)
            for row, name in ((6, "ev_q_g_2"), (7, "ev_k_g_2")):
                for dup in range(2):
                    sp.dma_start(small_st[row:row + 1, dup * HD:(dup + 1) * HD], t[name]).then_inc(ld_prm, 16)
            sp.wait_ge(v_ready, 8)
            sp.wait_ge(w_ready, 8)
            sp.wait_ge(prm_copied, 1)
            sp.wait_ge(k_done, 4)
            sp.wait_ge(k_copied, 4)
            sp.wait_ge(toe_zero, 1)
            for s in range(TOE_POOL):
                toeplitz_rows(sp, s, toe_ready)
            for name in run:
                st = ST[name]
                first = 1 if st.it0 == 0 else 0
                if first:
                    for half in range(2):
                        sp.dma_start(tile_view(wst, name, half), tile_source(name, 0, half)).then_inc(w_landed[half], 16)
                with sp.Fori(0, st.iters - first) as i:
                    for half in range(2):
                        source = tile_source(name, i, half, first)
                        sp.wait_ge(wlo_done, i * 2 + ((st.it0 + first) * 2 + half - 1))
                        sp.dma_start(tile_view(wst, name, half), source).then_inc(w_landed[half], 16)
            for n in range(TT):
                sp.wait_ge(out_rows, n + 1)
                sp.dma_start(out[0, n * P:(n + 1) * P, :], out_t[:, n, :]).then_inc(out_done, 16)
            sp.wait_ge(out_done, TT * 16)

        @block.gpsimd
        def _(pool):
            link = linker(pool, pool_link)
            link(nc.gpsimd.memset(ident[:, :], 0.0))
            nc.gpsimd.affine_select(out=ident[:, :], in_=ident[:, :], compare_op=ALU.not_equal, fill=1.0, base=0,
                                    pattern=[[-1, P]], channel_multiplier=1).then_inc(consts, 1)
            link(nc.gpsimd.memset(after[:, :], 1.0))
            nc.gpsimd.affine_select(out=after[:, :], in_=after[:, :], compare_op=ALU.is_gt, fill=0.0, base=0,
                                    pattern=[[1, P]], channel_multiplier=-1).then_inc(consts, 1)
            link(nc.gpsimd.memset(before[:, :], 1.0))
            nc.gpsimd.affine_select(out=before[:, :], in_=before[:, :], compare_op=ALU.is_gt, fill=0.0, base=0,
                                    pattern=[[-1, P]], channel_multiplier=1).then_inc(consts, 1)
            pool.wait_ge(mask_ones, 1)
            nc.gpsimd.affine_select(out=chunk_mask[:, :], in_=chunk_mask[:, :], compare_op=ALU.is_ge, fill=0.0, base=0,
                                    pattern=[[1, P]], channel_multiplier=-1).then_inc(consts, 1)
            nc.gpsimd.memset(toe[:, :, :], 0.0).then_inc(toe_zero, 1)
            pool.wait_ge(c_copied, 16)
            pool.wait_ge(lam_ready, 1)
            pool.wait_ge(tr_u, 8)
            shape = [P, 4, LAGS, GH]

            def still():
                nc.gpsimd.tensor_tensor(pool_pad[:, :], one_col[:, :], one_col[:, :], ALU.mult)

            with pool.Fori(0, PAIRS // 4) as i:
                js = bass.ds(i * 4, 4)
                l4, neg4 = ([x[:, ri, :, js].rearrange("p k j -> p j k").unsqueeze(3).to_broadcast(shape) for ri in range(2)]
                            for x in (lam, lam_neg))
                c4 = [ct[:, ri, js, :].unsqueeze(2).to_broadcast(shape) for ri in range(2)]
                wr, wi = w_re[:, js, :, :], w_im[:, js, :, :]
                nc.gpsimd.tensor_tensor(wr, c4[0], l4[0], ALU.mult).then_inc(pool_link, 1)
                nc.gpsimd.tensor_tensor(w_tmp[:, :, :, :], c4[1], neg4[1], ALU.mult).then_inc(pool_link, 1)
                nc.gpsimd.tensor_tensor(wi, c4[0], neg4[1], ALU.mult).then_inc(pool_link, 1)
                pool.wait_ge(pool_link, i * 5 + 6)
                still()
                nc.gpsimd.tensor_tensor(wr, wr, w_tmp[:, :, :, :], ALU.add).then_inc(pool_link, 1)
                pool.wait_ge(pool_link, i * 5 + 7)
                still()
                nc.gpsimd.tensor_tensor(w_tmp[:, :, :, :], c4[1], neg4[0], ALU.mult).then_inc(pool_link, 1)
                pool.wait_ge(pool_link, i * 5 + 8)
                still()
                nc.gpsimd.tensor_tensor(wi, wi, w_tmp[:, :, :, :], ALU.add).then_inc(w_ready, 1)
                pool.wait_ge(w_ready, i + 1)
            pool.wait_ge(toe_zero, 1)
            pool.wait_ge(k_copied, 4)
            for s in range(TOE_POOL, TAU):
                toeplitz_rows(pool, s, toe_last)
            pool.wait_ge(tr_x, 8)
            pool.wait_ge(tr_u, 8)
            pool.wait_ge(ld_d, 32)
            nc.gpsimd.tensor_tensor(xnat[:, :, :], xnat[:, :, :], d_bc[:, :].unsqueeze(1).to_broadcast([P, TAU, 512]),
                                    ALU.mult).then_inc(xd_ready, 1)

            sum_link = linker(pool, acc_link)

            def split_last(n):
                st = ST[norm_stage[n]]
                pool.wait_ge(whi_done, (st.it0 + st.iters) * 2 + 2)
                sum_link(nc.gpsimd.tensor_tensor(wlo[:, 1, :], wst[:, 1, :], whi[:, 1, :].bitcast(F32), ALU.subtract))

            def deviation_sums(n):
                pool.wait_ge(evac_done, chunk_done(n, 1))
                sum_link(nc.gpsimd.tensor_tensor(acc, res[:, 0, :], res[:, 1, :], ALU.add))
                pool.wait_ge(shift_done, n + 1)
                for c in range(1, DC - 1):
                    if c < 4:
                        pool.wait_ge(ln_shifted, n * DC + c + 1)
                    else:
                        pool.wait_ge(evac_done, chunk_done(n, c))
                    sum_link(nc.gpsimd.tensor_tensor(acc, res[:, 0, :] if c == 1 else acc, res[:, c, :], ALU.add))
                    pool.wait_ge(dev_sq, n * DC + c + 1)
                    sum_link(nc.gpsimd.tensor_tensor(acc_sq, acc_sq, dev_slot[c], ALU.add))
                pool.wait_ge(ln_m2, 2 * n + 2)
                pool.wait_ge(dev_sq, (n + 1) * DC)
                for c in range(4, DC):
                    sum_link(nc.gpsimd.tensor_tensor(res[:, c, :], res[:, c, :], mean, ALU.subtract))
                split_last(n)

            def square_sums(n):
                for c in range(DC - 1):
                    pool.wait_ge(evac_done, chunk_done(n, c))
                    chunk = res[:, c, :]
                    sum_link(nc.gpsimd.tensor_tensor(acc if c == 0 else acc_sq, chunk, chunk, ALU.mult))
                    if c > 0:
                        sum_link(nc.gpsimd.tensor_tensor(acc, acc, acc_sq, ALU.add))
                split_last(n)

            deviation_sums(0)
            deviation_sums(1)
            pool.wait_ge(consts, 4)
            pool.wait_ge(evac_done, ST["v"].evac1)

            def stage_pair(i, pp, after_mix=None):
                p = i * 2 + pp
                nc.gpsimd.tensor_copy(q_pair[:, pp:pp + 1, :], q_f[:, bass.ds(p, 1), :])
                nc.gpsimd.tensor_copy(k_pair[:, pp:pp + 1, :], k_f[:, bass.ds(p, 1), :]).then_inc(qk_staged, 1)
                if after_mix is not None:
                    pool.wait_ge(o_done, after_mix)
                nc.gpsimd.tensor_copy(v_pair[:, pp, :, :], v_t[:, :, bass.ds(p * P, P)]).then_inc(v_staged, 1)

            for pp in range(2):
                stage_pair(0, pp)
            with pool.Fori(0, HEADS // 4 - 1) as i:
                for pp in range(2):
                    pool.wait_ge(z_done, i * 4 + (2 * pp + 2))
                    stage_pair(i + 1, pp, i * 4 + (2 * pp + 3))

            deviation_sums(2)
            deviation_sums(3)
            pool.wait_ge(part_done, ST["down1"].part1)
            pool.dma_start(ws_st[:, :, :], t["ev_a_ws_2"][0].rearrange("g t s -> t g s")).then_inc(ld_even, 16)
            pool.dma_start(bs_st[:, :, :], t["ev_a_bs_2"]).then_inc(ld_even, 16)
            for n, name in enumerate(("ev_a_ln_g_2", "ev_a_ln_b_2")):
                pool.dma_start(gv_gb[:, n, :], t[name].to_broadcast([P, 512])).then_inc(ld_even, 16)
            pool.wait_ge(x_ready, 5 * DC)
            nc.gpsimd.memset(resid4[:, :, :], 0.0).then_inc(s4_ready, 1)
            pool.wait_ge(s4_ready, 1)
            for n, m in enumerate((4, 16)):
                nc.gpsimd.affine_select(out=resid4[:, n, :].rearrange("p (a b) -> p a b", b=m),
                                        in_=resid4[:, n, :].rearrange("p (a b) -> p a b", b=m),
                                        compare_op=ALU.not_equal, fill=1.0, base=0, pattern=[[0, P // m], [-1, m]],
                                        channel_multiplier=1).then_inc(s4_ready, 1)
            pool.wait_ge(ws_copied, 2)
            for g in range(8):
                nc.gpsimd.affine_select(out=ws_t[:, g, :], in_=ws_t[:, g, :], compare_op=ALU.is_ge, fill=0.0, base=0,
                                        pattern=[[1, P]], channel_multiplier=-1).then_inc(ws_ready, 1)
            for n in range(TT):
                pool.wait_ge(gv_scaled, n + 1)
                nc.gpsimd.tensor_tensor(gv_t[:, n, :], gv_t[:, n, :], gv_gb[:, 0, :], ALU.mult).then_inc(gv_gained, 1)
                pool.wait_ge(gv_gained, n + 1)
                nc.gpsimd.tensor_tensor(gv_t[:, n, :], gv_t[:, n, :], gv_gb[:, 1, :], ALU.add).then_inc(vn_ready, 1)
            pool.wait_ge(evac_done, ST["ev_vb"].evac1)
            for p in range(4):
                if p >= 2:
                    pool.wait_ge(pv_done, 2 * p - 1)
                nc.gpsimd.tensor_copy(vb_pair[:, p % 2, :, :], vb_t[:, :, p * P:(p + 1) * P]).then_inc(vb_staged, 1)
            pool.wait_ge(gm_copied, 4)
            for c in range(4):
                nc.gpsimd.tensor_copy(xhi[:, c, :], u_f[:, c, :]).then_inc(gm_hi, 1)
                pool.wait_ge(gm_hi, c + 1)
                nc.gpsimd.tensor_tensor(xlo[:, c, :], u_f[:, c, :], xhi[:, c, :].bitcast(F32), ALU.subtract).then_inc(gm_ready, 1)
            square_sums(5)
            square_sums(6)
            pool.wait_ge(part_done, ST["cdown0"].part1)
            pool.wait_ge(x_ready, 7 * DC)
            nc.gpsimd.memset(wga[:, :, :], 0.0).then_inc(wga_zero, 1)
            pool.wait_ge(wga_zero, 1)
            pool.dma_start(wga[:, :, 0:GATE_RANK], t["od_w_in_2"][0].rearrange("(k p) n -> p k n", p=P)[:, :, 3072:3088])\
                .then_inc(ld_odd, 16)
            pool.dma_start(wa2[:, :], t["od_w_a2_2"][0]).then_inc(ld_odd, 16)
            pool.wait_ge(ld_odd, 32)
            nc.gpsimd.tensor_copy(wga_hi[:, :, :], wga[:, :, :]).then_inc(wga_hi_s, 1)
            pool.wait_ge(wga_hi_s, 1)
            nc.gpsimd.tensor_tensor(wga_lo[:, :, :], wga[:, :, :], wga_hi[:, :, :].bitcast(F32), ALU.subtract).then_inc(wga_ready, 1)
            square_sums(7)

        @block.tensor
        def _(pe):
            pe.wait_ge(consts, 1)
            pe.wait_ge(a_rows, 1)
            for n in range(3):
                mm = nc.tensor.transpose(bank[0][:, n * PAIRS:(n + 1) * PAIRS], a_st[:, n, :], ident[0:PAIRS, 0:PAIRS])
            mm.then_inc(tr_a, 1)
            pe.wait_ge(ld_b, 32)
            for ri in range(2):
                rows = b_st[:, ri, :].rearrange("j (q h) -> j h q", h=GH)
                for h in range(GH):
                    mm = nc.tensor.transpose(bank[1 + ri][:, h * PAIRS:(h + 1) * PAIRS], rows[:, h, :],
                                             ident[0:PAIRS, 0:PAIRS])
                mm.then_inc(tr_b, 1)
            pe.wait_ge(ld_c, 64)
            for ri in range(2):
                for n in range(8):
                    mm = nc.tensor.transpose(bank[3 + 2 * ri + n // 4][:, (n % 4) * P:(n % 4 + 1) * P],
                                             c_st[:, ri, n, :, :].rearrange("p a b -> p (a b)"), ident[:, :])
                    if n % 4 == 3:
                        mm.then_inc(tr_c, 1)
            pe.wait_ge(ld_prm, 14 * 16)
            nc.tensor.transpose(bank[7][:, 0:NROW], prm_st[:, :], ident[0:NROW, 0:NROW])
            for layer in range(2):
                at_ = NROW + layer * CROW
                nc.tensor.transpose(bank[7][:, at_:at_ + CROW], conv_st[:, layer, :], ident[0:CROW, 0:CROW])
            nc.tensor.transpose(bank[7][:, small0:small0 + SROW], small_st[:, :], ident[0:SROW, 0:SROW]).then_inc(tr_prm, 1)
            pe.wait_ge(x_permuted, 1)
            pe.wait_ge(dve_link, 1)
            for b in range(8):
                if b == 1:
                    pe.wait_ge(b_copied, 2)
                if b == 3:
                    pe.wait_ge(c_copied, 16)
                if b == 7:
                    pe.wait_ge(prm_copied, 1)
                for n in range(8):
                    g = b * 8 + n
                    hf = g // 32
                    rows = x_perm[hf * 64:hf * 64 + 64, g % 32, :, :].rearrange("p s h -> p (s h)")
                    mm = nc.tensor.transpose(bank[b][:, n * NCH:(n + 1) * NCH], rows,
                                             ident[hf * 64:hf * 64 + 64, hf * 64:hf * 64 + 64])
                mm.then_inc(tr_u, 1)
            def x_features(f, b):
                hf = f // 4
                for s in range(TAU):
                    mm = nc.tensor.transpose(bank[b][:, s * NCH:(s + 1) * NCH],
                                             xnat[hf * 64:hf * 64 + 64, s, (f % 4) * P:(f % 4 + 1) * P],
                                             ident[hf * 64:hf * 64 + 64, hf * 64:hf * 64 + 64])
                return mm

            for f in range(DC):
                pe.wait_ge(u_copied, f + 1)
                x_features(f, f).then_inc(tr_x, 1)

            def v_rows(n):
                pe.wait_ge(v_ready, n + 1)
                if n >= 2:
                    pe.wait_ge(vt_copied, 2 * (n - 1) + 1)
                for ri in range(2):
                    for jj in range(4):
                        mm = nc.tensor.transpose(bank[2 * (n % 2) + ri][:, jj * P:(jj + 1) * P], v_buf[:, n % 2, ri, jj, :],
                                                 ident[:, :])
                    mm.then_inc(tr_v, 1)

            def state_inputs(n):
                pe.wait_ge(vt_copied, 2 * (n + 1) + 1)
                if n >= 2:
                    pe.wait_ge(s_copied, n - 1)
                for jj in range(4):
                    for ri in range(2):
                        for half in range(2):
                            mm = nc.tensor.matmul(bank[4 + n % 2][half * 64:half * 64 + 64, (jj * 2 + ri) * NCH:(jj * 2 + ri + 1) * NCH],
                                                  vt[n % 2][:, ri, jj, half * 64:half * 64 + 64], uu[:, 2 * (4 * n + jj) + half, :],
                                                  start=True, stop=True)
                mm.then_inc(s_in, 1)

            for n in range(8):
                v_rows(n)
                if n > 0:
                    state_inputs(n - 1)
            state_inputs(7)
            pe.wait_ge(s_copied, 8)
            for b in range(4):
                pe.wait_ge(w_ready, 4 + b + 1)
                for q in range(4):
                    for s in range(4):
                        g = (q // 2) * 32 + 2 * (b * 4 + s) + q % 2
                        j, half = g // 2, (g % 2) * 64
                        for ri, w in enumerate((w_re, w_im)):
                            mm = nc.tensor.matmul(bank[4 + b][q * 32:q * 32 + 32, s * P:(s + 1) * P],
                                                  bb[half:half + 64, ri, :, j], w[half:half + 64, j, 0:TAU, :], start=(ri == 0), stop=(ri == 1))
                mm.then_inc(k_done, 1)

            def y_parts(b):
                for hf in range(2):
                    for s in range(4):
                        yield hf * 32 + (b // 2) * 8 + 2 * s + b % 2, bank[b][hf * 64:hf * 64 + 64, s * P:(s + 1) * P]

            pe.wait_ge(s_copied, 8)
            pe.wait_ge(k_copied, 4)
            pe.wait_ge(toe_ready, TOE_POOL * 4 * 16)
            pe.wait_ge(toe_last, (TAU - TOE_POOL) * 4 * 16)
            for b in range(8):
                for n, (g, dst) in enumerate(y_parts(b)):
                    nc.tensor.matmul(dst, uu[:, g, :], toe[:, g, :], start=(n % 4 == 0), stop=False, skip_group_check=True)

            def y_features(n):
                pe.wait_ge(y_copied, n // 2 * 2 + 2)
                x_features((n % 2) * 4 + n // 2, n).then_inc(tr_y, 1)

            pe.wait_ge(scan_done, 1)
            for b in range(8):
                for g, dst in y_parts(b):
                    j, half = g // 2, (g % 2) * 64
                    for ri, w in enumerate((w_re, w_im)):
                        mm = nc.tensor.matmul(dst, states[half:half + 64, 0:NCH, ri, j], w[half:half + 64, j, 1:LAGS, :],
                                              start=False, stop=(ri == 1), skip_group_check=True)
                mm.then_inc(y_done, 1)
                if b >= 3 and b % 2 == 1:
                    y_features(b - 3)
                    y_features(b - 2)
            y_features(6)
            y_features(7)

            def products(dst, name, half, col, kn, xh, xl, k0, start, stop):
                wh, wl = tile_view(whi, name, half), tile_view(wlo, name, half)
                for k in range(kn):
                    hi, lo = wh[:, k, col:col + P], wl[:, k, col:col + P]
                    nc.tensor.matmul(dst, hi, xh[:, k0 + k, :], start=(start and k == 0), stop=False)
                    nc.tensor.matmul(dst, hi, xl[:, k0 + k, :], start=False, stop=False)
                    mm = nc.tensor.matmul(dst, lo, xh[:, k0 + k, :], start=False, stop=(stop and k == kn - 1))
                return mm

            def feature_stage(name, xh, xl, ready, shift_of=None):
                st = ST[name]

                def bank_free(i, b):
                    if st.evacs == 2:
                        pe.wait_ge(evac_done, i * 2 + (st.evac0 + b % 2 - 1))
                    else:
                        pe.wait_ge(evac_done, i * 4 + (st.evac0 + b - 3))

                pe.wait_ge(evac_done, st.evac0)

                def units4(i):
                    pe.wait_ge(wlo_done, i * 2 + (st.it0 * 2 + 1))
                    wh, wl = tile_view(whi, name, 0), tile_view(wlo, name, 0)
                    for k in range(DC):
                        pe.wait_ge(*ready(k))
                        for u in range(2):
                            if k == 0:
                                bank_free(i, u)
                            hi, lo = wh[:, k, u * P:(u + 1) * P], wl[:, k, u * P:(u + 1) * P]
                            nc.tensor.matmul(bank[u], hi, xh[:, k, :], start=(k == 0), stop=False)
                            nc.tensor.matmul(bank[u], hi, xl[:, k, :], start=False, stop=False)
                            mm = nc.tensor.matmul(bank[u], lo, xh[:, k, :], start=False, stop=(k == DC - 1))
                            if k == DC - 1:
                                mm.then_inc(part_done, 1)
                    pe.wait_ge(wlo_done, i * 2 + (st.it0 * 2 + 2))
                    for u in range(2):
                        bank_free(i, 2 + u)
                        products(bank[2 + u], name, 1, u * P, DC, xh, xl, 0, True, True).then_inc(part_done, 1)

                if shift_of is None:
                    with pe.Fori(0, st.iters) as i:
                        units4(i)
                else:
                    units4(0)
                    shift(shift_of)
                    units4(1)

            def down_stage(name, shift_of=None):
                st = ST[name]
                pe.wait_ge(evac_done, st.evac0)

                def units2(i):
                    for u in range(2):
                        pe.wait_ge(evac_done, i * 2 + (st.evac0 + u - 1))
                        for half in range(2):
                            pe.wait_ge(hid_ready, st.pair0 - (1 - half) * DOWN_K)
                            pe.wait_ge(wlo_done, i * 4 + ((st.it0 + u) * 2 + half + 1))
                            mm = products(bank[u][:, :], name, half, 0, DOWN_K, hhi, hlo, half * DOWN_K, half == 0, half == 1)
                            mm.then_inc(part_done, 1)

                pairs = st.iters // 2
                if shift_of is None:
                    with pe.Fori(0, pairs) as i:
                        units2(i)
                else:
                    with pe.Fori(0, pairs // 2) as i:
                        units2(i)
                    shift(shift_of)
                    with pe.Fori(0, pairs // 2) as i:
                        units2(i + pairs // 2)

            def shift(n):
                pe.wait_ge(acc_link, acc_count(n - 1) + 1)
                nc.tensor.matmul(bank[4], ones[:, :], acc[:, :], start=True, stop=True).then_inc(shift_done, 1)

            def mean_square(n, c, first, last):
                pe.wait_ge(ln_sq, sq_count(n) + c + 1)
                nc.tensor.matmul(bank[5], ones_mean[:, :], sq[:, c % 2, :], start=first, stop=last).then_inc(ln_sq_used, 1)

            def norm(n):
                if n == 4:
                    for c in range(DC):
                        mean_square(n, c, c == 0, c == DC - 1)
                    return
                pe.wait_ge(acc_link, acc_count(n - 1) + 13)
                nc.tensor.matmul(bank[5], ones_mean[:, :], acc[:, :], start=True, stop=False)
                if n > 4:
                    mean_square(n, 0, False, True)
                    return
                pe.wait_ge(evac_done, chunk_done(n, DC - 1))
                nc.tensor.matmul(bank[5], ones_mean[:, :], res[:, DC - 1, :], start=False, stop=True).then_inc(ln_sums, 1)
                nc.tensor.matmul(bank[6], ones_mean[:, :], acc_sq[:, :], start=True, stop=False)
                pe.wait_ge(dev_sq, (n + 1) * DC)
                nc.tensor.matmul(bank[6], ones_mean[:, :], dev_slot[DC - 1], start=False, stop=True).then_inc(ln_sums, 1)

            def token_stage(name, xh, xl):
                st = ST[name]
                pe.wait_ge(evac_done, st.evac0)
                with pe.Fori(0, st.iters) as i:
                    for half in range(2):
                        pe.wait_ge(wlo_done, i * 2 + (st.it0 * 2 + half + 1))
                        wh, wl = tile_view(whi, name, half), tile_view(wlo, name, half)
                        for n in range(TT):
                            pe.wait_ge(evac_done, i * 8 + (st.evac0 + 4 * half + n - 7))
                            dst = bank[4 * half + n][:, 0:256]
                            for k in range(DC):
                                hi, lo = xh[:, k, n * P:(n + 1) * P], xl[:, k, n * P:(n + 1) * P]
                                nc.tensor.matmul(dst, hi, wh[:, k, :], start=(k == 0), stop=False)
                                nc.tensor.matmul(dst, hi, wl[:, k, :], start=False, stop=False)
                                mm = nc.tensor.matmul(dst, lo, wh[:, k, :], start=False, stop=(k == DC - 1))
                            mm.then_inc(part_done, 1)

            def stick_attention():
                pe.wait_ge(evac_done, ST["v"].evac1)
                pe.wait_ge(consts, 4)
                pe.wait_ge(mask_rounded, 1)

                def scores(pair, hd, h):
                    pe.wait_ge(qk_staged, pair + 1)
                    pe.wait_ge(z_copied, h + 1)
                    half = slice((hd % 2) * 64, (hd % 2) * 64 + 64)
                    flat = psum[:, 0:3, :].rearrange("p b n -> p (b n)")
                    for j in range(TT):
                        kt = k_pair[half, (hd // 2) % 2, j * P:(j + 1) * P]
                        nc.tensor.matmul(flat[:, j * P:(j + 1) * P], kt, q_pair[half, (hd // 2) % 2, j * P:(j + 1) * P],
                                         start=True, stop=False)
                        mm = nc.tensor.matmul(flat[:, j * P:(j + 1) * P], ident_r[:, :], not_past[:, :], start=False, stop=True)
                        if j < TT - 1:
                            n = SEQ - (j + 1) * P
                            mm = nc.tensor.matmul(flat[:, REST[j]:REST[j] + n], kt,
                                                  q_pair[half, (hd // 2) % 2, (j + 1) * P:SEQ],
                                                  start=True, stop=True)
                    mm.then_inc(z_done, 1)

                def sums(hd, h):
                    pe.wait_ge(sp_done, h * 4 + 1)
                    pe.wait_ge(lw_done, h + 1)
                    flat = psum[:, 4:7, :].rearrange("p b n -> p (b n)")
                    sp = drop[:, hd % 2, :]
                    for c0, c1 in ((0, 512), (512, 1024), (1024, 1280)):
                        nc.tensor.matmul(flat[:, c0:c1], before[:, :], sp[:, c0:c1], start=True, stop=(c0 == 0),
                                         skip_group_check=True)
                    for j in range(TT - 1):
                        nc.tensor.matmul(flat[:, REST[j]:REST[j] + P], ones[:, :], sp[:, (j + 1) * P:(j + 2) * P],
                                         start=False, stop=True, skip_group_check=True)
                    pe.wait_ge(sp_done, h * 4 + 4)
                    for to, c0, c1 in ((REST[1] + P, 2 * P, 3 * P), (REST[0] + P, 0, 2 * P)):
                        mm = nc.tensor.matmul(flat[:, to:to + c1 - c0], ones[:, :], drop_sum[:, c0:c1], start=False, stop=True,
                                              skip_group_check=True)
                    mm.then_inc(cs_done, 1)

                def mix(hd, h, pair):
                    pe.wait_ge(w_done, h + 1)
                    pe.wait_ge(v_staged, pair + 1)
                    if hd % 2 == 0:
                        pe.wait_ge(o_ready, pair + 1)
                    half = (hd % 2) * 64
                    dst = bank[7][half:half + 64, :]
                    w = keep[:, hd % 2, :]
                    for j in range(TT):
                        vt_ = v_pair[:, (hd // 2) % 2, j, half:half + 64]
                        mm = nc.tensor.matmul(dst[:, j * P:(j + 1) * P], vt_, w[:, j * P:(j + 1) * P], start=(j == 0),
                                              stop=True, skip_group_check=True)
                        if j < TT - 1:
                            n = SEQ - (j + 1) * P
                            mm = nc.tensor.matmul(dst[:, (j + 1) * P:SEQ], vt_, w[:, REST[j]:REST[j] + n], start=False,
                                                  stop=True, skip_group_check=True)
                    mm.then_inc(o_done, 1)

                def heads4(i, last):
                    for hd in range(4):
                        sums(hd, i * 4 + hd)
                        if not (last and hd >= 2):
                            scores(i * 2 + (hd + 2) // 2, (hd + 2) % 4, i * 4 + (hd + 2))
                        mix(hd, i * 4 + hd, i * 2 + hd // 2)

                scores(0, 0, 0)
                scores(0, 1, 1)
                with pe.Fori(0, HEADS // 4 - 1) as i:
                    heads4(i, False)
                heads4(HEADS // 4 - 1, True)

            def even_tables():
                pe.wait_ge(evac_done, ST["ev_v"].evac1)
                pe.wait_ge(s4_ready, 3)
                nc.tensor.matmul(bank[4][:, 0:P], resid4[:, 0, :], resid4[:, 0, :], start=True, stop=False)
                nc.tensor.matmul(bank[4][:, 0:P], resid4[:, 1, :], resid4[:, 1, :], start=False, stop=True).then_inc(tab_done, 1)
                pe.wait_ge(ld_even, 4 * 16)
                for g in range(8):
                    mm = nc.tensor.transpose(bank[5 + g // 4][:, (g % 4) * P:(g % 4 + 1) * P], ws_st[:, g, :], ident[:, :])
                    if g % 4 == 3:
                        mm.then_inc(ws_tr, 1)

            def gated_mlp():
                pe.wait_ge(ws_ready, 8)
                pe.wait_ge(vn_ready, TT)
                for c in range(4):
                    if c >= 2:
                        pe.wait_ge(gm_copied, c - 1)
                    for gi in range(2):
                        g = 2 * c + gi
                        dst = bank[5 + c % 2][gi * 64:gi * 64 + 64, :]
                        nc.tensor.matmul(dst, ones[0:1, 0:64], bs_st[0:1, g:g + 1, :].to_broadcast([1, TT, P]), start=True,
                                         stop=False, skip_group_check=True)
                        for n in range(TT):
                            mm = nc.tensor.matmul(dst[:, n * P:(n + 1) * P], gv_t[:, n, g * 64:(g + 1) * 64], ws_t[:, g, :],
                                                  start=False, stop=True, skip_group_check=True)
                    mm.then_inc(gm_done, 1)
                pe.wait_ge(evac_done, ST["ev_qk"].evac1)
                for c in range(8):
                    pe.wait_ge(qk_sq, c + 1)
                    if c >= 4:
                        pe.wait_ge(qk_ln, c - 3)
                    nc.tensor.matmul(bank[c % 4], head_mean[:, :], sq_even[:, c % 2, :], start=True,
                                     stop=True).then_inc(qk_ms, 1)

            def dilated_attention():
                pe.wait_ge(gm_copied, 4)
                pe.wait_ge(tables, 1)
                pe.wait_ge(evac_done, ST["ev_vb"].evac1)

                def scores(hd, h, pair):
                    pe.wait_ge(qn_ready, pair + 1)
                    half = slice((hd % 2) * 64, (hd % 2) * 64 + 64)
                    for n in range(TT):
                        pe.wait_ge(sm_done, h * 4 + (n + 1))
                        nc.tensor.matmul(bank[n][:, 0:(n + 1) * P], qn_pair[half, hd // 2, n * P:(n + 1) * P],
                                         kn_pair[half, hd // 2, 0:(n + 1) * P], start=True, stop=True).then_inc(sc_done, 1)

                def turn(hd, h):
                    pe.wait_ge(pt_copied, h + 1)
                    flat = psum[:, 4:7, :].rearrange("p b n -> p (b n)")
                    for n in range(TT):
                        pe.wait_ge(pn_done, h * 4 + (n + 1))
                        for j in range(n + 1):
                            to = PT_AT[j] + (n - j) * P
                            mm = nc.tensor.transpose(flat[:, to:to + P], prob[:, hd % 2, ROW_AT[n] + j * P:ROW_AT[n] + (j + 1) * P],
                                                     ident[:, :])
                    mm.then_inc(tr_p, 1)

                def mix(hd, h, pair):
                    pe.wait_ge(pt_copied, h + 2)
                    pe.wait_ge(vb_staged, pair + 1)
                    if hd % 2 == 0:
                        pe.wait_ge(b_ready, pair + 1)
                    half = (hd % 2) * 64
                    for j in range(TT):
                        mm = nc.tensor.matmul(bank[7][half:half + 64, j * P:SEQ], vb_pair[:, hd // 2, j, half:half + 64],
                                              prob_t[:, PT_AT[j]:PT_AT[j] + SEQ - j * P], start=(j == 0), stop=(j == TT - 1))
                    mm.then_inc(pv_done, 1)

                def heads4(i, last):
                    for hd in range(4):
                        turn(hd, i * 4 + hd)
                        if not (last and hd >= 2):
                            scores((hd + 2) % 4, i * 4 + (hd + 2), i * 2 + (hd + 2) // 2)
                        mix(hd, i * 4 + hd, i * 2 + hd // 2)

                scores(0, 0, 0)
                scores(1, 1, 0)
                with pe.Fori(0, HEADS_B // 4 - 1) as i:
                    heads4(i, False)
                heads4(HEADS_B // 4 - 1, True)

            def gate_low():
                pe.wait_ge(wga_ready, 1)
                for k in range(DC):
                    nc.tensor.matmul(bank[4], wga_hi[:, k, :], xhi[:, k, :], start=(k == 0), stop=False)
                    nc.tensor.matmul(bank[4], wga_hi[:, k, :], xlo[:, k, :], start=False, stop=False)
                    mm = nc.tensor.matmul(bank[4], wga_lo[:, k, :], xhi[:, k, :], start=False, stop=(k == DC - 1))
                mm.then_inc(ga_done, 1)

            def gate_up():
                pe.wait_ge(ga_copied, 1)
                for h in range(GLA_HEADS):
                    nc.tensor.matmul(bank[4 + h], wa2[:, h * P:(h + 1) * P], ga_t[0:GATE_RANK, :], start=True,
                                     stop=True).then_inc(la_done, 1)

            def linear_attention():
                pe.wait_ge(evac_done, ST["od_r"].evac1)
                pe.wait_ge(gq_done, 1)
                pe.wait_ge(gkt_done, 1)
                for h in range(GLA_HEADS):
                    for n in range(TT):
                        mm = nc.tensor.matmul(bank[4 + h][:, n * P:(n + 1) * P], gkt[:, h, n * P:(n + 1) * P],
                                              gq[:, h, n * P:(n + 1) * P], start=True, stop=True)
                    mm.then_inc(at_done, 1)
                pe.wait_ge(gks_done, 1)
                for n in range(TT):
                    for h in range(GLA_HEADS):
                        mm = nc.tensor.transpose(bank[n][:, h * P:(h + 1) * P], gks[:, h, n * P:(n + 1) * P], ident[:, :])
                    mm.then_inc(tr_k, 1)
                pe.wait_ge(kt_copied, TT)
                pe.wait_ge(at_ready, GLA_HEADS)

                def chunk_products(h):
                    if h > 0:
                        pe.wait_ge(st_ready, h * GLA_CHUNKS)
                    for hf in range(2):
                        rows = slice(hf * 64, hf * 64 + 64)
                        for m in range(2):
                            for a in range(2):
                                n = 4 * m + 2 * a + hf
                                if n < GLA_CHUNKS - 1:
                                    mm = nc.tensor.matmul(bank[2 * hf + m][:, a * GLA_DV:(a + 1) * GLA_DV], gks_t[rows, n // 2, h, :],
                                                          gvt[rows, n // 2, h * GLA_DV:(h + 1) * GLA_DV], start=True, stop=True)
                    mm.then_inc(kv_done, 1)

                def outputs(h):
                    pe.wait_ge(st_ready, (h + 1) * GLA_CHUNKS)
                    if h >= 2:
                        pe.wait_ge(go_link, 2 * (h - 2) + 1)
                    for dv in range(2):
                        dst = bank[4 + 2 * (h % 2) + dv]
                        if h >= 2:
                            pe.wait_ge(go_copied, 2 * (h - 2) + dv + 1)
                        cols = slice(h * GLA_DV + dv * P, h * GLA_DV + (dv + 1) * P)
                        for n in range(TT):
                            nc.tensor.matmul(dst[:, n * P:(n + 1) * P], gvt[:, n, cols], attn_t[:, h, n, :], start=(n == 0),
                                             stop=False, skip_group_check=True)
                        for n in range(GLA_CHUNKS):
                            to = slice(n * GLA_CHUNK, (n + 1) * GLA_CHUNK)
                            mm = nc.tensor.matmul(dst[:, to], gst[:, h % 2, n, dv * P:(dv + 1) * P], gq[:, h, to],
                                                  start=False, stop=(n == GLA_CHUNKS - 1), skip_group_check=True)
                        mm.then_inc(go_done, 1)

                def mean_square_head(h):
                    for dv in range(2):
                        pe.wait_ge(go_sq, 2 * h + dv + 1)
                        mm = nc.tensor.matmul(bank[4 + 2 * (h % 2)], ones[:, :], sq_odd[:, dv, :], start=(dv == 0), stop=(dv == 1))
                    mm.then_inc(go_ms, 1)

                chunk_products(0)
                for h in range(GLA_HEADS):
                    if h < GLA_HEADS - 1:
                        chunk_products(h + 1)
                    if h > 0:
                        mean_square_head(h - 1)
                    outputs(h)
                mean_square_head(GLA_HEADS - 1)

            for name in run:
                if name == "glu":
                    feature_stage(name, hhi, hlo, lambda k: (hid_ready, (k % 4) * 2 + k // 4 + 1))
                elif name == "ssm_out":
                    feature_stage(name, hhi[:, DC:2 * DC, :], hlo[:, DC:2 * DC, :], lambda k: (hid_ready, DC + k + 1), 0)
                    norm(0)
                elif name == "gu0":
                    feature_stage(name, xhi, xlo, lambda k: (x_ready, 1 * DC + k + 1))
                elif name == "down0":
                    down_stage(name, 1)
                    norm(1)
                elif name == "q":
                    feature_stage(name, xhi, xlo, lambda k: (x_ready, 2 * DC + k + 1))
                elif name == "k":
                    feature_stage(name, xhi, xlo, lambda k: (x_ready, 2 * DC + k + 1))
                elif name == "v":
                    token_stage(name, xhi, xlo)
                    stick_attention()
                elif name == "w_o":
                    feature_stage(name, hhi, hlo, lambda k: (o_ready, k + 2), 2)
                    norm(2)
                elif name == "gu1":
                    feature_stage(name, xhi, xlo, lambda k: (x_ready, 3 * DC + k + 1))
                elif name == "down1":
                    down_stage(name, 3)
                    norm(3)
                    norm(4)
                elif name == "ev_u":
                    feature_stage(name, xhi, xlo, lambda k: (x_ready, 4 * DC + k + 1))
                elif name == "ev_v":
                    token_stage(name, xhi, xlo)
                    even_tables()
                elif name == "ev_qk":
                    feature_stage(name, xhi, xlo, lambda k: (x_ready, 4 * DC + k + 1))
                    gated_mlp()
                elif name == "ev_vb":
                    pe.wait_ge(qk_ln, 8)
                    pe.wait_ge(gm_copied, 4)
                    token_stage(name, xhi, xlo)
                    dilated_attention()
                elif name == "ev_out":
                    feature_stage(name, xhi, xlo, lambda k: (gm_ready, k + 1) if k < 4 else (b_ready, k - 4 + 2))
                    norm(5)
                elif name in ("conv0", "conv1"):
                    chunks0 = (5 if name == "conv0" else 7) * DC
                    feature_stage(name, xhi, xlo, lambda k: (x_ready, chunks0 + k + 1))
                elif name in ("cdown0", "cdown1"):
                    down_stage(name)
                    if name == "cdown0":
                        norm(6)
                    else:
                        pe.wait_ge(evac_done, ST[name].evac1)
                        for n in range(TT):
                            for c in range(DC):
                                mm = nc.tensor.transpose(bank[2 * n + c // 4][:, (c % 4) * P:(c % 4 + 1) * P],
                                                         res[:, c, n * P:(n + 1) * P], ident[:, :])
                                if c % 4 == 3:
                                    mm.then_inc(tr_out, 1)
                elif name == "od_q":
                    feature_stage(name, xhi, xlo, lambda k: (x_ready, 6 * DC + k + 1))
                    gate_low()
                elif name == "od_k":
                    feature_stage(name, xhi, xlo, lambda k: (x_ready, 6 * DC + k + 1))
                    gate_up()
                elif name == "od_v":
                    pe.wait_ge(la_lin, GLA_HEADS)
                    token_stage(name, xhi, xlo)
                elif name == "od_r":
                    feature_stage(name, xhi, xlo, lambda k: (x_ready, 6 * DC + k + 1))
                    linear_attention()
                elif name == "od_out":
                    feature_stage(name, xhi, xlo, lambda k: (go_ready, k + 1))
                    norm(7)

        @block.scalar
        def _(act):
            act.wait_ge(tr_c, 4)
            for ri in range(2):
                for n in range(8):
                    src = bank[3 + 2 * ri + n // 4][:, (n % 4) * P:(n % 4 + 1) * P].rearrange(
                        "p (j g h) -> p j g h", g=2, h=GH)
                    for gi in range(2):
                        half = slice(gi * 64, gi * 64 + 64)
                        ins = nc.scalar.copy(ct[half, ri, n * 4:(n + 1) * 4, :], src[half, :, gi, :])
                    ins.then_inc(c_copied, 1)
            act.wait_ge(tr_prm, 1)
            nc.scalar.copy(prm[:, :], bank[7][:, 0:small0 + SROW]).then_inc(prm_copied, 1)
            act.wait_ge(trig_in, 1)
            nc.scalar.activation(sp_[:, 8, :], sp_[:, 6, :], ACT.Sin).then_inc(trig_out, 1)
            nc.scalar.activation(sp_[:, 9, :], sp_[:, 7, :], ACT.Sin).then_inc(trig_out, 1)
            for b in range(8):
                act.wait_ge(tr_u, b + 1)
                nc.scalar.copy(uu[:, b * 8:(b + 1) * 8, :],
                               bank[b][:, :].rearrange("p (g c) -> p g c", g=8)).then_inc(u_copied, 1)
            def x_high(f):
                act.wait_ge(tr_x, f + 1)
                nc.scalar.copy(xhi[:, f, :].rearrange("p (c s) -> p s c", s=TAU),
                               bank[f][:, :].rearrange("p (s c) -> p s c", s=TAU)).then_inc(xhi_done, 1)

            for f in range(DC):
                x_high(f)

            def copy_states(n):
                act.wait_ge(s_in, n + 1)
                src = bank[4 + n % 2][:, :].rearrange("p (j r c) -> p r c j", j=4, r=2)
                dst = states[:, 1:NCH + 1, :, n * 4:(n + 1) * 4].rearrange("p c r j -> p r c j")
                nc.scalar.copy(dst, src).then_inc(s_copied, 1)

            for n in range(8):
                if n >= 2:
                    act.wait_ge(s_in, n - 1)
                for ri in range(2):
                    act.wait_ge(tr_v, 2 * n + ri + 4)
                    nc.scalar.copy(vt[n % 2][:, ri, :, :],
                                   bank[2 * (n % 2) + ri][:, :].rearrange("p (j n) -> p j n", j=4)).then_inc(vt_copied, 1)
                if n > 0:
                    copy_states(n - 1)
            copy_states(7)
            for b in range(4):
                act.wait_ge(k_done, b + 1)
                if b == 2:
                    act.wait_ge(w_ready, 8)
                nc.scalar.copy(k_rows[:, b * 4:(b + 1) * 4, :],
                               bank[4 + b][:, :].rearrange("p (g n) -> p g n", g=4)).then_inc(k_copied, 1)
            nc.scalar.preload_act_table(ACT.Gelu_apprx_tanh)

            def gelu(n):
                act.wait_ge(tr_y, n + 1)
                if n >= 4:
                    act.wait_ge(hid_ready, n - 3)
                nc.scalar.activation(y_gelu[:, n % 4, :].rearrange("p (c s) -> p s c", s=TAU),
                                     bank[n][:, :].rearrange("p (s c) -> p s c", s=TAU),
                                     ACT.Gelu_apprx_tanh).then_inc(gelu_done, 1)

            def split(it, half, wait_parts):
                act.wait_ge(w_landed[half], it * 16 + 16)
                if wait_parts is not None:
                    act.wait_ge(part_done, wait_parts)
                nc.scalar.copy(whi[:, half, :], wst[:, half, :]).then_inc(whi_done, 1)

            def stage_loop(name, body):
                st = ST[name]
                last = name == run[-1]
                def split_next(i):
                    def do(half):
                        split(i + (st.it0 + 1), half, i * st.parts + (st.part0 + st.parts // 2 * (half + 1)))
                    return do
                if st.iters > last:
                    with act.Fori(0, st.iters - last) as i:
                        body(i, split_next(i))
                if last:
                    body(st.iters - 1, lambda half: None)

            def gate_stage(name, func):
                st = ST[name]
                def body(i, split_next):
                    split_next(0)
                    for u in range(2):
                        act.wait_ge(part_done, i * 4 + (st.part0 + u + 1))
                        act.wait_ge(evac_done, i * 2 + (st.evac0 + u - 1))
                        nc.scalar.activation(tmp_a[:, u, :], bank[u][:, :], func).then_inc(act_out, 1)
                    split_next(1)
                stage_loop(name, body)

            def split_stage(name):
                def body(i, split_next):
                    split_next(0)
                    split_next(1)
                stage_loop(name, body)

            def split_stage_held(name):
                st = ST[name]
                parts = st.parts // 2
                with act.Fori(0, st.iters - 1) as i:
                    for half in range(2):
                        split(i + (st.it0 + 1), half, i * st.parts + (st.part0 + parts * (half + 1)))
                split(st.it0 + st.iters, 0, st.part1 - parts)

            def layer_norm(n, affine):
                act.wait_ge(ln_sums, 2 * n + 1)
                nc.scalar.activation(mean_sq, bank[5], ACT.Square).then_inc(ln_m2, 1)
                nc.scalar.copy(mean, bank[5]).then_inc(ln_m2, 1)
                act.wait_ge(ln_var, n + 1)
                nc.scalar.activation(rstd_ln, variance, ACT.Ln, bias=eps_ln[:, 0:1]).then_inc(act_link, 1)
                act.wait_ge(act_link, 2 * n + 1)
                nc.scalar.activation(rstd_ln, rstd_ln, ACT.Exp, scale=-0.5).then_inc(act_link, 1)
                for c in range(DC + 1):
                    if c < DC:
                        act.wait_ge(ln_n, n * DC + c + 1)
                        g, b = (prm[:, col + c:col + c + 1] for col in affine)
                        if n < 3:
                            nc.scalar.activation(xhi[:, c, :], res[:, c, :], ACT.Identity, bias=b, scale=g).then_inc(ln_hi, 1)
                        nc.scalar.activation(res[:, c, :], res[:, c, :], ACT.Identity, bias=b, scale=g).then_inc(ln_a, 1)
                    if n == 3 and c > 0:
                        act.wait_ge(ln_a, n * DC + c)
                        if c > 2:
                            act.wait_ge(ln_sq_used, c - 2)
                        nc.scalar.activation(sq[:, (c - 1) % 2, :], res[:, c - 1, :], ACT.Square).then_inc(ln_sq, 1)

            def rms_norm(n):
                if n > 4:
                    m = sq_count(n)
                    act.wait_ge(evac_done, chunk_done(n, DC - 1))
                    act.wait_ge(ln_sq_used, m)
                    nc.scalar.activation(sq[:, 0, :], res[:, DC - 1, :], ACT.Square).then_inc(ln_sq, 1)
                act.wait_ge(ln_sq_used, sq_count(n + 1))
                nc.scalar.activation(rstd, bank[5], ACT.Ln, bias=eps_rms[:, 0:1]).then_inc(act_link, 1)
                act.wait_ge(act_link, 2 * n + 1)
                nc.scalar.activation(rstd, rstd, ACT.Exp, scale=-0.5).then_inc(act_link, 1)
                for c in range(DC):
                    act.wait_ge(rms_t, (n - 4) * DC + c + 1)
                    nc.scalar.copy(xhi[:, c, :], tmp_c[:, c % 2, :]).then_inc(ln_hi, 1)
                    if n > 4 and c == 2:
                        st = ST[norm_stage[n]]
                        split(st.it0 + st.iters, 1, st.part1)

            def stick_attention():
                def soft(hd, h):
                    act.wait_ge(z_done, h + 1)
                    act.wait_ge(o_done, h)
                    z = psum[:, 0:3, :].rearrange("p b n -> p (b n)")[:, 0:STICK]
                    nc.scalar.copy(keep[:, hd % 2, :], z).then_inc(z_copied, 1)
                    act.wait_ge(z_copied, h + 2)
                    act.wait_ge(lb_done, h + 1)
                    nc.scalar.activation(lnp[:, :], keep[:, hd % 2, :], ACT.Abs).then_inc(soft_link, 1)
                    act.wait_ge(soft_link, h * 2 + 1)
                    nc.scalar.activation(lnp[:, :], lnp[:, :], ACT.Exp, scale=-1.0).then_inc(soft_link, 1)
                    act.wait_ge(soft_link, h * 2 + 2)
                    nc.scalar.activation(lnp[:, :], lnp[:, :], ACT.Ln, bias=one_col[:, 0:1]).then_inc(ln_part, 1)

                def weigh(hd, h):
                    act.wait_ge(lw_done, h + 2)
                    nc.scalar.activation(keep[:, hd % 2, :], keep[:, hd % 2, :], ACT.Exp).then_inc(w_done, 1)

                def heads4(i, last):
                    for hd in range(4):
                        if not (last and hd == 3):
                            soft((hd + 1) % 4, i * 4 + (hd + 1))
                        weigh(hd, i * 4 + hd)

                nc.scalar.preload_act_table_set(LN_EXP)
                soft(0, 0)
                with act.Fori(0, HEADS // 4 - 1) as i:
                    heads4(i, False)
                heads4(HEADS // 4 - 1, True)

            def feature_stage(name, func, dst):
                st = ST[name]
                def body(i, split_next):
                    for half in range(2):
                        for u in range(2):
                            n = 2 * half + u
                            act.wait_ge(part_done, i * 4 + (st.part0 + n + 1))
                            nc.scalar.activation(dst[:, bass.ds(i * 4 + n, 1), :], bank[n].unsqueeze(1), func).then_inc(evac_done, 1)
                        split_next(half)
                stage_loop(name, body)

            def token_stage(name, func, dst):
                st = ST[name]
                def body(i, split_next):
                    for half in range(2):
                        for n in range(TT):
                            act.wait_ge(part_done, i * 8 + (st.part0 + 4 * half + n + 1))
                            nc.scalar.activation(dst[:, n, bass.ds(i * 512 + half * 256, 256)], bank[4 * half + n][:, 0:256],
                                                 func).then_inc(evac_done, 1)
                        split_next(half)
                stage_loop(name, body)

            def conv_stage(name):
                st = ST[name]
                layer = int(name[-1])
                def body(i, split_next):
                    split_next(0)
                    for u in range(2):
                        act.wait_ge(part_done, i * 4 + (st.part0 + u + 1))
                        act.wait_ge(evac_done, i * 2 + (st.evac0 + u - 1))
                        nc.scalar.activation(tmp_a[:, u, :], bank[u], ACT.Identity, bias=tap(layer, TAPS, i * 2 + u),
                                             scale=tap(layer, TAPS - 1, i * 2 + u)).then_inc(conv_a, 1)
                    for u in range(2):
                        act.wait_ge(conv_b, i * 2 + (st.evac1 - st.evac0) * layer + (u + 1))
                        nc.scalar.activation(tmp_a[:, u, :], tmp_a[:, u, :], ACT.Silu).then_inc(act_out, 1)
                    split_next(1)
                stage_loop(name, body)

            def even_tables():
                for n in range(2):
                    act.wait_ge(ws_tr, n + 1)
                    nc.scalar.copy(ws_t[:, 4 * n:4 * n + 4, :], bank[5 + n].rearrange("p (g s) -> p g s", g=4)).then_inc(ws_copied, 1)
                act.wait_ge(gv_var, 1)
                nc.scalar.activation(gv_rs, gv_mv[:, :, 1], ACT.Ln, bias=eps_rms[:, 0:1]).then_inc(gv_link, 1)
                act.wait_ge(gv_link, 1)
                nc.scalar.activation(gv_rs, gv_rs, ACT.Exp, scale=-0.5).then_inc(gv_rstd, 1)

            def head_norms():
                act.wait_ge(evac_done, ST["ev_qk"].evac1)
                for c in range(9):
                    if c < 8:
                        if c >= 2:
                            act.wait_ge(qk_ms, c - 1)
                        nc.scalar.activation(sq_even[:, c % 2, :], qk_f[:, c, :], ACT.Square).then_inc(qk_sq, 1)
                    if c >= 1:
                        act.wait_ge(qk_ms, c)
                        nc.scalar.activation(qk_rs[:, c - 1, :], bank[(c - 1) % 4], ACT.Ln,
                                             bias=eps_rms[:, 0:1]).then_inc(qk_ln, 1)
                act.wait_ge(qk_ln, 8)
                nc.scalar.activation(qk_rs[:, :, :], qk_rs[:, :, :], ACT.Exp, scale=-0.5).then_inc(qk_rstd, 1)

            def dilated_attention():
                def expo(hd, h):
                    for n in range(TT):
                        act.wait_ge(mx_done, h * 4 + (n + 1))
                        row = prob[:, hd % 2, ROW_AT[n]:ROW_AT[n] + (n + 1) * P]
                        nc.scalar.activation(row, row, ACT.Exp, bias=neg_max[:, hd % 2, n:n + 1],
                                             accum_out=den[:, hd % 2, n:n + 1]).then_inc(pexp, 1)

                def normalise(hd, h):
                    act.wait_ge(den_done, h + 1)
                    for n in range(TT):
                        row = prob[:, hd % 2, ROW_AT[n]:ROW_AT[n] + (n + 1) * P]
                        nc.scalar.activation(row, row, ACT.Copy, scale=rden[:, hd % 2, n:n + 1]).then_inc(pn_done, 1)

                def copy_turned(h):
                    act.wait_ge(tr_p, h + 1)
                    act.wait_ge(pv_done, h + 1)
                    nc.scalar.copy(prob_t[:, :], psum[:, 4:7, :].rearrange("p b n -> p (b n)")[:, 0:STICK]).then_inc(pt_copied, 1)

                def heads4(i, last):
                    for hd in range(4):
                        copy_turned(i * 4 + hd)
                        if not (last and hd == 3):
                            normalise((hd + 1) % 4, i * 4 + (hd + 1))
                        if not (last and hd >= 2):
                            expo((hd + 2) % 4, i * 4 + (hd + 2))

                expo(0, 0)
                expo(1, 1)
                normalise(0, 0)
                with act.Fori(0, HEADS_B // 4 - 1) as i:
                    heads4(i, False)
                heads4(HEADS_B // 4 - 1, True)

            def log_decay():
                for h in range(GLA_HEADS):
                    act.wait_ge(la_done, h + 1)
                    nc.scalar.activation(la[:, h, :], bank[4 + h], ACT.Identity, bias=gate_bias[:, h:h + 1]).then_inc(la_lin, 1)
                act.wait_ge(la_lin, GLA_HEADS)
                nc.scalar.activation(ge[:, :, :], la[:, :, :], ACT.Abs).then_inc(la_link, 1)
                act.wait_ge(la_link, 1)
                nc.scalar.activation(ge[:, :, :], ge[:, :, :], ACT.Exp, scale=-1.0).then_inc(la_link, 1)
                act.wait_ge(la_link, 2)
                nc.scalar.activation(ge[:, :, :], ge[:, :, :], ACT.Ln, bias=one_col[:, 0:1]).then_inc(ln_a1, 1)

            def decays():
                act.wait_ge(cum_done, GLA_HEADS)
                nc.scalar.activation(ge[:, :, :], cum[:, :, :], ACT.Exp, scale=1.0 / GLA_TAU).then_inc(ek_done, 1)
                nc.scalar.activation(gkt[:, :, :], cum[:, :, :], ACT.Exp, scale=-1.0 / GLA_TAU).then_inc(en_done, 1)
                act.wait_ge(last_done, 1)
                nc.scalar.activation(gks[:, :, :], gks[:, :, :], ACT.Exp, scale=1.0 / GLA_TAU).then_inc(es_done, 1)

            def linear_attention():
                for n in range(TT):
                    act.wait_ge(tr_k, n + 1)
                    nc.scalar.copy(gks_t[:, n, :, :], bank[n].rearrange("p (h d) -> p h d", h=GLA_HEADS)).then_inc(kt_copied, 1)

                def rstd_head(h):
                    act.wait_ge(go_ms, h + 1)
                    if h >= 2:
                        act.wait_ge(go_hi, 2 * h - 2)
                    nc.scalar.activation(o_rs[:, h % 2, :], bank[4 + 2 * (h % 2)], ACT.Ln, bias=eps_rms[:, 0:1],
                                         scale=1.0 / GLA_DV).then_inc(go_link, 1)
                    act.wait_ge(go_link, 2 * h + 1)
                    nc.scalar.activation(o_rs[:, h % 2, :], o_rs[:, h % 2, :], ACT.Exp, scale=-0.5).then_inc(go_link, 1)

                for h in range(GLA_HEADS):
                    for dv in range(2):
                        m = 2 * h + dv
                        act.wait_ge(go_done, m + 1)
                        nc.scalar.copy(go[:, m, :], bank[4 + m % 4]).then_inc(go_copied, 1)
                    for dv in range(2):
                        m = 2 * h + dv
                        if h > 0:
                            act.wait_ge(go_ms, h)
                        act.wait_ge(go_copied, m + 1)
                        nc.scalar.activation(sq_odd[:, dv, :], go[:, m, :], ACT.Square).then_inc(go_sq, 1)
                    if h > 0:
                        rstd_head(h - 1)
                rstd_head(GLA_HEADS - 1)

            LN_EXP = "natural_log_exp_and_others"
            for n in range(4):
                gelu(n)
            act.wait_ge(y_done, 8)
            split(0, 0, None)
            for n in range(4, DC):
                gelu(n)
            split(0, 1, None)
            nc.scalar.preload_act_table(ACT.Sigmoid)
            for name in run:
                if name == "glu":
                    gate_stage(name, ACT.Sigmoid)
                elif name == "ssm_out":
                    nc.scalar.preload_act_table_set(LN_EXP)
                    split_stage(name)
                    layer_norm(0, (0, 16))
                elif name == "gu0":
                    nc.scalar.preload_act_table(ACT.Silu)
                    gate_stage(name, ACT.Silu)
                elif name == "down0":
                    nc.scalar.preload_act_table_set(LN_EXP)
                    split_stage(name)
                    layer_norm(1, (32, 48))
                elif name in ("q", "k"):
                    split_stage(name)
                elif name == "v":
                    split_stage(name)
                    stick_attention()
                elif name == "w_o":
                    nc.scalar.preload_act_table_set(LN_EXP)
                    split_stage(name)
                    layer_norm(2, (8, 24))
                elif name == "gu1":
                    nc.scalar.preload_act_table(ACT.Silu)
                    gate_stage(name, ACT.Silu)
                elif name == "down1":
                    nc.scalar.preload_act_table_set(LN_EXP)
                    split_stage(name)
                    layer_norm(3, (40, 56))
                    rms_norm(4)
                elif name == "ev_u":
                    nc.scalar.preload_act_table(ACT.Gelu)
                    feature_stage(name, ACT.Gelu, u_f)
                elif name == "ev_v":
                    token_stage(name, ACT.Gelu, gv_t)
                    nc.scalar.preload_act_table_set(LN_EXP)
                    even_tables()
                elif name == "ev_qk":
                    split_stage(name)
                    head_norms()
                elif name == "od_q":
                    split_stage(name)
                    act.wait_ge(ga_done, 1)
                    nc.scalar.copy(ga_t[:, :], bank[4]).then_inc(ga_copied, 1)
                elif name == "od_k":
                    split_stage(name)
                    log_decay()
                elif name == "od_v":
                    split_stage(name)
                    decays()
                elif name == "ev_vb":
                    split_stage(name)
                    dilated_attention()
                elif name == "ev_out":
                    nc.scalar.preload_act_table_set(LN_EXP)
                    split_stage_held(name)
                    rms_norm(5)
                elif name in ("conv0", "conv1"):
                    nc.scalar.preload_act_table(ACT.Silu)
                    conv_stage(name)
                elif name in ("cdown0", "cdown1"):
                    if name == "cdown0":
                        nc.scalar.preload_act_table_set(LN_EXP)
                        split_stage_held(name)
                        rms_norm(6)
                    else:
                        split_stage(name)
                        for n in range(2 * TT):
                            if n % 2 == 0:
                                continue
                            act.wait_ge(tr_out, n + 1)
                            nc.scalar.copy(out_t[:, n // 2, 512:1024], bank[n]).then_inc(go_link, 1)
                elif name == "od_r":
                    nc.scalar.preload_act_table(ACT.Silu)
                    feature_stage(name, ACT.Silu, gr)
                    nc.scalar.preload_act_table_set(LN_EXP)
                    linear_attention()
                elif name == "od_out":
                    nc.scalar.preload_act_table_set(LN_EXP)
                    split_stage_held(name)
                    rms_norm(7)

        @block.vector
        def _(dve):
            link = linker(dve, dve_link)
            V = nc.vector
            V.memset(ones_mean[:, :], 1.0 / D)
            V.memset(ones[:, :], 1.0)
            V.memset(eps_ln[:, :], LN_EPS)
            V.memset(eps_rms[:, :], RMS_EPS)
            for half in range(2):
                rows, other = slice(half * 64, half * 64 + 64), slice(64 - half * 64, 128 - half * 64)
                V.memset(head_mean[rows, rows], 1.0 / HD)
                V.memset(head_mean[rows, other], 0.0)
                V.memset(chunk_mask[rows, rows], 1.0)
                V.memset(chunk_mask[rows, other], 0.0)
            V.memset(one_col[:, :], 1.0).then_inc(mask_ones, 1)
            V.memset(marks[:, 0:1], 0.0).then_inc(evac_done, 4)
            for n, primed in enumerate((lw_done, o_ready, vt_copied, pt_copied, b_ready, lb_done, pv_done, o_done, tr_v, sc_done, z_copied)):
                V.memset(marks[:, n + 1:n + 2], 0.0).then_inc(primed, 3 if primed is tr_v else 1)
            dve.wait_ge(consts, 2)
            V.tensor_copy(ident_r[:, :], ident[:, :])
            V.tensor_scalar(not_past[:, :], after[:, :], -1.0, 2.0 ** 100, ALU.add, ALU.mult).then_inc(mask_rounded, 1)
            dve.wait_ge(ld_a, 48)
            V.tensor_copy(a_st[:, 2, :].rearrange("j (g p) -> j g p", g=2),
                          dt_st[:, :].unsqueeze(2).to_broadcast([PAIRS, 2, GP])).then_inc(a_rows, 1)
            dve.wait_ge(ld_x, 32)
            V.tensor_copy(x_perm[:, :, :, :], xnat[:, :, :].rearrange("p s (g h) -> p g s h", h=GH)).then_inc(x_permuted, 1)
            dve.wait_ge(tr_a, 1)
            link(V.tensor_copy(sp_[:, 0:3, :], bank[0][:, 0:3 * PAIRS].rearrange("p (n j) -> p n j", n=3)))

            def s(n):
                return sp_[:, n, :]

            def tt(o, a, b, op):
                link(V.tensor_tensor(o, a, b, op))

            def ts(o, a, c1, c2, op0, op1):
                link(V.tensor_scalar(o, a, c1, c2, op0, op1))

            def stt(o, a, c, b, op0, op1):
                link(V.scalar_tensor_tensor(o, a, c, b, op0, op1))

            def exp_(o, x):
                ts(s(12), x, -87.0, 88.0, ALU.max, ALU.min)
                ts(s(13), s(12), 1.4426950408889634, ROUND, ALU.mult, ALU.add)
                ts(s(13), s(13), -ROUND, 0.0, ALU.add, ALU.add)
                stt(s(14), s(13), -LN2[0], s(12), ALU.mult, ALU.add)
                stt(s(14), s(13), -LN2[1], s(14), ALU.mult, ALU.add)
                ts(s(15), s(14), EXP_TAYLOR[-1], 0.0, ALU.mult, ALU.add)
                for coef in EXP_TAYLOR[-2::-1]:
                    stt(s(15), s(15), coef, s(14), ALU.add, ALU.mult)
                ts(ki[:, :], s(13), 127.0, 2.0 ** 23, ALU.add, ALU.mult)
                stt(o, s(15), 1.0, ki[:, :].bitcast(F32), ALU.add, ALU.mult)

            exp_(s(3), s(2))
            ts(s(4), s(0), -1e-4, 0.0, ALU.min, ALU.add)
            tt(s(10), s(4), s(3), ALU.mult)
            exp_(s(5), s(10))
            tt(s(10), s(1), s(3), ALU.mult)
            ts(s(11), s(10), 0.15915494309189535, ROUND, ALU.mult, ALU.add)
            ts(s(11), s(11), -ROUND, 0.0, ALU.add, ALU.add)
            for part in TWO_PI:
                stt(s(10), s(11), -part, s(10), ALU.mult, ALU.add)
            ts(s(6), s(10), -3.1415925, 3.1415925, ALU.max, ALU.min)
            ts(s(7), s(6), -1.0, 0.0, ALU.mult, ALU.add)
            tt(s(7), s(7), s(6), ALU.max)
            V.tensor_scalar(s(7), s(7), -1.0, 1.5707963267948966, ALU.mult, ALU.add).then_inc(trig_in, 1)
            dve.wait_ge(tr_b, 2)
            for ri in range(2):
                V.tensor_copy(bt[:, ri, :, :], bank[1 + ri][:, :].rearrange("p (h j) -> p h j", h=GH)).then_inc(b_copied, 1)
            dve.wait_ge(trig_out, 2)
            link(V.memset(lam[:, 0, 0, :], 1.0))
            link(V.memset(lam[:, 1, 0, :], 0.0))
            tt(lam[:, 0, 1, :], s(5), s(9), ALU.mult)
            tt(lam[:, 1, 1, :], s(5), s(8), ALU.mult)

            def cmul(o, a, b, tmp):
                V.tensor_tensor(o[0], a[0], b[0], ALU.mult)
                tt(tmp[0], a[1], b[1], ALU.mult)
                V.tensor_tensor(o[1], a[0], b[1], ALU.mult)
                tt(tmp[1], a[1], b[0], ALU.mult)
                tt(o[0], o[0], tmp[0], ALU.subtract)
                tt(o[1], o[1], tmp[1], ALU.add)

            def powers(k0, n):
                return [lam[:, ri, k0:k0 + n, :] for ri in range(2)]

            def power(k, n):
                return [lam[:, ri, k:k + 1, :].to_broadcast([P, n, PAIRS]) for ri in range(2)]

            for n in (1, 2, 4):
                cmul(powers(n + 1, n), powers(1, n), power(n, n), [l_tmp[:, ri, 0:n, :] for ri in range(2)])
            for k in range(TAU):
                V.tensor_copy(lam_rev[:, :, k, :], lam[:, :, TAU - 1 - k, :])
            V.tensor_copy(ll[:, 0, :, :], lam[:, 0, TAU:TAU + 1, :].to_broadcast([P, 2, PAIRS]))
            V.tensor_copy(ll[:, 1, 0, :], lam[:, 1, TAU, :])
            V.tensor_scalar(lam_neg[:, :, :, :], lam[:, :, :, :], -1.0, 0.0, ALU.mult, ALU.add)
            V.tensor_scalar(ll[:, 1, 1, :], lam[:, 1, TAU, :], -1.0, 0.0, ALU.mult, ALU.add).then_inc(lam_ready, 1)
            tt(s(12), s(4), s(4), ALU.mult)
            tt(s(13), s(1), s(1), ALU.mult)
            tt(s(12), s(12), s(13), ALU.add)
            link(V.reciprocal(s(12), s(12)))
            ts(s(13), lam[:, 0, 1, :], -1.0, 0.0, ALU.add, ALU.add)
            tt(s(14), s(13), s(4), ALU.mult)
            tt(s(15), lam[:, 1, 1, :], s(1), ALU.mult)
            tt(s(14), s(14), s(15), ALU.add)
            tt(s(16), s(14), s(12), ALU.mult)
            tt(s(14), lam[:, 1, 1, :], s(4), ALU.mult)
            tt(s(15), s(13), s(1), ALU.mult)
            tt(s(14), s(14), s(15), ALU.subtract)
            tt(s(17), s(14), s(12), ALU.mult)
            cmul([bb[:, ri, 0:GH, :] for ri in range(2)], [bt[:, ri, :, :] for ri in range(2)],
                 [s(16 + ri).unsqueeze(1).to_broadcast([P, GH, PAIRS]) for ri in range(2)],
                 [l_tmp[:, ri, :, :] for ri in range(2)])
            link(V.tensor_copy(bb[:, :, GH:2 * GH, :], bb[:, :, 0:GH, :]))
            for f in range(DC):
                dve.wait_ge(xhi_done, f + 1)
                V.tensor_tensor(xlo[:, f, :].rearrange("p (c s) -> p s c", s=TAU),
                                bank[f][:, :].rearrange("p (s c) -> p s c", s=TAU),
                                xhi[:, f, :].bitcast(F32).rearrange("p (c s) -> p s c", s=TAU),
                                ALU.subtract).then_inc(x_ready, 1)
            shape = [P, 4, TAU, GH]
            with dve.Fori(0, 4) as i:
                for buf in range(2):
                    n = i * 2 + buf
                    js = bass.ds(i * 8 + buf * 4, 4)
                    lv = [lam_rev[:, ri, :, js].rearrange("p k j -> p j k").unsqueeze(3).to_broadcast(shape)
                          for ri in range(2)]
                    bv = [bb[:, ri, 0:GH, js].rearrange("p h j -> p j h").unsqueeze(2).to_broadcast(shape) for ri in range(2)]
                    o = [v_buf[:, buf, ri, :, :].rearrange("p j (k h) -> p j k h", k=TAU) for ri in range(2)]
                    dve.wait_ge(tr_v, i * 4 + (buf * 2 + 1))
                    V.tensor_tensor(o[0], lv[0], bv[0], ALU.mult)
                    V.tensor_tensor(v_tmp[:, 0], lv[1], bv[1], ALU.mult)
                    V.tensor_tensor(o[1], lv[0], bv[1], ALU.mult)
                    V.tensor_tensor(v_tmp[:, 1], lv[1], bv[0], ALU.mult).then_inc(bb_ready, 1)
                    dve.wait_ge(bb_ready, n + 1)
                    V.tensor_tensor(o[0], o[0], v_tmp[:, 0], ALU.subtract)
                    V.tensor_tensor(o[1], o[1], v_tmp[:, 1], ALU.add).then_inc(v_ready, 1)
                    dve.wait_ge(v_ready, n + 1)
            def decay_power(t0, n):
                return [seg_pow[:, k, t0:t0 + n, 0, :] for k in range(2)]

            dve.wait_ge(tr_v, 17 + 2)
            link(V.tensor_copy(seg_pow[:, :, 0, 0, :], ll[:, :, 0, :]))
            for n in (1, 2, 4):
                cmul(decay_power(n, n), decay_power(0, n), [x.to_broadcast([P, n, PAIRS]) for x in decay_power(n - 1, 1)],
                     [l_tmp[:, ri, 0:n, :] for ri in range(2)])
            V.tensor_copy(seg_pow[:, 0, :, 1, :], seg_pow[:, 0, :, 0, :])
            link(V.tensor_scalar(seg_pow[:, 1, :, 1, :], seg_pow[:, 1, :, 0, :], -1.0, 0.0, ALU.mult, ALU.add))
            dve.wait_ge(s_copied, 8)
            scan = link
            scan(V.memset(states[:, 0, :, :], 0.0))

            def advance(to, of, power, n, m):
                flat = [P, n, m, 2 * PAIRS]
                prod = s_tmp[:, 0:n * m * 2 * PAIRS].rearrange("p (g t x) -> p g t x", g=n, t=m)
                for k in range(2):
                    scan(V.tensor_tensor(prod, power[k].to_broadcast(flat), of.to_broadcast(flat), ALU.mult))
                    if k == 0:
                        scan(V.tensor_tensor(to, to, prod, ALU.add))
                    else:
                        V.tensor_tensor(to[:, :, :, 0:PAIRS], to[:, :, :, 0:PAIRS], prod[:, :, :, PAIRS:], ALU.add)
                        scan(V.tensor_tensor(to[:, :, :, PAIRS:], to[:, :, :, PAIRS:], prod[:, :, :, 0:PAIRS], ALU.add))

            by_segment = states[:, 1:NCH + 1, :, :].rearrange("p (g t) r j -> p g t (r j)", g=SEGS)

            def power(t0, n):
                return [seg_pow[:, k, t0:t0 + n, :, :].rearrange("p t r j -> p t (r j)").unsqueeze(1) for k in range(2)]

            per = NCH // SEGS
            for t in range(1, per):
                advance(by_segment[:, :, t:t + 1, :], by_segment[:, :, t - 1:t, :], power(0, 1), SEGS, 1)
            for g in range(1, SEGS):
                advance(by_segment[:, g:g + 1, per - 1:per, :], by_segment[:, g - 1:g, per - 1:per, :], power(per - 1, 1), 1, 1)
            for g0, g1 in ((1, 5), (5, SEGS)):
                advance(by_segment[:, g0:g1, 0:per - 1, :], by_segment[:, g0 - 1:g1 - 1, per - 1:per, :], power(0, per - 1),
                        g1 - g0, per - 1)
            V.memset(marks[:, 11:12], 0.0).then_inc(scan_done, 1)
            dve.wait_ge(xd_ready, 1)

            def put_gelu(n):
                f = (n % 2) * 4 + n // 2
                dve.wait_ge(gelu_done, n + 1)
                V.tensor_copy(hhi[:, f, :], y_gelu[:, n % 4, :]).then_inc(zhi_done, 1)
                dve.wait_ge(zhi_done, n + 1)
                V.tensor_tensor(hlo[:, f, :], y_gelu[:, n % 4, :], hhi[:, f, :].bitcast(F32), ALU.subtract).then_inc(hid_ready, 1)

            for b in range(8):
                dve.wait_ge(y_done, b + 1)
                y = xnat[:, :, (b // 2) * P:(b // 2 + 1) * P].rearrange("p s (g h) -> p g s h", g=8)[:, b % 2::2, :, :]
                V.tensor_tensor(y, bank[b][:, :].rearrange("p (g s h) -> p g s h", g=4, s=TAU), y, ALU.add).then_inc(y_copied, 1)

            def split(it, half):
                dve.wait_ge(whi_done, it * 2 + half + 1)
                V.tensor_tensor(wlo[:, half, :], wst[:, half, :], whi[:, half, :].bitcast(F32),
                                ALU.subtract).then_inc(wlo_done, 1)

            for n in range(DC):
                put_gelu(n)
                if n == 3:
                    split(0, 0)
            split(0, 1)

            def stage_loop(name, body):
                st = ST[name]
                last = name == run[-1]
                def split_next(i):
                    return lambda half: split(i + (st.it0 + 1), half)
                if st.iters > last:
                    with dve.Fori(0, st.iters - last) as i:
                        body(i, split_next(i))
                if last:
                    body(st.iters - 1, lambda half: None)

            def put_hidden(src, m, count):
                V.tensor_copy(hhi[:, bass.ds(m, 1), :], src).then_inc(zhi_done, 1)
                dve.wait_ge(zhi_done, count)
                V.tensor_tensor(hlo[:, bass.ds(m, 1), :], src, hhi[:, bass.ds(m, 1), :].bitcast(F32),
                                ALU.subtract).then_inc(hid_ready, 1)

            def gate_stage(name, m0):
                st = ST[name]
                def body(i, split_next):
                    split_next(0)
                    for u in range(2):
                        dve.wait_ge(part_done, i * 4 + (st.part0 + u + 3))
                        dve.wait_ge(act_out, i * 2 + (st.pair0 - DC + u + 1))
                        V.tensor_tensor(tmp_b[:, u, :], bank[2 + u][:, :], tmp_a[:, u, :], ALU.mult).then_inc(evac_done, 1)
                        dve.wait_ge(evac_done, i * 2 + (st.evac0 + u + 1))
                        put_hidden(tmp_b[:, u:u + 1, :], i * 2 + (m0 + u), i * 2 + (st.pair0 + u + 1))
                    split_next(1)
                stage_loop(name, body)

            def residual(bank_, m, n):
                here = res[:, bass.ds(m, 1), :]
                if n is None or n > 4:
                    V.tensor_tensor(here, here, bank_.unsqueeze(1), ALU.add).then_inc(evac_done, 1)
                else:
                    V.scalar_tensor_tensor(here, here, ALPHA, bank_.unsqueeze(1), ALU.mult, ALU.add).then_inc(evac_done, 1)

            def square(n, c):
                if c < 4:
                    dve.wait_ge(ln_shifted, n * DC + c + 1)
                else:
                    dve.wait_ge(evac_done, chunk_done(n, c))
                if c == DC - 1:
                    dve.wait_ge(acc_link, acc_count(n - 1) + 3)
                V.tensor_tensor(dev_slot[c], res[:, c, :], res[:, c, :], ALU.mult).then_inc(dev_sq, 1)

            def shift(n):
                dve.wait_ge(shift_done, n + 1)
                dve.wait_ge(evac_done, chunk_done(n, 3))
                for c in range(DC):
                    V.scalar_tensor_tensor(res[:, c, :], bank[4], -1.0 / (2 * P * (1.0 if c < 4 else ALPHA)), res[:, c, :],
                                           ALU.mult, ALU.add).then_inc(ln_shifted, 1)
                    if 1 <= c <= 4:
                        square(n, c - 1)

            def out_stage(name, n):
                st = ST[name]
                if n < 4:
                    for c in range(DC):
                        link(V.tensor_tensor(res[:, c, :], xhi[:, c, :].bitcast(F32), xlo[:, c, :].bitcast(F32), ALU.add))
                for c in range(DC):
                    dve.wait_ge(part_done, st.part0 + c + 1)
                    if n < 4 and c >= 4:
                        dve.wait_ge(ln_shifted, n * DC + c + 1)
                    residual(bank[c % 4], c, n)
                    if n < 4 and c >= 4:
                        square(n, c)
                    if n < 4 and c == 3:
                        shift(n)
                    if c % 2 == 1 and c < DC - 1:
                        split(st.it0 + 1 + c // 4, c % 4 // 2)

            def down_stage(name, n=None):
                st = ST[name]

                def unit(i, u, ahead, late=False):
                    split(i + (st.it0 + u + 1), 0)
                    dve.wait_ge(part_done, i * 2 + (st.part0 + 2 * u + 2))
                    if late:
                        dve.wait_ge(ln_shifted, n * DC + i + u + 1)
                    residual(bank[u], i + u, n)
                    if late:
                        square(n, i + u)
                    if ahead:
                        split(i + (st.it0 + u + 1), 1)

                looped = st.iters // 2 if n is not None and n < 4 else st.iters - 2
                with dve.Fori(0, looped // 2) as i:
                    for u in range(2):
                        unit(i * 2, u, True)
                if n is not None and n < 4:
                    shift(n)
                    for c in range(looped, DC):
                        unit(c - c % 2, c % 2, c < DC - 1, True)
                elif n is not None:
                    for u in range(2):
                        unit(looped, u, u == 0)
                else:
                    unit(looped, 0, True)
                    dve.wait_ge(part_done, st.part1)
                    residual(bank[1], DC - 1, n)

            def pass_split(n):
                dve.wait_ge(acc_link, acc_count(n))
                V.memset(marks[:, 15:16], 0.0).then_inc(wlo_done, 1)

            def norm(n):
                dve.wait_ge(ln_m2, 2 * n + 1)
                dve.wait_ge(ln_sums, 2 * n + 2)
                V.tensor_tensor(variance, bank[6], mean_sq, ALU.subtract).then_inc(ln_var, 1)
                dve.wait_ge(ln_m2, 2 * n + 2)

                def centre(c):
                    V.tensor_tensor(res[:, c, :], res[:, c, :], mean, ALU.subtract).then_inc(ln_xc, 1)

                centre(0)
                centre(1)
                dve.wait_ge(act_link, 2 * n + 2)
                for c in range(DC + 2):
                    if c < DC:
                        if c < 4:
                            dve.wait_ge(ln_xc, n * 4 + c + 1)
                        else:
                            dve.wait_ge(acc_link, acc_count(n) - 1 - DC + c + 1)
                        V.tensor_tensor(res[:, c, :], res[:, c, :], rstd_ln, ALU.mult).then_inc(ln_n, 1)
                        if c < 2:
                            centre(c + 2)
                        if c == DC - 1:
                            pass_split(n)
                    if n < 3 and c >= 2:
                        m = c - 2
                        dve.wait_ge(ln_a, n * DC + m + 1)
                        V.tensor_tensor(xlo[:, m, :], res[:, m, :], xhi[:, m, :].bitcast(F32), ALU.subtract).then_inc(x_ready, 1)

            def copy_stage(name, dst, scale):
                st = ST[name]
                def body(i, split_next):
                    for half in range(2):
                        for u in range(2):
                            n = 2 * half + u
                            dve.wait_ge(part_done, i * 4 + (st.part0 + n + 1))
                            V.tensor_scalar(dst[:, bass.ds(i * 4 + n, 1), :], bank[n].unsqueeze(1), scale, 0.0,
                                            ALU.mult, ALU.add).then_inc(evac_done, 1)
                        split_next(half)
                stage_loop(name, body)

            def token_stage(name, dst):
                st = ST[name]
                def body(i, split_next):
                    for half in range(2):
                        for n in range(TT):
                            dve.wait_ge(part_done, i * 8 + (st.part0 + 4 * half + n + 1))
                            V.tensor_copy(dst[:, n, bass.ds(i * 512 + half * 256, 256)],
                                          bank[4 * half + n][:, 0:256]).then_inc(evac_done, 1)
                        split_next(half)
                stage_loop(name, body)

            def stick_attention():
                cs = psum[:, 4:7, :].rearrange("p b n -> p (b n)")[:, 0:STICK]

                def soft(hd, h):
                    dve.wait_ge(ln_part, h + 1)
                    z = keep[:, hd % 2, :]
                    V.scalar_tensor_tensor(drop[:, hd % 2, :], z, 0.0, lnp[:, :], ALU.max, ALU.add).then_inc(sp_done, 1)
                    dve.wait_ge(sp_done, h * 4 + 1)
                    sp = drop[:, hd % 2, :]
                    V.tensor_tensor(drop_sum[:, 2 * P:3 * P], sp[:, REST[2]:REST[2] + P], sp[:, 3 * P:4 * P],
                                    ALU.add).then_inc(sp_done, 1)
                    V.tensor_tensor(drop_sum[:, 0:P], sp[:, REST[1]:REST[1] + P], sp[:, 2 * P:3 * P], ALU.add).then_inc(sp_done, 1)
                    V.scalar_tensor_tensor(z, z, 0.0, lnp[:, :], ALU.min, ALU.subtract).then_inc(lb_done, 1)
                    dve.wait_ge(sp_done, h * 4 + 2)
                    V.tensor_tensor(drop_sum[:, P:2 * P], sp[:, REST[1] + P:REST[1] + 2 * P], drop_sum[:, 2 * P:3 * P],
                                    ALU.add).then_inc(sp_done, 1)

                def log_weights(hd, h):
                    dve.wait_ge(cs_done, h + 1)
                    dve.wait_ge(lb_done, h + 2)
                    V.tensor_tensor(keep[:, hd % 2, :], keep[:, hd % 2, :], cs, ALU.subtract).then_inc(lw_done, 1)

                def put_pair(p):
                    dve.wait_ge(o_done, p * 2 + 3)
                    V.tensor_copy(hhi[:, bass.ds(p, 1), :], bank[7].unsqueeze(1)).then_inc(o_hi, 1)
                    dve.wait_ge(o_hi, p + 1)
                    V.tensor_tensor(hlo[:, bass.ds(p, 1), :], bank[7].unsqueeze(1), hhi[:, bass.ds(p, 1), :].bitcast(F32),
                                    ALU.subtract).then_inc(o_ready, 1)

                def heads4(i, last):
                    for hd in range(4):
                        log_weights(hd, i * 4 + hd)
                        if not (last and hd == 3):
                            soft((hd + 1) % 4, i * 4 + (hd + 1))
                        if hd % 2 == 1:
                            put_pair(i * 2 + hd // 2)

                soft(0, 0)
                with dve.Fori(0, HEADS // 4 - 1) as i:
                    heads4(i, False)
                heads4(HEADS // 4 - 1, True)

            def rms(n, gcol):
                dve.wait_ge(act_link, 2 * n + 2)
                first = (n - 4) * DC
                for c in range(DC + 1):
                    if 2 <= c < DC:
                        dve.wait_ge(x_ready, n * DC + c - 1)
                    if c < DC:
                        V.scalar_tensor_tensor(tmp_c[:, c % 2, :], res[:, c, :], prm[:, gcol + c:gcol + c + 1], rstd,
                                               ALU.mult, ALU.mult).then_inc(rms_t, 1)
                        if n > 4 and c == DC - 1:
                            pass_split(n)
                    if c >= 1:
                        m = c - 1
                        dve.wait_ge(ln_hi, 3 * DC + first + m + 1)
                        V.tensor_tensor(xlo[:, m, :], tmp_c[:, m % 2, :], xhi[:, m, :].bitcast(F32), ALU.subtract).then_inc(x_ready, 1)

            def split_stage(name):
                def body(i, split_next):
                    split_next(0)
                    split_next(1)
                stage_loop(name, body)

            def conv_stage(name):
                st = ST[name]
                layer = int(name[-1])
                n0 = (st.evac1 - st.evac0) * layer
                def body(i, split_next):
                    split_next(0)
                    for u in range(2):
                        dve.wait_ge(conv_a, i * 2 + (n0 + u + 1))
                        V.scalar_tensor_tensor(tmp_a[:, u, 1:SEQ], bank[u][:, 0:SEQ - 1], tap(layer, 1, i * 2 + u),
                                               tmp_a[:, u, 1:SEQ], ALU.mult, ALU.add).then_inc(ttr_link, 1)
                        dve.wait_ge(ttr_link, i * 2 + (n0 + u + 1))
                        V.scalar_tensor_tensor(tmp_a[:, u, 2:SEQ], bank[u][:, 0:SEQ - 2], tap(layer, 0, i * 2 + u),
                                               tmp_a[:, u, 2:SEQ], ALU.mult, ALU.add).then_inc(conv_b, 1)
                    for u in range(2):
                        dve.wait_ge(part_done, i * 4 + (st.part0 + u + 3))
                        dve.wait_ge(act_out, i * 2 + (st.pair0 - DC + u + 1))
                        V.tensor_tensor(tmp_b[:, u, :], bank[2 + u], tmp_a[:, u, :], ALU.mult).then_inc(evac_done, 1)
                        dve.wait_ge(evac_done, i * 2 + (st.evac0 + u + 1))
                        put_hidden(tmp_b[:, u:u + 1, :], i * 2 + u, i * 2 + (st.pair0 + u + 1))
                    split_next(1)
                stage_loop(name, body)

            def put_x(src, m, hi_sem, ready, count):
                V.tensor_copy(xhi[:, bass.ds(m, 1), :], src).then_inc(hi_sem, 1)
                dve.wait_ge(hi_sem, count)
                V.tensor_tensor(xlo[:, bass.ds(m, 1), :], src, xhi[:, bass.ds(m, 1), :].bitcast(F32),
                                ALU.subtract).then_inc(ready, 1)

            link = linker(dve, ev_link)

            def gate_norm():
                dve.wait_ge(evac_done, ST["ev_v"].evac1)
                for n in range(TT):
                    link(V.bn_stats(gv_stats[:, n, :], gv_t[:, n, :]))
                    link(V.bn_aggr(gv_mv[:, n, :], gv_stats[:, n, :]))
                V.memset(marks[:, 14:15], 0.0).then_inc(gv_var, 1)
                dve.wait_ge(gv_rstd, 1)
                for n in range(TT):
                    V.tensor_scalar(gv_t[:, n, :], gv_t[:, n, :], gv_mv[:, n, 0:1], gv_rs[:, n:n + 1],
                                    ALU.subtract, ALU.mult).then_inc(gv_scaled, 1)

            def gated_mlp():
                dve.wait_ge(tab_done, 1)
                dve.wait_ge(consts, 4)
                for n in range(3):
                    link(V.tensor_copy(mult_t[:, n, :], bank[4][:, 0:P]))
                link(V.tensor_scalar(mult_t[:, 3, :], bank[4][:, 0:P], 1.0, 0.0, ALU.add, ALU.add))
                for c in range(4):
                    dve.wait_ge(gm_done, c + 1)
                    V.tensor_tensor(u_f[:, c, :], u_f[:, c, :], bank[5 + c % 2], ALU.mult).then_inc(gm_copied, 1)
                link(V.tensor_tensor(mult_t[:, 2, :], mult_t[:, 2, :], after[:, :], ALU.add))
                link(V.tensor_tensor(mult_t[:, 2, :], mult_t[:, 2, :], ident[:, :], ALU.add))
                link(V.tensor_tensor(bias_t[:, 0, :], before[:, :], ident[:, :], ALU.add))
                link(V.tensor_tensor(mult_t[:, 3, :], mult_t[:, 3, :], bias_t[:, 0, :], ALU.mult))
                link(V.tensor_scalar(bias_t[:, :, :], mult_t[:, :, :], 1.0, -1.0, ALU.min, ALU.add))
                link(V.tensor_scalar(bias_t[:, :, :], bias_t[:, :, :], -NEG, 0.0, ALU.mult, ALU.add))
                link(V.tensor_scalar(mult_t[:, :, :], mult_t[:, :, :], 1.0, -1.0, ALU.max, ALU.add))
                link(V.scalar_tensor_tensor(bias_t[:, :, :], mult_t[:, :, :], math.log(2), bias_t[:, :, :], ALU.mult, ALU.add))
                link(V.scalar_tensor_tensor(mult_t[:, :, :], mult_t[:, :, :], -1.0, mult_t[:, :, :], ALU.add, ALU.mult))
                link(V.scalar_tensor_tensor(bias_t[:, :, :], mult_t[:, :, :], math.log(3) / 2 - math.log(2), bias_t[:, :, :],
                                            ALU.mult, ALU.add))
                V.memset(marks[:, 13:14], 0.0).then_inc(sm_done, 4)
                V.memset(marks[:, 12:13], 0.0).then_inc(tables, 1)

            def dilated_attention():
                dve.wait_ge(qk_rstd, 1)

                def rows(hd, h):
                    for n in range(TT):
                        dve.wait_ge(sc_done, h * 4 + (n + 2))
                        row = prob[:, hd % 2, ROW_AT[n]:ROW_AT[n] + (n + 1) * P]
                        V.scalar_tensor_tensor(row.rearrange("p (j k) -> p j k", k=P),
                                               bank[n][:, 0:(n + 1) * P].rearrange("p (j k) -> p j k", k=P), HD ** -0.5,
                                               bias_t[:, 3 - n:4, :], ALU.mult, ALU.add).then_inc(sm_done, 1)
                        dve.wait_ge(sm_done, h * 4 + (n + 5))
                        V.tensor_reduce(neg_max[:, hd % 2, n:n + 1], row, AX.X, ALU.max, negate=True).then_inc(mx_done, 1)

                def sums(hd, h):
                    dve.wait_ge(pexp, h * 4 + 4)
                    V.reciprocal(rden[:, hd % 2, :], den[:, hd % 2, :]).then_inc(den_done, 1)

                def put_pair(p):
                    dve.wait_ge(pv_done, p * 2 + 3)
                    put_x(bank[7].unsqueeze(1), p + 4, b_hi, b_ready, p + 1)

                def stage_pair(i, pp):
                    for dst, c0, g in ((qn_pair, 0, q_gain), (kn_pair, 4, k_gain)):
                        c = bass.ds(i * 2 + (c0 + pp), 1)
                        ins = V.scalar_tensor_tensor(dst[:, pp:pp + 1, :], qk_f[:, c, :], g, qk_rs[:, c, :], ALU.mult, ALU.mult)
                    ins.then_inc(qn_ready, 1)

                def heads4(i, first, last):
                    for hd in range(4):
                        if not (last and hd == 3):
                            sums((hd + 1) % 4, i * 4 + (hd + 1))
                        if hd == 0 and not first:
                            put_pair(i * 2 - 1)
                        if hd == 2:
                            put_pair(i * 2)
                        if not (last and hd >= 2):
                            rows((hd + 2) % 4, i * 4 + (hd + 2))
                        if hd % 2 == 1 and not last:
                            stage_pair(i + 1, hd // 2)

                stage_pair(0, 0)
                stage_pair(0, 1)
                rows(0, 0)
                rows(1, 1)
                sums(0, 0)
                with dve.Fori(0, HEADS_B // 4 - 1) as i:
                    heads4(i, True, False)
                heads4(HEADS_B // 4 - 1, False, True)
                put_pair(HEADS_B // 2 - 1)

            def cumulate():
                V.memset(keep_sum[:, :], 1.0).then_inc(st_link, 1)
                dve.wait_ge(st_link, 1)
                V.memset(keep_sum[:, ::GLA_CHUNK], 0.0).then_inc(st_link, 1)
                dve.wait_ge(ln_a1, 1)
                flat = "p h s -> p (h s)"
                V.scalar_tensor_tensor(la[:, :, :].rearrange(flat), la[:, :, :].rearrange(flat), 0.0, ge[:, :, :].rearrange(flat),
                                       ALU.min, ALU.subtract).then_inc(st_link, 1)
                dve.wait_ge(st_link, 3)
                for h in range(GLA_HEADS):
                    V.tensor_tensor_scan(cum[:, h, :], keep_sum[:, :], la[:, h, :], 0.0, ALU.mult, ALU.add).then_inc(cum_done, 1)
                dve.wait_ge(cum_done, GLA_HEADS)
                c4 = cum[:, :, :].rearrange("p h (n s) -> p (h n) s", s=GLA_CHUNK)
                V.tensor_tensor(gks[:, :, :].rearrange("p h (n s) -> p (h n) s", s=GLA_CHUNK),
                                c4[:, :, GLA_CHUNK - 1:GLA_CHUNK].to_broadcast([P, GLA_HEADS * GLA_CHUNKS, GLA_CHUNK]), c4,
                                ALU.subtract).then_inc(last_done, 1)

            def decayed():
                dve.wait_ge(ek_done, 1)
                V.tensor_copy(decay, ge[:, :, GLA_CHUNK - 1::GLA_CHUNK]).then_inc(st_link, 1)
                V.tensor_tensor(gq[:, :, :], gq[:, :, :], ge[:, :, :], ALU.mult).then_inc(gq_done, 1)
                dve.wait_ge(en_done, 1)
                V.tensor_tensor(gkt[:, :, :], gk[:, :, :], gkt[:, :, :], ALU.mult).then_inc(gkt_done, 1)
                dve.wait_ge(es_done, 1)
                V.tensor_tensor(gks[:, :, :], gk[:, :, :], gks[:, :, :], ALU.mult).then_inc(gks_done, 1)

            def linear_attention():
                for h in range(GLA_HEADS):
                    dve.wait_ge(at_done, h + 1)
                    V.tensor_tensor(attn_t[:, h, :, :], bank[4 + h].rearrange("p (n s) -> p n s", n=TT),
                                    chunk_mask[:, :].unsqueeze(1).to_broadcast([P, TT, P]), ALU.mult).then_inc(at_ready, 1)

                def states_of(h):
                    if h >= 2:
                        dve.wait_ge(go_done, 2 * h - 2)
                    else:
                        dve.wait_ge(ga_done, 1)
                    V.memset(gst[:, h % 2, 0, :], 0.0).then_inc(st_ready, 1)
                    dve.wait_ge(kv_done, h + 1)
                    for n in range(GLA_CHUNKS - 1):
                        hf, m, a = n % 2, n // 4, (n // 2) % 2
                        dve.wait_ge(st_ready, h * GLA_CHUNKS + n + 1)
                        V.scalar_tensor_tensor(gst[:, h % 2, n + 1, :], gst[:, h % 2, n, :], decay[:, h, n:n + 1],
                                               bank[2 * hf + m][:, a * GLA_DV:(a + 1) * GLA_DV], ALU.mult,
                                               ALU.add).then_inc(st_ready, 1)

                def put_head(h):
                    dve.wait_ge(go_link, 2 * h + 2)
                    for dv in range(2):
                        m = 2 * h + dv
                        V.scalar_tensor_tensor(go[:, m, :], go[:, m, :], head_gain[:, dv:dv + 1], o_rs[:, h % 2, :],
                                               ALU.mult, ALU.mult).then_inc(go_hi, 1)
                        dve.wait_ge(go_hi, m + 1)
                        V.tensor_tensor(go[:, m, :], go[:, m, :], gr[:, m, :], ALU.mult).then_inc(st_link, 1)
                        dve.wait_ge(st_link, m + 5)
                        put_x(go[:, m:m + 1, :], m, b_hi, go_ready, 4 + m + 1)

                for h in range(3):
                    states_of(h)
                put_head(0)
                states_of(3)
                for h in range(1, GLA_HEADS):
                    put_head(h)

            for name in run:
                if name == "glu":
                    gate_stage(name, DC)
                elif name == "ssm_out":
                    out_stage(name, 0)
                    norm(0)
                elif name == "gu0":
                    gate_stage(name, 0)
                elif name == "down0":
                    down_stage(name, 1)
                    norm(1)
                elif name == "q":
                    copy_stage(name, q_f, HD ** -0.5)
                elif name == "k":
                    copy_stage(name, k_f, 1.0)
                elif name == "v":
                    token_stage(name, v_t)
                    stick_attention()
                elif name == "w_o":
                    out_stage(name, 2)
                    norm(2)
                elif name == "gu1":
                    gate_stage(name, 0)
                elif name == "down1":
                    down_stage(name, 3)
                    norm(3)
                    rms(4, 64)
                elif name == "ev_u":
                    split_stage(name)
                elif name == "ev_v":
                    split_stage(name)
                    gate_norm()
                elif name == "ev_qk":
                    copy_stage(name, qk_f, 1.0)
                    gated_mlp()
                elif name == "ev_vb":
                    token_stage(name, vb_t)
                    dilated_attention()
                elif name == "ev_out":
                    out_stage(name, 5)
                    rms(5, 80)
                elif name in ("conv0", "conv1"):
                    conv_stage(name)
                elif name == "cdown0":
                    down_stage(name, 6)
                    rms(6, 72)
                elif name == "cdown1":
                    down_stage(name)
                    for n in range(TT):
                        dve.wait_ge(tr_out, 2 * n + 1)
                        V.tensor_copy(out_t[:, n, 0:512], bank[2 * n]).then_inc(go_hi, 1)
                        dve.wait_ge(go_hi, DC + n + 1)
                        dve.wait_ge(go_link, DC + n + 1)
                        V.memset(stat[:, 0:1], 0.0).then_inc(out_rows, 1)
                elif name == "od_q":
                    copy_stage(name, gq, 128 ** -0.5)
                elif name == "od_k":
                    copy_stage(name, gk, 1.0)
                    cumulate()
                elif name == "od_v":
                    token_stage(name, gvt)
                    decayed()
                elif name == "od_r":
                    split_stage(name)
                    linear_attention()
                elif name == "od_out":
                    out_stage(name, 7)
                    rms(7, 88)


_INS = [
    "x", "ssm_a_re", "ssm_a_im", "ssm_log_dt", "ssm_b_re", "ssm_b_im", "ssm_c_re", "ssm_c_im", "ssm_d", "ssm_w_glu",
    "ssm_w_out", "sb_w_qkv", "sb_w_o", "ffn_w_gu", "ffn_w_down", "ln_mix_g", "ln_mix_b", "ln_ffn_g", "ln_ffn_b",
    "norm_mix_g_2", "norm_ffn_g_2", "ev_w_in_2", "ev_a_ln_g_2", "ev_a_ln_b_2", "ev_a_ws_2", "ev_a_bs_2",
    "ev_q_g_2", "ev_k_g_2", "ev_w_out_2", "od_w_in_2", "od_w_a2_2", "od_b_a_2", "od_head_g_2", "od_w_out_2",
    "ffn_w_gate_2", "ffn_w_up_2", "ffn_conv_w_2", "ffn_conv_b_2", "ffn_w_down_2",
]


def kernel(**inputs):
    import numpy as _np
    import concourse.bacc as _bacc
    from concourse import mybir as _mybir
    from concourse.bass_utils import run_bass_kernel_spmd as _run

    nc = _bacc.Bacc("TRN2", target_bir_lowering=False, num_devices=1)
    arrays, views = {}, {}
    for name in _INS:
        a = _np.ascontiguousarray(inputs[name])
        arrays[f"in_{name}_dram"] = a
        views[name] = nc.dram_tensor(f"in_{name}_dram", a.shape, _mybir.dt.from_np(a.dtype), kind="ExternalInput").ap()
    out = nc.dram_tensor("out_0_dram", (1, SEQ, D), _mybir.dt.float32, kind="ExternalOutput").ap()
    build_blocks(nc, views, out)
    r = _run(nc, [arrays], core_ids=[0])
    return r.results[0]["out_0_dram"]
```
